# Optimizing a Trainium2 kernel written in Bass

```python
import jax, jax.numpy as jnp
from jax import lax
import numpy as np

D_MODEL = 1024
BATCH = 1
SEQ = 256
DEPTH = 1
DEC_BATCH = 8
DEC_SEQ = 16
PAST_LEN = 128

CHUNK = 64
ATT_HEADS = 16
ATT_HEAD_DIM = 64
ATT_KV_HEADS = 4
ATT_WIDTH = ATT_HEADS * ATT_HEAD_DIM
KV_WIDTH = ATT_KV_HEADS * ATT_HEAD_DIM
IDX_HEADS = 4
IDX_DIM = 64
TOPK_MAX = 256
Q_BLOCK = 128
ROPE_THETA = 500000.0
ROPE_FRACTION = 4
SSM_D_INNER = 2 * D_MODEL
SSM_HEAD_DIM = 64
SSM_HEADS = SSM_D_INNER // SSM_HEAD_DIM
SSM_GROUPS = 4
SSM_D_STATE = 128
CONV_WIDTH = 4
CONV_DIM = SSM_D_INNER + 2 * SSM_GROUPS * SSM_D_STATE
N_BRANCHES = 2
IN_SPLITS = (ATT_WIDTH, KV_WIDTH, KV_WIDTH, IDX_HEADS * IDX_DIM, IDX_DIM, IDX_HEADS,
             SSM_D_INNER, CONV_DIM, SSM_HEADS, N_BRANCHES * D_MODEL)
IN_DIM = sum(IN_SPLITS)
PEER_HEADS = 8
PEER_NKEYS = 128
PEER_EXPERTS = PEER_NKEYS * PEER_NKEYS
PEER_QDIM = 256
PEER_TOPK = 16
PEER_BLOCK = 256
DN_ALPHA = (2.0 * DEPTH) ** 0.25
DN_BETA = (8.0 * DEPTH) ** -0.25
LN_EPS = 1e-5
RMS_EPS = 1e-5
NEG_INF = -1e30

kernel_name = "chunk_causal_dsa_ssd_peer_deepnorm_step"

def layer_norm(x, g, b):
    xf = x.astype(jnp.float32)
    mu = jnp.mean(xf, axis=-1, keepdims=True)
    var = jnp.mean(jnp.square(xf - mu), axis=-1, keepdims=True)
    return ((xf - mu) * lax.rsqrt(var + LN_EPS) * g + b).astype(x.dtype)

def partial_rope(x, pos):
    d = x.shape[-1]
    rd = d // ROPE_FRACTION
    half = rd // 2
    inv = ROPE_THETA ** (-(jnp.arange(half, dtype=jnp.float32) * 2.0) / rd)
    ang = pos.astype(jnp.float32)[:, None] * inv[None, :]
    cos = jnp.cos(ang)[:, None, :]
    sin = jnp.sin(ang)[:, None, :]
    xf = x.astype(jnp.float32)
    x1, x2, xp = xf[..., :half], xf[..., half:rd], xf[..., rd:]
    return jnp.concatenate([x1 * cos - x2 * sin, x2 * cos + x1 * sin, xp], axis=-1).astype(x.dtype)

def dsa_attend(q, qi, wi, q_chunk, k, v, ki, k_chunk, k_sel):
    b, nq = q.shape[0], q.shape[1]
    idx_logits = jnp.einsum('bqhd,bsd->bqhs', qi.astype(jnp.float32), ki.astype(jnp.float32))
    score = jnp.einsum('bqhs,bqh->bqs', jax.nn.relu(idx_logits), wi.astype(jnp.float32))
    admissible = k_chunk[None, :] <= q_chunk[:, None]
    score = jnp.where(admissible[None], score, NEG_INF)
    _, sel = lax.top_k(score, k_sel)
    take = jax.vmap(lambda rows, ids: rows[ids])
    kg = take(k, sel)
    vg = take(v, sel)
    valid = k_chunk[sel] <= q_chunk[None, :, None]
    qg = q.reshape(b, nq, ATT_KV_HEADS, ATT_HEADS // ATT_KV_HEADS, ATT_HEAD_DIM)
    logits = jnp.einsum('bqgrd,bqkgd->bqgrk', qg.astype(jnp.float32), kg.astype(jnp.float32)) * (ATT_HEAD_DIM ** -0.5)
    logits = jnp.where(valid[:, :, None, None, :], logits, NEG_INF)
    probs = jax.nn.softmax(logits, axis=-1)
    out = jnp.einsum('bqgrk,bqkgd->bqgrd', probs, vg.astype(jnp.float32))
    return out.reshape(b, nq, ATT_WIDTH).astype(q.dtype)

def causal_conv(xbc, prev, w, bias):
    L = xbc.shape[1]
    xpad = jnp.concatenate([prev.astype(xbc.dtype), xbc], axis=1)
    out = sum(xpad[:, j:j + L] * w[j] for j in range(CONV_WIDTH)) + bias
    return jax.nn.silu(out), xpad[:, xpad.shape[1] - (CONV_WIDTH - 1):]

def ssd(x, dt, A, Bm, Cm, init_state, chunk):
    b, L, h, p = x.shape
    g, n = Bm.shape[2], Bm.shape[3]
    r = h // g
    nc = L // chunk
    a = (dt * A).reshape(b, nc, chunk, g, r).transpose(0, 3, 4, 1, 2)
    xdt = (x * dt[..., None]).reshape(b, nc, chunk, g, r, p)
    Bc = Bm.reshape(b, nc, chunk, g, n)
    Cc = Cm.reshape(b, nc, chunk, g, n)
    a_cum = jnp.cumsum(a, axis=-1)
    seg = a_cum[..., :, None] - a_cum[..., None, :]
    tri = jnp.tril(jnp.ones((chunk, chunk), dtype=bool))
    decay_in = jnp.exp(jnp.where(tri, seg, -jnp.inf))
    cb = jnp.einsum('bclgn,bcsgn->bgcls', Cc, Bc)
    y_diag = jnp.einsum('bgcls,bgrcls,bcsgrp->bclgrp', cb, decay_in, xdt)
    decay_to_end = jnp.exp(a_cum[..., -1:] - a_cum)
    chunk_states = jnp.einsum('bcsgn,bgrcs,bcsgrp->cbgrpn', Bc, decay_to_end, xdt)
    chunk_decay = jnp.exp(a_cum[..., -1]).transpose(3, 0, 1, 2)

    def step(s, inp):
        dec, st = inp
        return s * dec[..., None, None] + st, s

    final, prev = lax.scan(step, init_state.reshape(b, g, r, p, n), (chunk_decay, chunk_states))
    y_off = jnp.einsum('bclgn,cbgrpn,bgrcl->bclgrp', Cc, prev, jnp.exp(a_cum))
    return (y_diag + y_off).reshape(b, L, h, p), final.reshape(b, h, p, n)

def ssm_branch(xbc_raw, z, dt_raw, conv_prev, ssm_prev, conv_w, conv_b, dt_bias, a_log, d_skip, norm_w):
    b, L, _ = xbc_raw.shape
    xbc, conv_new = causal_conv(xbc_raw, conv_prev, conv_w, conv_b)
    gn = SSM_GROUPS * SSM_D_STATE
    xs = xbc[..., :SSM_D_INNER].reshape(b, L, SSM_HEADS, SSM_HEAD_DIM).astype(jnp.float32)
    Bm = xbc[..., SSM_D_INNER:SSM_D_INNER + gn].reshape(b, L, SSM_GROUPS, SSM_D_STATE).astype(jnp.float32)
    Cm = xbc[..., SSM_D_INNER + gn:].reshape(b, L, SSM_GROUPS, SSM_D_STATE).astype(jnp.float32)
    dt = jax.nn.softplus(dt_raw.astype(jnp.float32) + dt_bias.astype(jnp.float32))
    A = -jnp.exp(a_log.astype(jnp.float32))
    chunk = CHUNK if L % CHUNK == 0 else L
    y, ssm_new = ssd(xs, dt, A, Bm, Cm, ssm_prev.astype(jnp.float32), chunk)
    y = y + d_skip.astype(jnp.float32)[:, None] * xs
    y = y.reshape(b, L, SSM_D_INNER) * jax.nn.silu(z.astype(jnp.float32))
    yg = y.reshape(b, L, SSM_GROUPS, SSM_D_INNER // SSM_GROUPS)
    yg = yg * lax.rsqrt(jnp.mean(jnp.square(yg), axis=-1, keepdims=True) + RMS_EPS)
    y = yg.reshape(b, L, SSM_D_INNER) * norm_w
    return y.astype(xbc_raw.dtype), conv_new, ssm_new

def token_mixer(x, pos, past, w_in, b_gate, conv_w, conv_b, dt_bias, a_log, d_skip, ssm_norm_w,
                w_attn_br, w_ssm_br, w_out):
    b, L, _ = x.shape
    proj = jnp.einsum('bld,de->ble', x, w_in)
    offs = np.cumsum(IN_SPLITS)[:-1].tolist()
    q, k, v, qi, ki, wi, z, xbc_raw, dt_raw, gate_pre = jnp.split(proj, offs, axis=-1)
    q = partial_rope(q.reshape(b, L, ATT_HEADS, ATT_HEAD_DIM), pos)
    k = partial_rope(k.reshape(b, L, ATT_KV_HEADS, ATT_HEAD_DIM), pos)
    v = v.reshape(b, L, ATT_KV_HEADS, ATT_HEAD_DIM)
    qi = partial_rope(qi.reshape(b, L, IDX_HEADS, IDX_DIM), pos)
    ki = partial_rope(ki[:, :, None, :], pos)[:, :, 0]
    if past is None:
        k_chunk = pos // CHUNK
        k_sel = min(TOPK_MAX, L // 4)
        qb = Q_BLOCK if L % Q_BLOCK == 0 else L
        nb = L // qb

        def blocks(a):
            return a.reshape((b, nb, qb) + a.shape[2:]).swapaxes(0, 1)

        attn = lax.map(lambda blk: dsa_attend(blk[0], blk[1], blk[2], blk[3] // CHUNK, k, v, ki, k_chunk, k_sel),
                       (blocks(q), blocks(qi), blocks(wi), pos.reshape(nb, qb)))
        attn = attn.swapaxes(0, 1).reshape(b, L, ATT_WIDTH)
        conv_prev = jnp.zeros((b, CONV_WIDTH - 1, CONV_DIM), x.dtype)
        ssm_prev = jnp.zeros((b, SSM_HEADS, SSM_HEAD_DIM, SSM_D_STATE), jnp.float32)
    else:
        ck, cv, cki, conv_prev, ssm_prev = past
        k_all = jnp.concatenate([ck.astype(k.dtype), k], axis=1)
        v_all = jnp.concatenate([cv.astype(v.dtype), v], axis=1)
        ki_all = jnp.concatenate([cki.astype(ki.dtype), ki], axis=1)
        n_keys = k_all.shape[1]
        k_chunk = jnp.arange(n_keys) // CHUNK
        attn = dsa_attend(q, qi, wi, pos // CHUNK, k_all, v_all, ki_all, k_chunk, min(TOPK_MAX, n_keys // 4))
    y_ssm, conv_new, ssm_new = ssm_branch(xbc_raw, z, dt_raw, conv_prev, ssm_prev, conv_w, conv_b,
                                          dt_bias, a_log, d_skip, ssm_norm_w)
    ya = jnp.einsum('ble,ed->bld', attn, w_attn_br)
    ym = jnp.einsum('ble,ed->bld', y_ssm, w_ssm_br)
    gates = jax.nn.sigmoid((gate_pre + b_gate).astype(jnp.float32)).astype(x.dtype)
    gates = gates.reshape(b, L, N_BRANCHES, D_MODEL)
    mixed = gates[:, :, 0] * ya + gates[:, :, 1] * ym
    out = jnp.einsum('bld,de->ble', mixed, w_out)
    return out, (k, v, ki, conv_new, ssm_new)

def peer(x, wq, keys1, keys2, u, v):
    b, L, d = x.shape
    t = b * L
    nb = -(-t // PEER_BLOCK)
    xf = jnp.pad(x.reshape(t, d), ((0, nb * PEER_BLOCK - t), (0, 0))).reshape(nb, PEER_BLOCK, d)
    half = PEER_QDIM // 2

    def block(xb):
        q = (xb @ wq).reshape(PEER_BLOCK, PEER_HEADS, PEER_QDIM).astype(jnp.float32)
        s1 = jnp.einsum('thd,nd->thn', q[..., :half], keys1.astype(jnp.float32))
        s2 = jnp.einsum('thd,nd->thn', q[..., half:], keys2.astype(jnp.float32))
        v1, i1 = lax.top_k(s1, PEER_TOPK)
        v2, i2 = lax.top_k(s2, PEER_TOPK)
        cand = (v1[..., :, None] + v2[..., None, :]).reshape(PEER_BLOCK, PEER_HEADS, PEER_TOPK * PEER_TOPK)
        cidx = (i1[..., :, None] * PEER_NKEYS + i2[..., None, :]).reshape(PEER_BLOCK, PEER_HEADS, PEER_TOPK * PEER_TOPK)
        top_s, top_i = lax.top_k(cand, PEER_TOPK)
        expert = jnp.take_along_axis(cidx, top_i, axis=-1)
        gate = jax.nn.softmax(top_s, axis=-1)
        ug = u[expert]
        vg = v[expert]
        act = jax.nn.gelu(jnp.einsum('td,thkd->thk', xb, ug).astype(jnp.float32), approximate=False)
        return jnp.einsum('thk,thkd->td', (gate * act).astype(xb.dtype), vg)

    out = lax.map(block, xf).reshape(nb * PEER_BLOCK, d)[:t]
    return out.reshape(b, L, d)

def trunk_layer(x, pos, past, lw):
    (w_in, b_gate, conv_w, conv_b, dt_bias, a_log, d_skip, ssm_norm_w, w_attn_br, w_ssm_br, w_out,
     ln1_g, ln1_b, peer_wq, peer_keys1, peer_keys2, peer_u, peer_v, ln2_g, ln2_b) = lw
    mix, state = token_mixer(x, pos, past, w_in, b_gate, conv_w, conv_b, dt_bias, a_log, d_skip,
                             ssm_norm_w, w_attn_br, w_ssm_br, w_out)
    h = layer_norm(DN_ALPHA * x + mix, ln1_g, ln1_b)
    h = layer_norm(DN_ALPHA * h + peer(h, peer_wq, peer_keys1, peer_keys2, peer_u, peer_v), ln2_g, ln2_b)
    return h, state

def setup_inputs(seed: int = 0) -> dict:
    key = jax.random.key(seed)
    ks = jax.random.split(key, 32)
    f32 = jnp.float32

    def nrm(k, shape, scale):
        return jax.random.normal(k, shape, f32) * scale

    dt0 = jnp.exp(jax.random.uniform(ks[10], (DEPTH, SSM_HEADS), f32, float(np.log(1e-3)), float(np.log(1e-1))))
    return {
        "x_prompt": nrm(ks[0], (BATCH, SEQ, D_MODEL), 1.0),
        "x_sample": nrm(ks[1], (DEC_BATCH, DEC_SEQ, D_MODEL), 1.0),
        "cache_k": nrm(ks[2], (DEPTH, DEC_BATCH, PAST_LEN, ATT_KV_HEADS, ATT_HEAD_DIM), 1.0),
        "cache_v": nrm(ks[3], (DEPTH, DEC_BATCH, PAST_LEN, ATT_KV_HEADS, ATT_HEAD_DIM), 1.0),
        "cache_kidx": nrm(ks[4], (DEPTH, DEC_BATCH, PAST_LEN, IDX_DIM), 1.0),
        "state_conv": nrm(ks[5], (DEPTH, DEC_BATCH, CONV_WIDTH - 1, CONV_DIM), 1.0),
        "state_ssm": nrm(ks[6], (DEPTH, DEC_BATCH, SSM_HEADS, SSM_HEAD_DIM, SSM_D_STATE), 0.5),
        "w_in": nrm(ks[7], (DEPTH, D_MODEL, IN_DIM), D_MODEL ** -0.5),
        "b_gate": nrm(ks[8], (DEPTH, N_BRANCHES * D_MODEL), 0.02),
        "conv_w": nrm(ks[9], (DEPTH, CONV_WIDTH, CONV_DIM), CONV_WIDTH ** -0.5),
        "conv_b": nrm(ks[11], (DEPTH, CONV_DIM), 0.02),
        "dt_bias": dt0 + jnp.log(-jnp.expm1(-dt0)),
        "a_log": jnp.log(jax.random.uniform(ks[12], (DEPTH, SSM_HEADS), f32, 1.0, 16.0)),
        "d_skip": 1.0 + nrm(ks[13], (DEPTH, SSM_HEADS), 0.02),
        "ssm_norm_w": 1.0 + nrm(ks[14], (DEPTH, SSM_D_INNER), 0.02),
        "w_attn_br": nrm(ks[15], (DEPTH, ATT_WIDTH, D_MODEL), ATT_WIDTH ** -0.5),
        "w_ssm_br": nrm(ks[16], (DEPTH, SSM_D_INNER, D_MODEL), SSM_D_INNER ** -0.5),
        "w_out": nrm(ks[17], (DEPTH, D_MODEL, D_MODEL), DN_BETA * D_MODEL ** -0.5),
        "ln1_g": 1.0 + nrm(ks[18], (DEPTH, D_MODEL), 0.02),
        "ln1_b": nrm(ks[19], (DEPTH, D_MODEL), 0.02),
        "peer_wq": nrm(ks[20], (DEPTH, D_MODEL, PEER_HEADS * PEER_QDIM), D_MODEL ** -0.5),
        "peer_keys1": nrm(ks[21], (DEPTH, PEER_NKEYS, PEER_QDIM // 2), (PEER_QDIM // 2) ** -0.5),
        "peer_keys2": nrm(ks[22], (DEPTH, PEER_NKEYS, PEER_QDIM // 2), (PEER_QDIM // 2) ** -0.5),
        "peer_u": nrm(ks[23], (DEPTH, PEER_EXPERTS, D_MODEL), D_MODEL ** -0.5),
        "peer_v": nrm(ks[24], (DEPTH, PEER_EXPERTS, D_MODEL), DN_BETA),
        "ln2_g": 1.0 + nrm(ks[25], (DEPTH, D_MODEL), 0.02),
        "ln2_b": nrm(ks[26], (DEPTH, D_MODEL), 0.02),
    }

def reference(x_prompt, x_sample, cache_k, cache_v, cache_kidx, state_conv, state_ssm,
              w_in, b_gate, conv_w, conv_b, dt_bias, a_log, d_skip, ssm_norm_w,
              w_attn_br, w_ssm_br, w_out, ln1_g, ln1_b,
              peer_wq, peer_keys1, peer_keys2, peer_u, peer_v, ln2_g, ln2_b):
    pos_p = jnp.arange(x_prompt.shape[1])
    pos_s = cache_k.shape[2] + jnp.arange(x_sample.shape[1])
    hp, hs = x_prompt, x_sample
    new_p, new_s = [], []
    for l in range(DEPTH):
        lw = (w_in[l], b_gate[l], conv_w[l], conv_b[l], dt_bias[l], a_log[l], d_skip[l], ssm_norm_w[l],
              w_attn_br[l], w_ssm_br[l], w_out[l], ln1_g[l], ln1_b[l],
              peer_wq[l], peer_keys1[l], peer_keys2[l], peer_u[l], peer_v[l], ln2_g[l], ln2_b[l])
        hp, sp = trunk_layer(hp, pos_p, None, lw)
        hs, ss = trunk_layer(hs, pos_s, (cache_k[l], cache_v[l], cache_kidx[l], state_conv[l], state_ssm[l]), lw)
        new_p.append(sp)
        new_s.append(ss)

    def stack(lst, i):
        return jnp.stack([e[i] for e in lst], axis=0)

    p_k, p_v, p_kidx, p_conv, p_ssm = stack(new_p, 0), stack(new_p, 1), stack(new_p, 2), stack(new_p, 3), stack(new_p, 4)
    s_k, s_v, s_kidx, s_conv, s_ssm = stack(new_s, 0), stack(new_s, 1), stack(new_s, 2), stack(new_s, 3), stack(new_s, 4)
    return (hp, hs, p_k, p_v, p_kidx, p_conv, p_ssm, s_k, s_v, s_kidx, s_conv, s_ssm)


_drawn_inputs = setup_inputs


def setup_inputs(seed=0):
    import zlib

    import numpy as np

    out = dict(_drawn_inputs(seed))
    spreads = {}
    factors = {'b_gate': 4.625, 'd_skip': 3.157, 'ssm_norm_w': 2.809, 'ln2_g': 2.793, 'ln2_b': 2.803}
    for name, (base, spread) in spreads.items():
        noise = np.random.default_rng([zlib.crc32(name.encode()), seed]).standard_normal(out[name].shape)
        drawn = base * np.exp(spread * noise) if base else spread * noise
        out[name] = __import__('jax').numpy.asarray(drawn.astype(out[name].dtype))
    for name, factor in factors.items():
        out[name] = (out[name] * factor).astype(out[name].dtype)
    return out
```

```python
from contextlib import ExitStack, contextmanager

import numpy as np

import concourse.bass as bass
from concourse import mybir
from concourse.alu_op_type import AluOpType as ALU

ACT = mybir.ActivationFunctionType
F32 = mybir.dt.float32
U32 = mybir.dt.uint32
AX_X = mybir.AxisListType.X
ds = bass.ds

P = 128
D = 1024
KC = D // P
TILES = 3
TOK = TILES * P
SEQ, DEC_B, DEC_S, PAST = 256, 8, 16, 128
HEADS, HD, KVH, REP = 16, 64, 4, 4
IH = 4
CHUNK = 64
TOPK_P, TOPK_S = 64, 36
DI, SH, G, N = 2048, 32, 4, 128
CONV, CW = 3072, 4
CC = CONV // P
PH, NK, PTOP = 8, 128, 16
ALPHA = 2.0 ** 0.25
EPS = 1e-5
NEG = -1e30
GONE = -3e38
LOG_SCALE = HD ** -0.5

O_K, O_V, O_QI, O_KI, O_WI = 1024, 1280, 1536, 1792, 1856
O_Z = 1860
O_XBC = O_Z + DI
O_DT = O_XBC + CONV
O_GATE = O_DT + SH

SEG = DEC_S + CW - 1
RAW = CW - 1 + SEQ + DEC_B * SEG
ROWS = DEC_B * (CW - 1) + CW + 1

PB = 8
BLOCKS = PH * PTOP // PB

CONSTS = {}


def const_table():
    t = np.arange(P)
    parts = {}
    parts["ident"] = np.eye(P)
    stream = t // DEC_S
    same = (stream[:, None] == stream[None, :])
    causal = (t[:, None] <= t[None, :])
    parts["tri"] = np.stack([causal, causal & same], 1)
    parts["same"] = np.stack([np.ones((P, P)), same], 1)
    adm = np.zeros((P, TILES, 2 * P))
    for tile in range(2):
        q = (tile * P + t) // CHUNK
        k = np.arange(2 * P) // CHUNK
        adm[:, tile] = k[None, :] <= q[:, None]
    adm[:, 2, :P] = 1
    adm[:, 2, P:] = same
    parts["adm"] = adm
    parts["nadm"] = (1 - adm) * NEG
    parts["blk"] = stream[:, None] == np.arange(DEC_B)[None, :]
    parts["blkcol"] = np.broadcast_to(np.arange(DEC_B)[:, None] == stream[None, :], (P, DEC_B, P))
    pair = np.zeros((P, 4, P))
    for j in range(4):
        pair[:64, j] = stream == 2 * j
        pair[64:, j] = stream == 2 * j + 1
    parts["pair"] = pair
    rd = HD // 4
    half = rd // 2
    inv = np.float32(500000.0) ** (-(np.arange(half, dtype=np.float32) * np.float32(2)) / np.float32(rd))
    pos = np.stack([t, P + t, PAST + t % DEC_S], 1).astype(np.float32)
    ang = pos[:, :, None] * inv.astype(np.float32)
    parts["cos"] = np.cos(ang.astype(np.float32))
    parts["sin"] = np.sin(ang.astype(np.float32))
    parts["iota"] = np.broadcast_to(np.arange(PTOP), (P, PTOP))
    parts["eps"] = np.full((P, 1), EPS)
    at, cols = 0, []
    where = {}
    for name, v in parts.items():
        v = np.ascontiguousarray(v, dtype=np.float32)
        where[name] = (at, v.shape[1:])
        at += int(np.prod(v.shape[1:]))
        cols.append(v.reshape(P, -1))
    return np.concatenate(cols, 1), where


class Count:

    def __init__(self, sem, start=0, step=1):
        self.sem, self.n, self.step, self.extra = sem, start, step, None

    def value(self, n=None):
        n = self.n if n is None else n
        return n * self.step if self.extra is None else (self.extra + n) * self.step

    def give(self, ins):
        ins.then_inc(self.sem, self.step)
        self.n += 1
        return ins

    def take(self, eng):
        self.n += 1
        eng.wait_ge(self.sem, self.value())

    def upto(self, eng):
        eng.wait_ge(self.sem, self.value())


class Own:

    def __init__(self, eng, sem):
        self.eng, self.step = eng, Count(sem)
        self.last = self.step

    def __call__(self, ins, signal=None):
        self.last = self.step if signal is None else signal
        return self.last.give(ins)

    def settle(self):
        self.last.upto(self.eng)


@contextmanager
def loop(eng, times, *per):
    starts = [c.n for c, _ in per]
    with eng.Fori(0, times) as i:
        for c, k in per:
            c.extra = i * k
        yield i
        for (c, k), s in zip(per, starts):
            assert c.n == s + k, (c.sem, c.n, s, k)
    for (c, k), s in zip(per, starts):
        c.extra, c.n = None, s + times * k


def build(nc, a, out, where):
    ctx = ExitStack()
    with ctx:
        def sb(name, words, dt=F32):
            return ctx.enter_context(nc.sbuf_tensor(name, [P, words], dt))

        def sem(name):
            return ctx.enter_context(nc.semaphore(name))

        cst = sb("cst", a["table"].shape[1])

        def const(name):
            at, shape = where[name]
            v = cst[:, at:at + int(np.prod(shape))]
            if len(shape) == 2:
                v = v.rearrange("p (a b) -> p a b", a=shape[0])
            return v

        ident, tri, same, adm, nadm = (const(k) for k in ("ident", "tri", "same", "adm", "nadm"))
        blk, blkcol, pair, cos, sin, iota = (const(k) for k in ("blk", "blkcol", "pair", "cos", "sin", "iota"))
        eps = const("eps")
        rowsT = sb("rowsT", CC * ROWS)[:, :].rearrange("p (c r) -> p c r", c=CC)
        normT = sb("normT", 16)
        headp = sb("headp", 3 * SH)
        wdt = sb("wdt", KC * SH)[:, :].rearrange("p (k n) -> p k n", k=KC)
        wbuf = [sb(f"wbuf{i}", KC * 512)[:, :].rearrange("p (k n) -> p k n", k=KC) for i in range(2)]
        xT = sb("xT", KC * TOK)[:, :].rearrange("p (k t) -> p k t", k=KC)
        YD = sb("YD", 6144)
        B = sb("B", 6144)
        BIG = sb("BIG", 14080 + 9216)
        C = BIG[:, 14080:14080 + 9216]
        small = sb("small", 1320)

        at, room = [0], [small[:, :]]

        def tiny(words, dt=F32):
            v = room[0][:, at[0]:at[0] + words]
            at[0] += words
            assert at[0] <= room[0].shape[1], at[0]
            return v if dt is F32 else v.bitcast(dt)

        lm = [YD[:, i * 1024:(i + 1) * 1024].rearrange("p (r s) -> p r s", r=REP) for i in range(2)]
        PT = YD[:, 2048:3072].rearrange("p (h r t) -> p h r t", h=2, r=REP)
        rowsin = YD[:, 0:3072]
        ya = YD[:, 0:3072].rearrange("p (t n) -> p t n", t=TILES)
        tails = YD[:, 3072:6144]
        attnT = YD[:, 3072:6144].rearrange("p (k t) -> p k t", k=KC)
        xbt = YD[:, 3072:3072 + 2560]
        ym = YD[:, 3072:6144].rearrange("p (t n) -> p t n", t=TILES)
        qp = YD[:, 0:6144].rearrange("p (t n) -> p t n", t=TILES)
        qkv = B[:, :].rearrange("p (t n) -> p t n", t=TILES)
        y = B[:, :].rearrange("p (t n) -> p t n", t=TILES)
        h = B[:, 0:3072].rearrange("p (t n) -> p t n", t=TILES)
        x2 = B[:, 3072:6144].rearrange("p (t n) -> p t n", t=TILES)
        xc = C.rearrange("p (c t) -> p c t", c=CC)
        yT = C[:, 0:6144].rearrange("p (k t) -> p k t", k=16)
        xraw = BIG[:, 0:CC * RAW].rearrange("p (c t) -> p c t", c=CC)
        x1 = BIG[:, CC * RAW:CC * RAW + 3072].rearrange("p (t n) -> p t n", t=TILES)
        big = [0]

        def take(words):
            v = BIG[:, big[0]:big[0] + words]
            big[0] += words
            assert big[0] <= 14080, big[0]
            return v

        kc = take(5 * 512).rearrange("p (v n) -> p v n", v=5)
        vc = take(2048).rearrange("p (b n) -> p b n", b=DEC_B)
        kT = take(5 * TOK).rearrange("p (v t) -> p v t", v=5)
        kcT = take(5 * 512).rearrange("p (v j s) -> p v j s", v=5, j=4)
        qm = take(2048).rearrange("p (r j t) -> p r j t", r=REP, j=4)
        qn = take(512).rearrange("p (r t) -> p r t", r=REP)
        score, scoret, negm = take(256), take(256), take(256)
        big[0] = 0
        xdt, xdtd = take(2048), take(2048)
        CTm = take(1024).rearrange("p (b t) -> p b t", b=DEC_B)
        Bm = take(1024).rearrange("p (b n) -> p b n", b=DEC_B)
        MT = take(1024).rearrange("p (r l) -> p r l", r=8)
        pT = take(4096).rearrange("p (b n) -> p b n", b=DEC_B)
        stateT = pT.rearrange("p b n -> p (b n)")[:, 0:2048]
        pso = pT.rearrange("p b n -> p (b n)")[:, 2048:4096]
        sst = [take(1024).rearrange("p (b n) -> p b n", b=DEC_B) for _ in range(2)]
        cbm = take(128)
        ytmp = take(512)
        big[0] = 0
        zs = take(3072).rearrange("p (j n) -> p j n", j=6)
        gt = take(3072).rearrange("p (j n) -> p j n", j=6)
        bg = take(2048)
        big[0] = 0
        lnp = BIG[:, 2 * PB * D:2 * PB * D + 4096].rearrange("p (a n) -> p a n", a=4)
        uslot = [BIG[:, j * D:(j + 1) * D] for j in range(PB)]
        vslot = [BIG[:, (PB + j) * D:(PB + j + 1) * D] for j in range(PB)]
        behind = 2 * PB * D + 4096
        diag = BIG[:, behind:behind + PB * P].rearrange("p (j n) -> p j n", j=PB)
        zero = BIG[:, behind + 1024:behind + 1152]
        yout = BIG[:, behind + 1152:behind + 2176]
        keys = BIG[:, behind + 2176:behind + 2432].rearrange("p (a n) -> p a n", a=2)
        keysT = BIG[:, behind + 2432:behind + 2688].rearrange("p (a n) -> p a n", a=2)
        assert behind + 2688 <= 14080 + 9216
        qT = BIG[:, 0:2048].rearrange("p (c t) -> p c t", c=16)
        sc = [wbuf[0].rearrange("p k n -> p (k n)")[:, 0:2048], wbuf[0].rearrange("p k n -> p (k n)")[:, 2048:4096],
              wbuf[1].rearrange("p k n -> p (k n)")[:, 0:2048]]
        cand = YD[:, 0:2048]
        hot = YD[:, 2048:4096].rearrange("p (k j) -> p k j", j=PTOP)

        dtr = tiny(96)
        dtv, dta, dtu, dtw = tiny(96), tiny(96), tiny(96), tiny(96)
        negA = tiny(32)
        av = tiny(96)
        acs = tiny(192).rearrange("p (t n) -> p t n", t=TILES)
        ex = tiny(288).rearrange("p (t n) -> p t n", t=TILES)
        dec = tiny(128).rearrange("p (c b) -> p c b", c=16)
        m8 = tiny(8)
        nmx, sums, rec = tiny(8), tiny(8), tiny(8)
        rtmp = [qm.rearrange("p r j t -> p (r j t)")[:, k * 480:(k + 1) * 480] for k in range(4)]
        ms = tiny(12)
        bns = tiny(12)
        mv = tiny(2)
        rstd = tiny(12)
        at[0], room[0] = 0, xT.rearrange("p k t -> p (k t)")
        v16 = tiny(256).rearrange("p (c k) -> p c k", c=16)
        i16 = tiny(256, U32).rearrange("p (c k) -> p c k", c=16)
        f16 = tiny(256).rearrange("p (c k) -> p c k", c=16)
        ts16 = tiny(128).rearrange("p (h k) -> p h k", h=PH)
        pos = tiny(128, U32)
        ph = tiny(128, U32)
        phf, e1, e2 = tiny(128), tiny(128), tiny(128)
        gate = tiny(TILES * 128).rearrange("p (t k) -> p t k", t=TILES)
        eidx = tiny(TILES * 128, U32).rearrange("p (t k) -> p t k", t=TILES)
        s8 = tiny(8)
        dots, gl, w8 = tiny(PB), tiny(PB), tiny(PB)
        islot = [tiny(PB, U32) for _ in range(2)]

        psum = [ctx.enter_context(nc.psum_tensor(f"bank{i}", [P, 512], F32)) for i in range(8)]
        acc = psum[6:8]

        const_in, x_in, rows_in, par_in, wdt_in = (sem(s) for s in ("const_in", "x_in", "rows_in", "par_in", "wdt_in"))
        w_in_sem = [sem("wbuf0_loaded"), sem("wbuf1_loaded")]
        vb_filled, vb_drained = sem("v_bank_filled"), sem("v_bank_drained")
        sb_filled, sb_drained = sem("s_bank_filled"), sem("s_bank_drained")
        dve_step, act_step, pool_step = sem("dve_step"), sem("act_step"), sem("pool_step")
        conv_done, silu_done, tails_ready, tails_out = sem("conv_done"), sem("silu_done"), sem("tails_ready"), sem("tails_out")
        rope_done, cache_in, kv_out = sem("rope_done"), sem("cache_in"), sem("kv_out")
        max_ready, exp_done, probs_ready = sem("max_ready"), sem("exp_done"), sem("probs_ready")
        dt_e, a_ready, sum_ready, ex_ready = sem("dt_steps_by_act"), sem("a_ready"), sem("sums_ready"), sem("decays_ready")
        dt_v = sem("dt_steps_by_dve")
        seg_ready, seg_exp, mt_ready = sem("seg_ready"), sem("seg_exp"), sem("mt_ready")
        old_in = [sem("old_state0_in"), sem("old_state1_in")]
        new_ready, new_out = sem("new_state_ready"), [sem("new_state0_out"), sem("new_state1_out")]
        pso_out = sem("prompt_state_out")
        y_done = sem("tile_y_done")
        gated, ms_ready, rms_root, yn_ready = sem("y_gated"), sem("ms_ready"), sem("rms_root"), sem("yn_ready")
        bg_in, gate_pre, gate_ready, mixed_ready = sem("bg_in"), sem("gate_pre"), sem("gate_ready"), sem("mixed_ready")
        x2_in, lnp_in, var1_ready, root1_ready, h_ready = (sem(s) for s in ("x2_in", "lnp_in", "var1_ready", "root1_ready", "h_ready"))
        keys_in, score_e, score_v = sem("keys_in"), sem("ts_shifted"), sem("ts_exp")
        idx_ready = sem("idx_ready")
        u_in = [sem(f"u_in{j}") for j in range(PB)]
        v_in = [sem(f"v_in{j}") for j in range(PB)]
        dot_done, gelu_done, w_ready, diag_ready, v_used = (sem(s) for s in ("dot_done", "gelu_done", "w_ready", "diag_ready", "v_used"))
        acc_full, var2_ready, root2_ready, y_out_ready, y_out = (sem(s) for s in ("acc_full", "var2_ready", "root2_ready", "y_out_ready", "y_out"))

        attn_v = TILES * (1 + 2 + KVH * 3)
        attn_s = 6 + 5 + TILES * KVH * 3
        ssd_v = TILES + TILES * G * 4 + 2 * G + 2 * G + 16 * 2
        ssd_s = 3 * 5 + 4 + 1 + 16 * 2
        phases = [("start", 9, 0), ("conv", 0, 24), ("dt", 0, 3), ("qkv", 12, 0), ("tails", 0, 6),
                  ("attention", attn_v, attn_s), ("ya", 6, 0), ("ssd", ssd_v, ssd_s), ("z", 0, 12),
                  ("yT", 0, 12), ("ym", 12, 0), ("gates", 12, 0), ("mixedT", 0, 6), ("out", 6, 0),
                  ("hT", 0, 6), ("wq", 0, 12), ("keysT", 0, 1), ("scores", 12, 12)]
        before, nv, ns = {}, 0, 0
        for name, v, s in phases:
            before[name] = (nv, ns)
            nv, ns = nv + v, ns + s

        block = ctx.enter_context(nc.Block())

        @block.sync
        def _(sp):
            sp.dma_start(cst[:, :], a["table"]).then_inc(const_in, 16)
            sp.dma_start(x1[:, 0:2, :], a["x_prompt"][0].rearrange("(t p) n -> p t n", p=P)).then_inc(x_in, 16)
            sp.dma_start(x1[:, 2, :], a["x_sample"].rearrange("b s n -> (b s) n")).then_inc(x_in, 16)

            def cols(w, at, n):
                return w[:, at:at + n] if isinstance(at, int) else w[:, ds(at, n)]

            def wtile(w, at, n):
                return cols(w, at, n).rearrange("(k p) n -> p k n", p=P)

            w_in = a["w_in"][0]
            free = [None, None]

            def weights(name, ring, turns, source, width=512):
                first = before[name][0 if ring is vb_filled else 1]

                def load(turn, b):
                    sp.dma_start(wbuf[b][:, :, 0:width], source(turn, b)).then_inc(w_in_sem[b], 16)

                for b in range(2):
                    if free[b] is not None:
                        sp.wait_ge(*free[b])
                    load(0, b)
                if turns > 1:
                    with sp.Fori(1, turns) as i:
                        for b in range(2):
                            sp.wait_ge(ring, i * 6 + (first - 6 + 3 * b + 3))
                            load(i, b)
                for b in range(2):
                    free[b] = (ring, first + 6 * (turns - 1) + 3 * b + 3)

            weights("conv", sb_filled, 4, lambda i, b: wtile(w_in, i * 768 + (O_XBC + 384 * b), 384), 384)
            weights("qkv", vb_filled, 2, lambda i, b: wtile(w_in, i * 1024 + 512 * b, 512))
            weights("ya", vb_filled, 1, lambda i, b: wtile(a["w_attn_br"][0], 512 * b, 512))
            weights("z", sb_filled, 2, lambda i, b: wtile(w_in, i * 1024 + (O_Z + 512 * b), 512))
            weights("ym", vb_filled, 2, lambda i, b: wtile(a["w_ssm_br"][0][D * b:D * (b + 1)], i * 512, 512))
            weights("gates", vb_filled, 2, lambda i, b: wtile(w_in, i * 512 + (O_GATE + 1024 * b), 512))
            weights("out", vb_filled, 1, lambda i, b: wtile(a["w_out"][0], 512 * b, 512))
            weights("wq", sb_filled, 2, lambda i, b: wtile(a["peer_wq"][0], i * 1024 + 512 * b, 512))
            for t in range(TILES):
                sp.wait_ge(y_out_ready, t + 1)
                dst = out["y_prompt"][0][t * P:(t + 1) * P] if t < 2 else out["y_sample"].rearrange("b s n -> (b s) n")
                sp.dma_start(dst, yout).then_inc(y_out, 16)
            sp.wait_ge(y_out, 16 * TILES)

        @block.gpsimd
        def _(pool):
            own = Own(pool, pool_step)
            pool.dma_start(rowsin[0:24, :], a["state_conv"][0].rearrange("b j n -> (b j) n")).then_inc(rows_in, 16)
            pool.dma_start(rowsin[24:28, :], a["conv_w"][0]).then_inc(rows_in, 16)
            pool.dma_start(rowsin[28:29, :], a["conv_b"]).then_inc(rows_in, 16)
            pool.dma_start(tails[0:16, 0:P], a["ssm_norm_w"][0].rearrange("(c p) -> c p", p=P)).then_inc(rows_in, 16)
            for i, name in enumerate(("dt_bias", "a_log", "d_skip")):
                pool.dma_start(headp[:, i * SH:(i + 1) * SH], a[name][0].partition_broadcast(P)).then_inc(par_in, 16)
            pool.dma_start(wdt, a["w_in"][0][:, O_DT:O_DT + SH].rearrange("(k p) n -> p k n", p=P)).then_inc(wdt_in, 16)
            pool.wait_ge(conv_done, CC)
            pool.wait_ge(tails_ready, 1)
            for v in range(KVH):
                pool.dma_start(kc[:, v, :].rearrange("p (b n) -> p b n", b=DEC_B),
                               a["cache_k"][0][:, :, v, :].rearrange("b s n -> s b n")).then_inc(cache_in, 16)
            pool.dma_start(kc[:, 4, :].rearrange("p (b n) -> p b n", b=DEC_B),
                           a["cache_kidx"][0].rearrange("b s n -> s b n")).then_inc(cache_in, 16)
            pool.dma_start(vc, a["cache_v"][0].rearrange("b s v n -> s b (v n)")).then_inc(cache_in, 16)
            pool.wait_ge(sb_drained, 3 + before["attention"][1])
            pool.dma_start(out["p_conv"][0, 0], tails[0:3, :]).then_inc(tails_out, 16)
            pool.dma_start(out["s_conv"][0].rearrange("b j n -> (b j) n"), tails[3:27, :]).then_inc(tails_out, 16)
            pool.wait_ge(rope_done, 1)
            for t in range(TILES):
                for name, o, n in (("k", O_K, 256), ("v", O_V, 256), ("kidx", O_KI, 64)):
                    if t < 2:
                        dst = out["p_" + name][0, 0, t * P:(t + 1) * P]
                        dst = dst.rearrange("s v n -> s (v n)") if n == 256 else dst
                    else:
                        dst = out["s_" + name][0]
                        dst = dst.rearrange("b s v n -> (b s) (v n)") if n == 256 else dst.rearrange("b s n -> (b s) n")
                    pool.dma_start(dst, qkv[:, t, o:o + n]).then_inc(kv_out, 16)
            pool.wait_ge(sb_drained, 3 + before["ssd"][1] + 2 * 5 + 4)
            pool.dma_start(out["p_ssm"][0, 0].rearrange("(c h) q n -> (h q) c n", h=2),
                           pso.rearrange("p (c n) -> p c n", c=16)).then_inc(pso_out, 16)
            old = a["state_ssm"][0].rearrange("b (c h) q n -> c (h q) b n", h=2)
            new = out["s_ssm"][0].rearrange("b (c h) q n -> c (h q) b n", h=2)
            for c in range(16):
                if c >= 2:
                    pool.wait_ge(new_ready, 2 * (c - 1))
                    pool.dma_start(new[c - 2], sst[c % 2]).then_inc(new_out[c % 2], 16)
                    pool.wait_ge(new_out[c % 2], 16 * (c // 2))
                pool.dma_start(sst[c % 2], old[c]).then_inc(old_in[c % 2], 16)
            for c in (16, 17):
                pool.wait_ge(new_ready, 2 * (c - 1))
                pool.dma_start(new[c - 2], sst[c % 2]).then_inc(new_out[c % 2], 16)
            for b in range(2):
                pool.wait_ge(new_out[b], 16 * 8)
            pool.wait_ge(y_done, 3)
            pool.dma_start(bg, a["b_gate"][0].partition_broadcast(P)).then_inc(bg_in, 16)
            pool.wait_ge(sb_filled, before["ym"][1])
            pool.wait_ge(vb_filled, before["gates"][0])
            pool.dma_start(x2[:, 0:2, :], a["x_prompt"][0].rearrange("(t p) n -> p t n", p=P)).then_inc(x2_in, 16)
            pool.dma_start(x2[:, 2, :], a["x_sample"].rearrange("b s n -> (b s) n")).then_inc(x2_in, 16)
            for i, name in enumerate(("ln1_g", "ln1_b", "ln2_g", "ln2_b")):
                pool.dma_start(lnp[:, i, :], a[name][0].partition_broadcast(P)).then_inc(lnp_in, 16)
            pool.dma_start(keys[:, 0, :], a["peer_keys1"][0]).then_inc(keys_in, 16)
            pool.dma_start(keys[:, 1, :], a["peer_keys2"][0]).then_inc(keys_in, 16)
            pool.wait_ge(tails_out, 32)
            pool.wait_ge(kv_out, 16 * 9)
            pool.wait_ge(pso_out, 16)

            want_u, want_v = pool.alloc_register("want_dots"), pool.alloc_register("want_used")
            pool.reg_mov(want_u, 1)
            pool.reg_mov(want_v, 1)
            table_u, table_v = a["peer_u"][0], a["peer_v"][0]
            pool.sem_inc(dot_done, PB)
            pool.sem_inc(v_used, PB)
            for t in range(TILES):
                pool.wait_ge(idx_ready, t + 1)
                with loop(pool, BLOCKS // 2, (own.step, 2)) as i:
                    for b in range(2):
                        own(pool.tensor_copy(islot[b], eidx[:, t, ds(i * (2 * PB) + b * PB, PB)]))
                        own.settle()
                        for j in range(PB):
                            pool.wait_ge(dot_done, want_u)
                            pool.reg_add(want_u, want_u, 1)
                            pool.indirect_dma_start(uslot[j], None, table_u,
                                                    bass.IndirectOffsetOnAxis(ap=islot[b][:, j:j + 1], axis=0)
                                                    ).then_inc(u_in[j], 16)
                        for j in range(PB):
                            pool.wait_ge(v_used, want_v)
                            pool.reg_add(want_v, want_v, 1)
                            pool.indirect_dma_start(vslot[j], None, table_v,
                                                    bass.IndirectOffsetOnAxis(ap=islot[b][:, j:j + 1], axis=0)
                                                    ).then_inc(v_in[j], 16)

        @block.tensor
        def _(pe):
            vf, vd = Count(vb_filled), Count(vb_drained)
            sf, sd = Count(sb_filled), Count(sb_drained)
            loaded = [Count(s, step=16) for s in w_in_sem]

            def vbank():
                vd.take(pe)
                return psum[vf.n % 3]

            def sbank():
                sd.take(pe)
                return psum[3 + sf.n % 3]

            def v_written():
                pe.wait_ge(vb_drained, 3 + vf.n)

            def s_written():
                pe.wait_ge(sb_drained, 3 + sf.n)

            def phase(name):
                assert (vf.n, sf.n) == before[name], (name, vf.n, sf.n, before[name])

            mm = nc.tensor.matmul

            def turn(dst, src, ids):
                return nc.tensor.transpose(dst, src, ids)

            def product(lhs, ring, bank, b, chunks=KC):
                loaded[b].take(pe)
                for t in range(TILES):
                    dst = bank()
                    for k in range(chunks):
                        last = mm(dst[:, :], lhs(b, k, t), wbuf[b][:, k, :], start=(k == 0), stop=(k == chunks - 1))
                    ring.give(last)

            def products(turns, lhs, ring, drained, bank):
                if turns == 1:
                    for b in range(2):
                        product(lhs, ring, bank, b)
                    return
                with loop(pe, turns, (ring, 6), (drained, 6), (loaded[0], 1), (loaded[1], 1)):
                    for b in range(2):
                        product(lhs, ring, bank, b)

            phase("start")
            pe.wait_ge(const_in, 16)
            pe.wait_ge(x_in, 32)
            for t in range(TILES):
                for q in range(2):
                    dst = vbank()
                    for i in range(4):
                        last = turn(dst[:, i * P:(i + 1) * P], x1[:, t, (4 * q + i) * P:(4 * q + i + 1) * P], ident)
                    vf.give(last)
            pe.wait_ge(rows_in, 64)
            for q in range(2):
                dst = vbank()
                for i in range(12):
                    last = turn(dst[:, i * ROWS:(i + 1) * ROWS], rowsin[0:ROWS, (12 * q + i) * P:(12 * q + i + 1) * P],
                                ident[0:ROWS, 0:ROWS])
                vf.give(last)
            dst = vbank()
            vf.give(turn(dst[:, 0:16], tails[0:16, 0:P], ident[0:16, 0:16]))
            v_written()

            phase("conv")
            with loop(pe, 4, (sf, 6), (sd, 6), (loaded[0], 1), (loaded[1], 1)):
                for b in range(2):
                    loaded[b].take(pe)
                    for j in range(3):
                        dst = sbank()
                        for k in range(KC):
                            last = mm(dst[:, 0:TOK], wbuf[b][:, k, j * P:(j + 1) * P], xT[:, k, :],
                                      start=(k == 0), stop=(k == KC - 1))
                        sf.give(last)

            phase("dt")
            pe.wait_ge(wdt_in, 16)
            for t in range(TILES):
                dst = sbank()
                for k in range(KC):
                    last = mm(dst[:, 0:SH], xT[:, k, t * P:(t + 1) * P], wdt[:, k, :], start=(k == 0), stop=(k == KC - 1))
                sf.give(last)

            def x_part(b, k, t):
                return xT[:, k, t * P:(t + 1) * P]

            phase("qkv")
            products(2, x_part, vf, vd, vbank)

            phase("tails")
            pe.wait_ge(tails_ready, 1)
            tail = xc_tail(BIG)
            for q in range(6):
                dst = sbank()
                for i in range(4):
                    last = turn(dst[0:27, i * P:(i + 1) * P], tail[:, 4 * q + i, :], ident)
                sf.give(last)

            phase("attention")
            pe.wait_ge(rope_done, 1)
            for t in range(TILES):
                dst = sbank()
                for v in range(KVH):
                    last = mm(dst[0:64, v * P:(v + 1) * P], qkv[:, t, O_K + v * HD:O_K + (v + 1) * HD], ident,
                              start=True, stop=True)
                sf.give(last)
                dst = sbank()
                sf.give(mm(dst[0:64, 0:P], qkv[:, t, O_KI:O_KI + HD], ident, start=True, stop=True))
            pe.wait_ge(cache_in, 16 * 6)
            for v in range(5):
                dst = sbank()
                for j in range(4):
                    last = turn(dst[:, j * P:(j + 1) * P], kc[:, v, j * P:(j + 1) * P], ident)
                sf.give(last)
            s_written()

            def turn_q(t, o):
                dst = vbank()
                for r in range(REP):
                    for half in range(2 if t == 2 else 1):
                        last = mm(dst[64 * half:64 * half + 64, r * P:(r + 1) * P],
                                  qkv[:, t, o + r * HD:o + (r + 1) * HD], ident, start=True, stop=True)
                vf.give(last)
                v_written()

            def dot_keys(t, v):
                for q in range(2):
                    dst = vbank()
                    for r in (2 * q, 2 * q + 1):
                        o = (r % 2) * 256
                        if t < 2:
                            last = mm(dst[:, o:o + P * (t + 1)], qn[0:64, r, :], kT[0:64, v, 0:P * (t + 1)],
                                      start=True, stop=True)
                        else:
                            for j in range(4):
                                mm(dst[:, o:o + P], qm[:, r, j, :], kcT[:, v, j, :], start=(j == 0), stop=(j == 3))
                            last = mm(dst[:, o + P:o + 2 * P], qn[0:64, r, :], kT[0:64, v, 2 * P:3 * P],
                                      start=True, stop=True)
                    vf.give(last)

            def attend(t, v):
                n = t * KVH + v
                pe.wait_ge(probs_ready, n + 1)
                for half in range(2):
                    dst = sbank()
                    for r in range(REP):
                        if half == 0 or t > 0:
                            last = turn(dst[:, r * P:(r + 1) * P], lm[n % 2][:, r, half * P:(half + 1) * P], ident)
                        elif r == 0:
                            last = turn(dst[:, 0:P], lm[n % 2][:, 0, 0:P], ident)
                    sf.give(last)
                s_written()
                dst = sbank()
                for par in range(2):
                    o = dst[64 * par:64 * par + 64, 0:256]
                    vs = slice(O_V + v * HD, O_V + (v + 1) * HD)
                    if t < 2:
                        for half in range(t + 1):
                            last = mm(o, qkv[:, half, vs], PT[:, half, par::2, :],
                                      start=(half == 0), stop=(half == t))
                    else:
                        mm(o, qkv[:, 2, vs], PT[:, 1, par::2, :], start=True, stop=False, skip_group_check=True)
                        for b in range(DEC_B):
                            ob = o.rearrange("p (r t) -> p r t", r=2)[:, :, b * DEC_S:(b + 1) * DEC_S]
                            last = mm(ob, vc[:, b, v * HD:(v + 1) * HD], PT[:, 0, par::2, b * DEC_S:(b + 1) * DEC_S],
                                      start=False, stop=(b == DEC_B - 1), skip_group_check=True)
                sf.give(last)

            for t in range(TILES):
                turn_q(t, O_QI)
                dot_keys(t, 4)
                for v in range(KVH):
                    turn_q(t, v * REP * HD)
                    dot_keys(t, v)
                    if t or v:
                        n = t * KVH + v - 1
                        attend(n // KVH, n % KVH)
            attend(TILES - 1, KVH - 1)
            s_written()

            phase("ya")
            products(1, lambda b, k, t: attnT[:, k, t * P:(t + 1) * P], vf, vd, vbank)

            phase("ssd")
            pe.wait_ge(a_ready, 1)
            pe.wait_ge(silu_done, 1)
            for t in range(TILES):
                dst = vbank()
                mm(dst[:, 0:SH], tri[:, t // 2, :], av[:, t * SH:(t + 1) * SH], start=True, stop=True)
                vf.give(mm(dst[:, SH:2 * SH], same[:, t // 2, :], av[:, t * SH:(t + 1) * SH], start=True, stop=True))
            for t in range(TILES):
                tok = slice(t * P, (t + 1) * P)
                for q in range(5):
                    dst = sbank()
                    for i in range(4):
                        last = turn(dst[:, i * P:(i + 1) * P], xc[:, 4 * q + i, tok], ident)
                    sf.give(last)
                if t == 2:
                    dst = sbank()
                    for hh in range(SH):
                        last = mm(dst[64 * (hh % 2):64 * (hh % 2) + 64, (hh // 2) * 8:(hh // 2) * 8 + 8],
                                  av[:, 2 * SH + hh:2 * SH + hh + 1].to_broadcast([P, 64]), blk, start=True, stop=True)
                    sf.give(last)
                s_written()
                for g in range(G):
                    BT, CT = xc[:, 16 + g, tok], xc[:, 20 + g, tok]
                    dst = vbank()
                    vf.give(mm(dst[:, 0:P], BT, CT, start=True, stop=True))
                    for q in range(2):
                        dst = vbank()
                        for i in range(4):
                            hh = t * SH + g * 8 + q * 4 + i
                            last = mm(dst[:, i * P:(i + 1) * P], av[:, hh:hh + 1].to_broadcast([P, P]), tri[:, t // 2, :],
                                      start=True, stop=True)
                        vf.give(last)
                    pe.wait_ge(seg_ready, t * G + g + 1)
                    Bg = xbt[:, DI + g * P:DI + (g + 1) * P]
                    if t == 2:
                        for c in range(4 * g, 4 * g + 4):
                            pe.wait_ge(old_in[c % 2], 16 * (c // 2 + 1))
                            for q in range(2):
                                dst = sbank()
                                for i in range(4):
                                    last = turn(dst[:, i * P:(i + 1) * P], sst[c % 2][:, 4 * q + i, :], ident)
                                sf.give(last)
                            for q in range(2):
                                dst = vbank()
                                vf.give(mm(dst[:, :], xdtd[:, c * P:(c + 1) * P], Bm[:, 4 * q:4 * q + 4, :],
                                           start=True, stop=True))
                        s_written()
                    if t > 0:
                        dst = vbank()
                        if t == 1:
                            vf.give(mm(dst[:, :], CT, stateT[:, g * 512:(g + 1) * 512], start=True, stop=True))
                        else:
                            for b in range(DEC_B):
                                last = mm(dst[:, :], CTm[:, b, :], pT[:, b, :], start=(b == 0), stop=(b == DEC_B - 1))
                            vf.give(last)
                    pe.wait_ge(mt_ready, t * G + g + 1)
                    dst = vbank()
                    for r in range(8):
                        last = mm(dst[:, r * HD:(r + 1) * HD], MT[:, r, :], xdt[:, g * 512 + r * HD:g * 512 + (r + 1) * HD],
                                  start=True, stop=True)
                    vf.give(last)
                    if t < 2:
                        dst = vbank()
                        vf.give(mm(dst[:, :], Bg, xdtd[:, g * 512:(g + 1) * 512], start=True, stop=True))
                if t == 1:
                    v_written()
                    for q in range(4):
                        dst = sbank()
                        for i in range(4):
                            last = turn(dst[:, i * P:(i + 1) * P], stateT[:, (4 * q + i) * P:(4 * q + i + 1) * P], ident)
                        sf.give(last)

            phase("z")
            products(2, x_part, sf, sd, sbank)
            phase("yT")
            for t in range(TILES):
                pe.wait_ge(yn_ready, t + 1)
                for q in range(4):
                    dst = sbank()
                    for i in range(4):
                        last = turn(dst[:, i * P:(i + 1) * P], y[:, t, (4 * q + i) * P:(4 * q + i + 1) * P], ident)
                    sf.give(last)
            s_written()
            phase("ym")
            products(2, lambda b, k, t: yT[:, 8 * b + k, t * P:(t + 1) * P], vf, vd, vbank)
            phase("gates")
            products(2, x_part, vf, vd, vbank)
            phase("mixedT")
            pe.wait_ge(mixed_ready, 6)

            def rows_to_T(src, t, q):
                dst = sbank()
                for i in range(4):
                    last = turn(dst[:, i * P:(i + 1) * P], src[:, t, (4 * q + i) * P:(4 * q + i + 1) * P], ident)
                sf.give(last)

            for t in range(TILES):
                for q in range(2):
                    rows_to_T(ya, t, q)
            s_written()
            phase("out")
            products(1, x_part, vf, vd, vbank)
            phase("hT")
            for t in range(TILES):
                pe.wait_ge(h_ready, t + 1)
                for q in range(2):
                    rows_to_T(h, t, q)
            s_written()
            phase("wq")
            products(2, x_part, sf, sd, sbank)
            phase("keysT")
            pe.wait_ge(keys_in, 32)
            dst = sbank()
            for i in range(2):
                last = turn(dst[:, i * P:(i + 1) * P], keys[:, i, :], ident)
            sf.give(last)
            phase("scores")
            s_written()
            for t in range(TILES):
                for q in range(4):
                    dst = sbank()
                    for i in range(4):
                        last = turn(dst[:, i * P:(i + 1) * P], qp[:, t, (4 * q + i) * P:(4 * q + i + 1) * P], ident)
                    sf.give(last)
                s_written()
                for q in range(4):
                    dst = vbank()
                    for i in range(4):
                        last = mm(dst[:, i * P:(i + 1) * P], qT[:, 4 * q + i, :], keysT[:, i % 2, :], start=True, stop=True)
                    vf.give(last)

            used, dg = Count(v_used), Count(diag_ready)
            landed = [Count(s, step=16) for s in v_in]
            for t in range(TILES):
                if t:
                    pe.wait_ge(y_out_ready, t)
                else:
                    pe.wait_ge(idx_ready, 1)
                for n in range(2):
                    mm(acc[n][:, :], zero, lnp[:, 0, 0:512], start=True, stop=False, skip_group_check=True)
                with loop(pe, BLOCKS, (dg, 1), *((c, 1) for c in landed)):
                    dg.take(pe)
                    for j in range(PB):
                        landed[j].take(pe)
                        mm(acc[0][:, :], diag[:, j, :], vslot[j][:, 0:512], start=False, stop=False, skip_group_check=True)
                        mm(acc[1][:, :], diag[:, j, :], vslot[j][:, 512:1024], start=False, stop=False,
                           skip_group_check=True).then_inc(v_used, 1)
                for n in range(2):
                    last = mm(acc[n][:, :], zero, lnp[:, 0, 0:512], start=False, stop=True, skip_group_check=True)
                last.then_inc(acc_full, 1)

        @block.scalar
        def _(act):
            own = Own(act, act_step)
            sf, sd = Count(sb_filled), Count(sb_drained, start=3)
            act.sem_inc(sb_drained, 3)

            def bank():
                k = sf.n % 3
                sf.take(act)
                return psum[3 + k]

            def f(o, i, func=ACT.Copy, **kw):
                return nc.scalar.activation(o, i, func, **kw)

            with loop(act, 4, (sf, 6), (sd, 6)) as i:
                for j in range(6):
                    src = bank()
                    row = BIG[:, ds(i * (6 * RAW) + j * RAW, RAW)]
                    f(row[:, 3:3 + SEQ], src[:, 0:SEQ])
                    sd.give(f(row[:, 3 + SEQ:RAW].rearrange("p (b s) -> p b s", b=DEC_B)[:, :, 3:SEG],
                              src[:, SEQ:TOK].rearrange("p (b s) -> p b s", b=DEC_B)))
            for t in range(TILES):
                src = bank()
                sd.give(f(dtr[:, t * SH:(t + 1) * SH], src[:, 0:SH]))
            act.wait_ge(dt_v, 1)
            own(f(dtu, dta, ACT.Exp, scale=-1.0), Count(dt_e))
            f(negA, headp[:, SH:2 * SH], ACT.Exp).then_inc(dt_e, 1)
            act.wait_ge(dt_v, 2)
            f(dtw, dtw, ACT.Ln).then_inc(dt_e, 1)
            act.wait_ge(conv_done, CC)
            for q in range(6):
                last = f(xc[:, 4 * q:4 * q + 4, :], xc[:, 4 * q:4 * q + 4, :], ACT.Silu)
            last.then_inc(silu_done, 1)
            for q in range(6):
                src = bank()
                sd.give(f(tails[0:27, q * 512:(q + 1) * 512], src[0:27, :]))

            act.wait_ge(cache_in, 16 * 6)
            for t in range(TILES):
                src = bank()
                sd.give(f(kT[0:64, 0:4, t * P:(t + 1) * P], src[0:64, :].rearrange("p (v s) -> p v s", v=4)))
                src = bank()
                sd.give(f(kT[0:64, 4, t * P:(t + 1) * P], src[0:64, 0:P]))
            for v in range(5):
                src = bank()
                sd.give(f(kcT[:, v, :, :], src[:, :].rearrange("p (j s) -> p j s", j=4)))

            def exps(n):
                act.wait_ge(max_ready, n + 1)
                t = n // KVH
                S = P if t == 0 else 2 * P
                for r in range(REP):
                    last = f(lm[n % 2][:, r, 0:S], lm[n % 2][:, r, 0:S], ACT.Exp, scale=LOG_SCALE,
                             bias=nmx[:, 4 * (n % 2) + r:4 * (n % 2) + r + 1],
                             accum_out=sums[:, 4 * (n % 2) + r:4 * (n % 2) + r + 1])
                last.then_inc(exp_done, 1)

            def keep(n):
                t, v = n // KVH, n % KVH
                for half in range(2):
                    src = bank()
                    if half == 0 or t > 0:
                        sd.give(f(PT[:, half, :, :], src[:, :].rearrange("p (r s) -> p r s", r=REP)))
                    else:
                        sd.give(f(PT[:, 1, 0, :], src[:, 0:P]))
                if n == 0:
                    act.wait_ge(tails_out, 32)
                src = bank()
                sd.give(f(attnT[:, 2 * v:2 * v + 2, t * P:(t + 1) * P], src[:, 0:256].rearrange("p (r s) -> p r s", r=2)))

            for n in range(TILES * KVH):
                exps(n)
                if n:
                    keep(n - 1)
            keep(TILES * KVH - 1)

            act.wait_ge(sum_ready, 1)
            f(ex[:, :, 0:2 * SH], acs, ACT.Exp)
            f(ex[:, :, 2 * SH:3 * SH], ex[:, :, 2 * SH:3 * SH], ACT.Exp).then_inc(ex_ready, 1)
            for t in range(TILES):
                if t:
                    act.wait_ge(y_done, t)
                else:
                    act.wait_ge(vb_filled, before["ssd"][0])
                for q in range(5):
                    src = bank()
                    sd.give(f(xbt[:, q * 512:(q + 1) * 512], src[:, :]))
                if t == 2:
                    src = bank()
                    sd.give(f(dec.rearrange("p c b -> p (c b)"), src[:, 0:P], ACT.Exp))
                for g in range(G):
                    act.wait_ge(seg_ready, t * G + g + 1)
                    f(MT, MT, ACT.Exp).then_inc(seg_exp, 1)
                    if t == 2:
                        if g == 0:
                            act.wait_ge(pso_out, 16)
                        for c in range(4):
                            for q in range(2):
                                src = bank()
                                sd.give(f(pT[:, 4 * q:4 * q + 4, c * P:(c + 1) * P],
                                          src[:, :].rearrange("p (b s) -> p b s", b=4)))
                if t == 1:
                    for q in range(4):
                        src = bank()
                        sd.give(f(pso[:, q * 512:(q + 1) * 512], src[:, :]))

            act.wait_ge(y_done, 3)
            with loop(act, 2, (sf, 6), (sd, 6)) as i:
                act.wait_ge(gated, i * 6 + 1)
                for j in range(6):
                    src = bank()
                    sd.give(f(zs[:, j, :], src[:, :], ACT.Silu))
            act.wait_ge(ms_ready, 1)
            f(rstd, ms, ACT.Sqrt, scale=1.0 / 512, bias=eps).then_inc(rms_root, 1)
            for t in range(TILES):
                for q in range(4):
                    src = bank()
                    for i in range(4):
                        last = f(yT[:, 4 * q + i, t * P:(t + 1) * P], src[:, i * P:(i + 1) * P],
                                 scale=normT[:, 4 * q + i:4 * q + i + 1])
                    sd.give(last)
            pre = Count(gate_pre)
            with loop(act, 2, (pre, 6)):
                for j in range(6):
                    pre.take(act)
                    f(gt[:, j, :], gt[:, j, :], ACT.Sigmoid).then_inc(gate_ready, 1)
            for t in range(TILES):
                for q in range(2):
                    src = bank()
                    sd.give(f(xT[:, 4 * q:4 * q + 4, t * P:(t + 1) * P], src[:, :].rearrange("p (k s) -> p k s", k=4)))

            def root(m, ready, done):
                act.wait_ge(ready, m + 1)
                f(rstd[:, 0:1], mv[:, 1:2], ACT.Sqrt, bias=eps).then_inc(done, 1)

            for t in range(TILES):
                root(t, var1_ready, root1_ready)
            for t in range(TILES):
                for q in range(2):
                    src = bank()
                    sd.give(f(xT[:, 4 * q:4 * q + 4, t * P:(t + 1) * P], src[:, :].rearrange("p (k s) -> p k s", k=4)))
            act.wait_ge(h_ready, 3)
            with loop(act, 2, (sf, 6), (sd, 6)) as i:
                for j in range(6):
                    b, t = j // 3, j % 3
                    src = bank()
                    sd.give(f(YD[:, ds(i * 1024 + (t * 2048 + b * 512), 512)], src[:, :]))
            src = bank()
            sd.give(f(keysT, src[:, 0:256].rearrange("p (a n) -> p a n", a=2)))
            for t in range(TILES):
                for q in range(4):
                    src = bank()
                    sd.give(f(qT[:, 4 * q:4 * q + 4, :], src[:, :].rearrange("p (c s) -> p c s", c=4)))

            for t in range(TILES):
                act.wait_ge(score_e, t + 1)
                f(ts16, ts16, ACT.Exp).then_inc(score_v, 1)
                dots_c, w_c, vu = Count(dot_done), Count(w_ready), Count(v_used)
                dots_c.n, w_c.n, vu.n = PB + t * BLOCKS * PB, t * BLOCKS, t * BLOCKS * PB
                with loop(act, BLOCKS, (dots_c, PB), (w_c, 1), (vu, PB)):
                    dots_c.n += PB - 1
                    dots_c.take(act)
                    f(gl, dots, ACT.Gelu).then_inc(gelu_done, 1)
                    w_c.take(act)
                    vu.n += PB - 1
                    vu.take(act)
                    for j in range(PB):
                        last = f(diag[:, j, :], ident, scale=w8[:, j:j + 1])
                    last.then_inc(diag_ready, 1)
                root(t, var2_ready, root2_ready)

        @block.vector
        def _(dve):
            own = Own(dve, dve_step)
            vf, vd = Count(vb_filled), Count(vb_drained, start=3)
            dve.sem_inc(vb_drained, 3)
            tt, tsc, stt = nc.vector.tensor_tensor, nc.vector.tensor_scalar, nc.vector.scalar_tensor_tensor
            cp = nc.vector.tensor_copy

            def bank():
                k = vf.n % 3
                vf.take(dve)
                return psum[k]

            def bc(ap, shape):
                return ap.to_broadcast([P] + list(shape))

            for t in range(TILES):
                for q in range(2):
                    src = bank()
                    vd.give(cp(xT[:, 4 * q:4 * q + 4, t * P:(t + 1) * P], src[:, :].rearrange("p (k s) -> p k s", k=4)))
            for q in range(2):
                src = bank()
                own(cp(rowsT[:, 12 * q:12 * q + 12, :], src[:, 0:12 * ROWS].rearrange("p (c r) -> p c r", c=12)), vd)
            src = bank()
            own(cp(normT[:, :], src[:, 0:16]), vd)
            own.settle()
            own(nc.vector.memset(xraw[:, :, 0:3], 0.0))
            own(cp(xraw[:, :, 3 + SEQ:RAW].rearrange("p c (b s) -> p c b s", b=DEC_B)[:, :, :, 0:3],
                   rowsT[:, :, 0:24].rearrange("p c (b j) -> p c b j", b=DEC_B)))
            own.settle()

            arrived = Count(sb_drained, start=3)
            conv_c = Count(conv_done)
            with loop(dve, 4, (own.step, 6 * 6), (arrived, 6), (conv_c, 6)) as i:
                for j in range(6):
                    arrived.take(dve)
                    row = BIG[:, ds(i * (6 * RAW) + j * RAW, RAW)]
                    res = C[:, ds(i * (6 * TOK) + j * TOK, TOK)]
                    wr = rowsT.rearrange("p c r -> p (c r)")[:, ds(i * (6 * ROWS) + j * ROWS, ROWS)]
                    streams = row[:, 3 + SEQ:RAW].rearrange("p (b s) -> p b s", b=DEC_B)
                    parts = [(res[:, 0:SEQ], lambda k: row[:, k:k + SEQ]),
                             (res[:, SEQ:TOK].rearrange("p (b s) -> p b s", b=DEC_B), lambda k: streams[:, :, k:k + DEC_S])]
                    for k in range(CW):
                        for n, (o, tap) in enumerate(parts):
                            if k == 0:
                                own(tsc(o, tap(0), wr[:, 24:25], wr[:, 28:29], ALU.mult, ALU.add))
                            elif k < CW - 1:
                                own(stt(o, tap(k), wr[:, 24 + k:25 + k], o, ALU.mult, ALU.add))
                            elif n == 0:
                                stt(o, tap(k), wr[:, 24 + k:25 + k], o, ALU.mult, ALU.add)
                            else:
                                conv_c.give(stt(o, tap(k), wr[:, 24 + k:25 + k], o, ALU.mult, ALU.add))
                        if k < CW - 1:
                            own.settle()
            tail = xc_tail(BIG)
            cp(tail[:, :, 0:3], xraw[:, :, SEQ:SEQ + 3])
            cp(tail[:, :, 3:27].rearrange("p c (b j) -> p c b j", b=DEC_B),
               xraw[:, :, 3 + SEQ:RAW].rearrange("p c (b s) -> p c b s", b=DEC_B)[:, :, :, DEC_S:SEG]).then_inc(tails_ready, 1)

            dve.wait_ge(par_in, 48)
            dve.wait_ge(sb_drained, 3 + before["dt"][1] + 3)
            t3 = [TILES, SH]
            own(tt(dtr.rearrange("p (t n) -> p t n", t=TILES), dtr.rearrange("p (t n) -> p t n", t=TILES),
                   bc(headp[:, 0:SH].unsqueeze(1), t3), ALU.add))
            own.settle()
            own(tsc(dta, dtr, -1.0, None, ALU.mult))
            own.settle()
            tt(dta, dta, dtr, ALU.max).then_inc(dt_v, 1)
            dve.wait_ge(dt_e, 2)
            tsc(dtw, dtu, 1.0, None, ALU.add).then_inc(dt_v, 1)
            dve.wait_ge(dt_v, 2)
            own(tsc(dtv, dtu, 1.0, -1.0, ALU.add, ALU.add))
            dve.wait_ge(dt_e, 3)
            own.settle()
            own(tsc(dta, dtv, 0.0, None, ALU.is_equal))
            own.settle()
            own(tt(dtv, dtv, dta, ALU.add))
            own(tt(dtw, dtw, dta, ALU.add))
            own.settle()
            own(nc.vector.reciprocal(dtv, dtv))
            own.settle()
            own(tt(dtw, dtw, dtu, ALU.mult))
            own.settle()
            own(tt(dtv, dtv, dtw, ALU.mult))
            own.settle()
            own(stt(dtv, dtr, 0.0, dtv, ALU.max, ALU.add))
            own(tsc(negA, negA, -1.0, None, ALU.mult))
            own.settle()
            tt(av.rearrange("p (t n) -> p t n", t=TILES), dtv.rearrange("p (t n) -> p t n", t=TILES),
               bc(negA.unsqueeze(1), t3), ALU.mult).then_inc(a_ready, 1)

            with loop(dve, 2, (vf, 6), (vd, 6)) as i:
                for j in range(6):
                    src = bank()
                    vd.give(cp(B[:, ds(i * 1024 + ((j % 3) * 2048 + (j // 3) * 512), 512)], src[:, :]))
            vd.upto(dve)

            def rope(o, heads, tmp):
                v = [qkv[:, t, o:o + heads * HD].rearrange("p (h n) -> p h n", h=heads) for t in range(TILES)]
                shape = [heads, 8]
                T = [tmp[k][:, 0:TILES * heads * 8].rearrange("p (t h n) -> p t h n", t=TILES, h=heads) for k in range(4)]
                for t in range(TILES):
                    c, s = bc(cos[:, t, :].unsqueeze(1), shape), bc(sin[:, t, :].unsqueeze(1), shape)
                    own(tt(T[0][:, t], v[t][:, :, 0:8], c, ALU.mult))
                    own(tt(T[1][:, t], v[t][:, :, 8:16], s, ALU.mult))
                    own(tt(T[2][:, t], v[t][:, :, 8:16], c, ALU.mult))
                    own(tt(T[3][:, t], v[t][:, :, 0:8], s, ALU.mult))
                own.settle()
                for t in range(TILES):
                    own(tt(v[t][:, :, 0:8], T[0][:, t], T[1][:, t], ALU.subtract))
                    own(tt(v[t][:, :, 8:16], T[2][:, t], T[3][:, t], ALU.add))
                own.settle()

            dve.wait_ge(sb_filled, before["attention"][1])
            rope(0, HEADS + KVH, rtmp)
            rope(O_QI, IH + 1, rtmp)
            dve.sem_inc(rope_done, 1)

            def keep_q(t):
                src = bank()
                v = src[:, :].rearrange("p (r s) -> p r s", r=REP)
                if t < 2:
                    vd.give(cp(qn[0:64, :, :], v[0:64]))
                else:
                    cp(qn[0:64, :, :], v[0:64])
                    for r in range(REP):
                        last = tt(qm[:, r, :, :], bc(v[:, r, :].unsqueeze(1), [4, P]), pair, ALU.mult)
                    vd.give(last)

            def select(t):
                S = P if t == 0 else 2 * P
                s, tmp, neg = score[:, 0:S], scoret[:, 0:S], negm[:, 0:S]
                for q in range(2):
                    src = bank()
                    for r in range(2):
                        hh = 2 * q + r
                        wi = qkv[:, t, O_WI + hh:O_WI + hh + 1]
                        o = s if hh == 0 else tmp
                        ins = tsc(o, src[:, r * 256:r * 256 + S], 0.0, wi, ALU.max, ALU.mult)
                        own(ins, vd if r == 1 else None)
                        own.settle()
                        if hh:
                            own(tt(s, s, tmp, ALU.add))
                            own.settle()
                own(tt(s, s, adm[:, t, 0:S], ALU.mult))
                own.settle()
                own(tt(s, s, nadm[:, t, 0:S], ALU.add))
                own.settle()
                k = TOPK_P if t < 2 else TOPK_S
                while k > 0:
                    own(nc.vector.max(m8, s))
                    own.settle()
                    if k < 8:
                        own(nc.vector.memset(m8[:, k:8], GONE))
                        own.settle()
                    own(nc.vector.match_replace(s, m8, s, GONE))
                    own.settle()
                    k -= 8
                own(tsc(neg, s, GONE, NEG, ALU.not_equal, ALU.mult))
                own.settle()

            def logits(n):
                t = n // KVH
                S = P if t == 0 else 2 * P
                if n >= 2:
                    dve.wait_ge(sb_filled, before["attention"][1] + 11 + 3 * (n - 2) + 2)
                for q in range(2):
                    src = bank()
                    own(tt(lm[n % 2][:, 2 * q:2 * q + 2, 0:S], src[:, :].rearrange("p (r s) -> p r s", r=2)[:, :, 0:S],
                           bc(negm[:, 0:S].unsqueeze(1), [2, S]), ALU.add), vd)
                own.settle()
                o = 4 * (n % 2)
                own(nc.vector.tensor_reduce(nmx[:, o:o + 4], lm[n % 2][:, :, 0:S], AX_X, ALU.max))
                own.settle()
                tsc(nmx[:, o:o + 4], nmx[:, o:o + 4], -LOG_SCALE, None, ALU.mult).then_inc(max_ready, 1)

            def normalise(n):
                S = P if n < KVH else 2 * P
                o = 4 * (n % 2)
                dve.wait_ge(exp_done, n + 1)
                own(nc.vector.reciprocal(rec[:, o:o + 4], sums[:, o:o + 4]))
                own.settle()
                tt(lm[n % 2][:, :, 0:S], lm[n % 2][:, :, 0:S], bc(rec[:, o:o + 4].unsqueeze(2), [REP, S]),
                   ALU.mult).then_inc(probs_ready, 1)

            dve.wait_ge(cache_in, 16 * 6)
            for t in range(TILES):
                keep_q(t)
                select(t)
                for v in range(KVH):
                    n = t * KVH + v
                    keep_q(t)
                    logits(n)
                    normalise(n)
            for j in range(6):
                src = bank()
                vd.give(cp(ya[:, j % 3, (j // 3) * 512:(j // 3 + 1) * 512], src[:, :]))

            for t in range(TILES):
                src = bank()
                own(cp(acs[:, t, :], src[:, 0:64]), vd)
            own.settle()
            tt(ex[:, :, 2 * SH:3 * SH], acs[:, :, SH:2 * SH], acs[:, :, 0:SH], ALU.subtract).then_inc(sum_ready, 1)
            dve.wait_ge(ex_ready, 1)
            dve.wait_ge(kv_out, 16 * 9)
            for t in range(TILES):
                dve.wait_ge(sb_drained, 3 + before["ssd"][1] + 5 * (t + 1) + (4 + 1 if t == 2 else 0))
                xs = xbt[:, 0:DI].rearrange("p (h n) -> p h n", h=SH)
                own(tt(xdt.rearrange("p (h n) -> p h n", h=SH), xs, bc(dtv[:, t * SH:(t + 1) * SH].unsqueeze(2), [SH, HD]), ALU.mult))
                own.settle()
                own(tt(xdtd.rearrange("p (h n) -> p h n", h=SH), xdt.rearrange("p (h n) -> p h n", h=SH),
                       bc(ex[:, t, 2 * SH:3 * SH].unsqueeze(2), [SH, HD]), ALU.mult))
                for g in range(G):
                    src = bank()
                    own(tt(cbm, src[:, 0:P], tri[:, t // 2, :], ALU.mult), vd)
                    for q in range(2):
                        src = bank()
                        for i in range(4):
                            hh = g * 8 + q * 4 + i
                            ins = tsc(MT[:, q * 4 + i, :], src[:, i * P:(i + 1) * P], acs[:, t, hh:hh + 1], 0.0,
                                      ALU.subtract, ALU.min)
                            own(ins, vd if i == 3 else None)
                    own.settle()
                    if t == 2:
                        own(tt(CTm, bc(xc[:, 20 + g, 2 * P:3 * P].unsqueeze(1), [DEC_B, P]), blkcol, ALU.mult))
                        own(tt(Bm, bc(xbt[:, DI + g * P:DI + (g + 1) * P].unsqueeze(1), [DEC_B, P]),
                               bc(blk.unsqueeze(2), [DEC_B, P]), ALU.mult))
                        own.settle()
                    dve.sem_inc(seg_ready, 1)
                    dve.wait_ge(seg_exp, t * G + g + 1)
                    tt(MT, MT, bc(cbm.unsqueeze(1), [8, P]), ALU.mult).then_inc(mt_ready, 1)
                    if t == 2:
                        for c in range(4 * g, 4 * g + 4):
                            for q in range(2):
                                src = bank()
                                for b in range(4):
                                    bb = 4 * q + b
                                    last = stt(sst[c % 2][:, bb, :], sst[c % 2][:, bb, :], dec[:, c, bb:bb + 1],
                                               src[:, b * P:(b + 1) * P], ALU.mult, ALU.add)
                                vd.give(last)
                                vd.upto(dve)
                                dve.sem_inc(new_ready, 1)
                    yg = y[:, t, g * 512:(g + 1) * 512]
                    y3 = yg.rearrange("p (r n) -> p r n", r=8)
                    tmp = ytmp.rearrange("p (r n) -> p r n", r=8)
                    hs = slice(g * 8, g * 8 + 8)
                    own(tt(y3, xs[:, hs, :], bc(headp[:, 2 * SH + g * 8:2 * SH + g * 8 + 8].unsqueeze(2), [8, HD]), ALU.mult))
                    own.settle()
                    if t > 0:
                        src = bank()
                        own(tt(tmp, src[:, :].rearrange("p (r n) -> p r n", r=8), bc(ex[:, t, hs].unsqueeze(2), [8, HD]),
                               ALU.mult), vd)
                        own.settle()
                        own(tt(yg, yg, ytmp, ALU.add))
                        own.settle()
                    src = bank()
                    own(tt(yg, yg, src[:, :], ALU.add), vd)
                    if t < 2:
                        src = bank()
                        st = stateT[:, g * 512:(g + 1) * 512]
                        if t == 0:
                            own(cp(st, src[:, :]), vd)
                        else:
                            s3 = st.rearrange("p (r n) -> p r n", r=8)
                            own(tt(s3, s3, bc(ex[:, 1, SH + g * 8:SH + g * 8 + 8].unsqueeze(2), [8, HD]), ALU.mult))
                            own.settle()
                            own(tt(st, st, src[:, :], ALU.add), vd)
                own.settle()
                dve.sem_inc(y_done, 1)

            dve.sem_inc(gated, 1)
            zin, gated_c = Count(sb_drained), Count(gated, start=1)
            zin.n = 3 + before["z"][1]
            with loop(dve, 2, (zin, 6), (gated_c, 6)) as i:
                for j in range(6):
                    zin.take(dve)
                    yv = B[:, ds(i * 1024 + ((j % 3) * 2048 + (j // 3) * 512), 512)]
                    gated_c.give(tt(yv, yv, zs[:, j, :], ALU.mult))
            dve.wait_ge(gated, 13)
            dve.wait_ge(bg_in, 16)
            for t in range(TILES):
                for g in range(G):
                    yg = y[:, t, g * 512:(g + 1) * 512]
                    own(nc.vector.tensor_tensor_reduce((zs if t * G + g < 6 else gt)[:, (t * G + g) % 6, :], yg, yg, 1.0, 0.0,
                                                       ALU.mult, ALU.add, ms[:, t * G + g:t * G + g + 1]))
            own.settle()
            dve.sem_inc(ms_ready, 1)
            dve.wait_ge(rms_root, 1)
            own(nc.vector.reciprocal(rstd, rstd))
            own.settle()
            for t in range(TILES):
                y4 = y[:, t, :].rearrange("p (g n) -> p g n", g=G)
                tt(y4, y4, bc(rstd[:, t * G:(t + 1) * G].unsqueeze(2), [G, 512]), ALU.mult).then_inc(yn_ready, 1)

            with loop(dve, 2, (vf, 6), (vd, 6)) as i:
                for j in range(6):
                    b, t = j // 3, j % 3
                    src = bank()
                    o = YD[:, ds(i * 512 + (3072 + t * D), 512)]
                    if b == 0:
                        vd.give(cp(o, src[:, :]))
                    else:
                        if t == 0:
                            vd.upto(dve)
                        vd.give(tt(o, o, src[:, :], ALU.add))
            vd.upto(dve)

            mixed_c, gr, gp = Count(mixed_ready), Count(gate_ready), Count(gate_pre)
            with loop(dve, 2, (vf, 6), (vd, 6), (gr, 6), (gp, 6), (own.step, 6), (mixed_c, 3)) as i:
                for b in range(2):
                    bgv = bg[:, ds(i * 512 + b * 1024, 512)]
                    for t in range(TILES):
                        src = bank()
                        own(tt(gt[:, 3 * b + t, :], src[:, :], bgv, ALU.add), vd)
                    vd.upto(dve)
                    dve.sem_inc(gate_pre, TILES)
                    gp.n += TILES
                for t in range(TILES):
                    gr.take(dve)
                    yav = YD[:, ds(i * 512 + t * D, 512)]
                    own(tt(yav, yav, gt[:, t, :], ALU.mult))
                for t in range(TILES):
                    gr.take(dve)
                    own(tt(gt[:, 3 + t, :], gt[:, 3 + t, :], YD[:, ds(i * 512 + (3072 + t * D), 512)], ALU.mult))
                own.settle()
                for t in range(TILES):
                    yav = YD[:, ds(i * 512 + t * D, 512)]
                    mixed_c.give(tt(yav, yav, gt[:, 3 + t, :], ALU.add))

            dve.wait_ge(x2_in, 32)
            for j in range(6):
                src = bank()
                c = slice((j // 3) * 512, (j // 3 + 1) * 512)
                own(stt(h[:, j % 3, c], x2[:, j % 3, c], ALPHA, src[:, :], ALU.mult, ALU.add), vd)
            own.settle()
            dve.wait_ge(lnp_in, 64)

            def layer_norm(v, o, t, which, ready, done, final):
                for q in range(2):
                    own(nc.vector.bn_stats(bns[:, 6 * q:6 * q + 6], v[:, q * 512:(q + 1) * 512]))
                own.settle()
                own(nc.vector.bn_aggr(mv, bns))
                own.settle()
                dve.sem_inc(ready, 1)
                dve.wait_ge(done, t + 1)
                own(nc.vector.reciprocal(rstd[:, 1:2], rstd[:, 0:1]))
                own.settle()
                own(tsc(v, v, mv[:, 0:1], rstd[:, 1:2], ALU.subtract, ALU.mult))
                own.settle()
                own(tt(v, v, lnp[:, which, :], ALU.mult))
                own.settle()
                tt(o, v, lnp[:, which + 1, :], ALU.add).then_inc(final, 1)

            for t in range(TILES):
                layer_norm(h[:, t, :], h[:, t, :], t, 0, var1_ready, root1_ready, h_ready)

            for t in range(TILES):
                for q in range(4):
                    src = bank()
                    own(cp(sc[t][:, q * 512:(q + 1) * 512], src[:, :]), vd)
            own.settle()
            own(nc.vector.memset(zero, 0.0))

            def pick(t):
                for c in range(16):
                    s = sc[t][:, c * NK:(c + 1) * NK]
                    own(nc.vector.max(v16[:, c, 0:8], s))
                    own.settle()
                    own(nc.vector.max_index(i16[:, c, 0:8], v16[:, c, 0:8], s))
                    own.settle()
                    own(nc.vector.match_replace(s, v16[:, c, 0:8], s, GONE))
                    own.settle()
                    own(nc.vector.max(v16[:, c, 8:16], s))
                    own.settle()
                    own(nc.vector.max_index(i16[:, c, 8:16], v16[:, c, 8:16], s))
                own.settle()
                own(cp(f16, i16))
                v4 = v16.rearrange("p (h a) k -> p h a k", a=2)
                for hh in range(PH):
                    own(tt(cand[:, hh * 256:(hh + 1) * 256].rearrange("p (i j) -> p i j", i=PTOP),
                           bc(v4[:, hh, 0, :].unsqueeze(2), [PTOP, PTOP]), bc(v4[:, hh, 1, :].unsqueeze(1), [PTOP, PTOP]),
                           ALU.add))
                own.settle()
                for hh in range(PH):
                    s = cand[:, hh * 256:(hh + 1) * 256]
                    o = hh * PTOP
                    own(nc.vector.max(ts16[:, hh, 0:8], s))
                    own.settle()
                    own(nc.vector.max_index(pos[:, o:o + 8], ts16[:, hh, 0:8], s))
                    own.settle()
                    own(nc.vector.match_replace(s, ts16[:, hh, 0:8], s, GONE))
                    own.settle()
                    own(nc.vector.max(ts16[:, hh, 8:16], s))
                    own.settle()
                    own(nc.vector.max_index(pos[:, o + 8:o + 16], ts16[:, hh, 8:16], s))
                own.settle()
                f4 = f16.rearrange("p (h a) k -> p h a k", a=2)
                for half, (op, by, e) in enumerate(((ALU.logical_shift_right, 4, e1), (ALU.bitwise_and, 15, e2))):
                    own(tsc(ph, pos, by, None, op))
                    own.settle()
                    own(cp(phf, ph))
                    own.settle()
                    own(tt(hot, bc(phf.unsqueeze(2), [128, PTOP]), bc(iota.unsqueeze(1), [128, PTOP]), ALU.is_equal))
                    own.settle()
                    for hh in range(PH):
                        hv = hot[:, hh * PTOP:(hh + 1) * PTOP, :]
                        own(tt(hv, hv, bc(f4[:, hh, half, :].unsqueeze(1), [PTOP, PTOP]), ALU.mult))
                    own.settle()
                    own(nc.vector.tensor_reduce(e, hot, AX_X, ALU.add))
                    own.settle()
                own(stt(eidx[:, t, :], e1, float(NK), e2, ALU.mult, ALU.add))
                own(cp(s8, ts16[:, :, 0]))
                own.settle()
                tt(ts16, ts16, bc(s8.unsqueeze(2), [PH, PTOP]), ALU.subtract).then_inc(score_e, 1)
                dve.sem_inc(idx_ready, 1)
                dve.wait_ge(score_v, t + 1)
                own(nc.vector.tensor_reduce(s8, ts16, AX_X, ALU.add))
                own.settle()
                own(nc.vector.reciprocal(s8, s8))
                own.settle()
                own(tt(gate[:, t, :].rearrange("p (h k) -> p h k", h=PH), ts16, bc(s8.unsqueeze(2), [PH, PTOP]), ALU.mult))
                own.settle()

            landed = [Count(s, step=16) for s in u_in]
            dot_c, gelu_c, w_c = Count(dot_done), Count(gelu_done), Count(w_ready)
            for t in range(TILES):
                pick(t)
                with loop(dve, BLOCKS, (gelu_c, 1), (w_c, 1), (dot_c, PB), *((c, 1) for c in landed)) as i:
                    for j in range(PB):
                        landed[j].take(dve)
                        dot_c.give(nc.vector.tensor_tensor_reduce(uslot[j], uslot[j], h[:, t, :], 1.0, 0.0,
                                                                  ALU.mult, ALU.add, dots[:, j:j + 1]))
                    gelu_c.take(dve)
                    w_c.give(tt(w8, gl, gate[:, t, ds(i * PB, PB)], ALU.mult))
                dve.wait_ge(acc_full, t + 1)
                for n in range(2):
                    c = slice(n * 512, (n + 1) * 512)
                    own(stt(h[:, t, c], h[:, t, c], ALPHA, acc[n][:, :], ALU.mult, ALU.add))
                own.settle()
                if t:
                    dve.wait_ge(y_out, 16 * t)
                layer_norm(h[:, t, :], yout, t, 2, var2_ready, root2_ready, y_out_ready)


def xc_tail(BIG):
    return BIG[:, CC * RAW:CC * RAW + CC * 27].rearrange("p (c j) -> p c j", c=CC)


_INS = ['x_prompt', 'x_sample', 'cache_k', 'cache_v', 'cache_kidx', 'state_conv', 'state_ssm', 'w_in', 'b_gate', 'conv_w',
        'conv_b', 'dt_bias', 'a_log', 'd_skip', 'ssm_norm_w', 'w_attn_br', 'w_ssm_br', 'w_out', 'ln1_g', 'ln1_b',
        'peer_wq', 'peer_keys1', 'peer_keys2', 'peer_u', 'peer_v', 'ln2_g', 'ln2_b']
_OUTS = [("y_prompt", (1, SEQ, D)), ("y_sample", (DEC_B, DEC_S, D)), ("p_k", (1, 1, SEQ, KVH, HD)), ("p_v", (1, 1, SEQ, KVH, HD)),
         ("p_kidx", (1, 1, SEQ, HD)), ("p_conv", (1, 1, CW - 1, CONV)), ("p_ssm", (1, 1, SH, HD, N)),
         ("s_k", (1, DEC_B, DEC_S, KVH, HD)), ("s_v", (1, DEC_B, DEC_S, KVH, HD)), ("s_kidx", (1, DEC_B, DEC_S, HD)),
         ("s_conv", (1, DEC_B, CW - 1, CONV)), ("s_ssm", (1, DEC_B, SH, HD, N))]


def kernel(**inputs):
    import concourse.bacc as _bacc
    from concourse import mybir as _mybir
    from concourse.bass_utils import run_bass_kernel_spmd as _run

    nc = _bacc.Bacc("TRN2", target_bir_lowering=False, num_devices=1)
    arrays, a, out = {}, {}, {}
    table, where = const_table()
    for name in _INS + ["table"]:
        v = np.ascontiguousarray(table if name == "table" else inputs[name])
        arrays[f"in_{name}_dram"] = v
        a[name] = nc.dram_tensor(f"in_{name}_dram", v.shape, _mybir.dt.from_np(v.dtype), kind="ExternalInput").ap()
    for name, shape in _OUTS:
        out[name] = nc.dram_tensor(f"out_{name}_dram", shape, F32, kind="ExternalOutput").ap()
    build(nc, a, out, where)
    r = _run(nc, [arrays], core_ids=[0])
    return tuple(r.results[0][f"out_{name}_dram"] for name, _ in _OUTS)
```

```python
from contextlib import ExitStack, contextmanager

import numpy as np

import concourse.bass as bass
from concourse import mybir
from concourse.alu_op_type import AluOpType as ALU

ACT = mybir.ActivationFunctionType
F32 = mybir.dt.float32
U32 = mybir.dt.uint32
AX_X = mybir.AxisListType.X
ds = bass.ds

P = 128
D = 1024
KC = D // P
TILES = 3
TOK = TILES * P
SEQ, DEC_B, DEC_S, PAST = 256, 8, 16, 128
HEADS, HD, KVH, REP = 16, 64, 4, 4
IH = 4
CHUNK = 64
TOPK_P, TOPK_S = 64, 36
DI, SH, G, N = 2048, 32, 4, 128
CONV, CW = 3072, 4
CC = CONV // P
PH, NK, PTOP = 8, 128, 16
ALPHA = 2.0 ** 0.25
EPS = 1e-5
NEG = -1e30
GONE = -3e38
LOG_SCALE = HD ** -0.5

O_K, O_V, O_QI, O_KI, O_WI = 1024, 1280, 1536, 1792, 1856
O_Z = 1860
O_XBC = O_Z + DI
O_DT = O_XBC + CONV
O_GATE = O_DT + SH

SEG = DEC_S + CW - 1
ROWS = DEC_B * (CW - 1) + CW + 1
VR, SR = 4, 2

WB = 4
BLOCKS = PH * PTOP // WB
PROMPT_BLOCKS = 2 * BLOCKS
TICKS = PROMPT_BLOCKS + 2
PB = 8
PAUSES = 5


def const_table():
    t = np.arange(P)
    parts = {}
    parts["ident"] = np.eye(P)
    stream = t // DEC_S
    same = (stream[:, None] == stream[None, :])
    causal = (t[:, None] <= t[None, :])
    parts["tri"] = np.stack([causal, causal & same], 1)
    parts["same"] = np.stack([np.ones((P, P)), same], 1)
    adm = np.zeros((P, TILES, 2 * P))
    for tile in range(2):
        q = (tile * P + t) // CHUNK
        k = np.arange(2 * P) // CHUNK
        adm[:, tile] = k[None, :] <= q[:, None]
    adm[:, 2, :P] = 1
    adm[:, 2, P:] = same
    parts["adm"] = adm
    parts["nadm"] = (1 - adm) * NEG
    parts["blk"] = stream[:, None] == np.arange(DEC_B)[None, :]
    parts["blkcol"] = np.broadcast_to(np.arange(DEC_B)[:, None] == stream[None, :], (P, DEC_B, P))
    pair = np.zeros((P, 4, P))
    for j in range(4):
        pair[:64, j] = stream == 2 * j
        pair[64:, j] = stream == 2 * j + 1
    parts["pair"] = pair
    rd = HD // 4
    half = rd // 2
    inv = np.float32(500000.0) ** (-(np.arange(half, dtype=np.float32) * np.float32(2)) / np.float32(rd))
    pos = np.stack([t, P + t, PAST + t % DEC_S], 1).astype(np.float32)
    ang = pos[:, :, None] * inv.astype(np.float32)
    parts["cos"] = np.cos(ang.astype(np.float32))
    parts["sin"] = np.sin(ang.astype(np.float32))
    parts["iota"] = np.broadcast_to(np.arange(PTOP), (P, PTOP))
    parts["eps"] = np.full((P, 1), EPS)
    at, cols = 0, []
    where = {}
    for name, v in parts.items():
        v = np.ascontiguousarray(v, dtype=np.float32)
        where[name] = (at, v.shape[1:])
        at += int(np.prod(v.shape[1:]))
        cols.append(v.reshape(P, -1))
    return np.concatenate(cols, 1), where


class Count:

    def __init__(self, sem, start=0, step=1):
        self.sem, self.n, self.step, self.extra = sem, start, step, None

    def value(self, n=None):
        n = self.n if n is None else n
        return n * self.step if self.extra is None else (self.extra + n) * self.step

    def give(self, ins):
        ins.then_inc(self.sem, self.step)
        self.n += 1
        return ins

    def take(self, eng):
        self.n += 1
        eng.wait_ge(self.sem, self.value())

    def upto(self, eng):
        eng.wait_ge(self.sem, self.value())


class Own:

    def __init__(self, eng, sem):
        self.eng, self.step = eng, Count(sem)
        self.last = self.step

    def __call__(self, ins, signal=None):
        self.last = self.step if signal is None else signal
        return self.last.give(ins)

    def settle(self):
        self.last.upto(self.eng)


@contextmanager
def loop(eng, times, *per):
    starts = [c.n for c, _ in per]
    with eng.Fori(0, times) as i:
        for c, k in per:
            c.extra = i * k
        yield i
        for (c, k), s in zip(per, starts):
            assert c.n == s + k, (c.sem, c.n, s, k)
    for (c, k), s in zip(per, starts):
        c.extra, c.n = None, s + times * k


def turns(eng, straight, times, *per):
    if straight:
        yield from range(times)
    else:
        with loop(eng, times, *per) as i:
            yield i


class Pass:

    def __init__(self, n, tiles):
        self.n, self.tiles, self.nt, self.streams = n, tiles, len(tiles), n == 1
        self.tok = P * self.nt
        self.raw = DEC_B * SEG if self.streams else CW - 1 + SEQ

    def at(self, t):
        k = self.tiles.index(t)
        return slice(k * P, (k + 1) * P)


def build(nc, a, out, where):
    ctx = ExitStack()
    with ctx:
        def sb(name, words, dt=F32):
            return ctx.enter_context(nc.sbuf_tensor(name, [P, words], dt))

        def sem(name):
            return ctx.enter_context(nc.semaphore(name))

        cst = sb("cst", a["table"].shape[1])

        def const(name):
            at, shape = where[name]
            v = cst[:, at:at + int(np.prod(shape))]
            if len(shape) == 2:
                v = v.rearrange("p (a b) -> p a b", a=shape[0])
            return v

        ident, tri, same, adm, nadm = (const(k) for k in ("ident", "tri", "same", "adm", "nadm"))
        blk, blkcol, pair, cos, sin, iota = (const(k) for k in ("blk", "blkcol", "pair", "cos", "sin", "iota"))
        eps = const("eps")
        rowsT = sb("rowsT", CC * ROWS)[:, :].rearrange("p (c r) -> p c r", c=CC)
        normT = sb("normT", 16)
        headp = sb("headp", 3 * SH)
        wdt = sb("wdt", KC * SH)[:, :].rearrange("p (k n) -> p k n", k=KC)
        wbuf = [sb(f"wbuf{i}", KC * 512)[:, :].rearrange("p (k n) -> p k n", k=KC) for i in range(2)]
        small = sb("small", 1050)

        ZONE = 24128
        EX = 2 * WB * D
        BIG = sb("BIG", ZONE + EX + 2048 + WB * P + 2048 + D + P + 2 * TILES * P + 256)
        big = [0]

        def take(words, end=None):
            v = BIG[:, big[0]:big[0] + words]
            big[0] += words
            assert end is None or big[0] <= end, (big[0], end)
            return v

        def tiles3(v, nt):
            return v.rearrange("p (t n) -> p t n", t=nt)

        def lay(q, end):
            nt, tok, first = q.nt, q.tok, big[0]
            q.xT = take(KC * tok).rearrange("p (k t) -> p k t", k=KC)
            YD = take(nt * D + 2560)
            q.YD = YD
            q.ya = tiles3(YD[:, 0:nt * D], nt)
            q.attnT = YD[:, nt * D:2 * nt * D].rearrange("p (k t) -> p k t", k=KC)
            q.xbt = YD[:, nt * D:nt * D + 2560]
            q.ym = tiles3(YD[:, nt * D:2 * nt * D], nt)
            q.tails = YD[:, 0:3072]
            q.qp = tiles3(YD[:, 0:nt * 2048], nt)
            q.B = take(nt * 2048)
            q.qkv = q.y = tiles3(q.B, nt)
            q.C = take(CC * tok)
            q.xc = q.C.rearrange("p (c t) -> p c t", c=CC)
            q.yTv = q.C[:, 0:16 * tok].rearrange("p (k t) -> p k t", k=16)
            A = q.A = big[0]

            def cut(v, pattern=None, **kw):
                return v if pattern is None else v.rearrange(pattern, **kw)

            q.xraw2 = take(CC * q.raw)
            q.xraw = q.xraw2.rearrange("p (c t) -> p c t", c=CC)
            q.x1 = tiles3(take(nt * D), nt)
            q.nrow = DEC_B * (CW - 1) if q.streams else CW - 1
            if q.streams:
                assert big[0] - A == 4672
                q.kc = take(5 * 512).rearrange("p (v n) -> p v n", v=5)
                q.vc = take(2048).rearrange("p (b n) -> p b n", b=DEC_B)
            q.tail = take(CC * q.nrow).rearrange("p (c j) -> p c j", c=CC)
            top = big[0]
            big[0] = A
            q.kT = take(5 * tok).rearrange("p (v t) -> p v t", v=5)
            if q.streams:
                q.kcT = take(5 * 512).rearrange("p (v j s) -> p v j s", v=5, j=4)
            q.qn = take(512).rearrange("p (r t) -> p r t", r=REP)
            q.score, q.scoret, q.negm = take(256), take(256), take(256)
            if q.streams:
                assert big[0] <= A + 4672
                big[0] = A + 4672 + 5 * 512 + 2048
            q.lm = [take(1024).rearrange("p (r s) -> p r s", r=REP) for _ in range(2)]
            q.PT = take(1024).rearrange("p (h r t) -> p h r t", h=2, r=REP)
            spot = big[0]
            if q.streams:
                q.qm = take(2048).rearrange("p (r j t) -> p r j t", r=REP, j=4)
            top = max(top, big[0])
            big[0] = spot
            q.rtmp = [take(nt * 160) for _ in range(4)]
            top = max(top, big[0])
            big[0] = A
            q.xdt, q.xdtd = take(2048), take(2048)
            q.MT = take(1024).rearrange("p (r l) -> p r l", r=8)
            if q.streams:
                q.CTm = take(1024).rearrange("p (b t) -> p b t", b=DEC_B)
                q.Bm = take(1024).rearrange("p (b n) -> p b n", b=DEC_B)
                q.pT = take(4096).rearrange("p (b n) -> p b n", b=DEC_B)
                q.sst = [take(1024).rearrange("p (b n) -> p b n", b=DEC_B) for _ in range(2)]
            else:
                q.stateT, q.pso = take(2048), take(2048)
            q.cbm, q.ytmp = take(128), take(512)
            top = max(top, big[0])
            big[0] = A
            q.zs = take(2048).rearrange("p (j n) -> p j n", j=4)
            q.gt = take(2048).rearrange("p (j n) -> p j n", j=4)
            q.bg = take(2048)
            q.ln1 = take(2048).rearrange("p (a n) -> p a n", a=2)
            q.keys = take(256).rearrange("p (a n) -> p a n", a=2)
            top = max(top, big[0])
            big[0] = A
            q.qT = take(2048).rearrange("p (c t) -> p c t", c=16)
            q.x2 = tiles3(q.B[:, nt * D:2 * nt * D], nt)
            assert top - first <= end, (top, first, end)
            big[0] = top

        PR, ST = Pass(0, (0, 1)), Pass(1, (2,))
        lay(PR, ZONE + EX)
        big[0] = 0
        lay(ST, ZONE)
        rowsin = PR.YD[:, 0:3072]
        normin = PR.YD[:, 3072:3072 + P]
        SZ = ST.A
        sc = [ST.C[:, 0:2048], ST.B, ST.C[:, 0:2048]]
        room = [[BIG[:, 1024:4608], 0]]

        def tiny(words, dt=F32):
            r = room[0]
            v = r[0][:, r[1]:r[1] + words]
            r[1] += words
            assert r[1] <= r[0].shape[1], r[1]
            return v if dt is F32 else v.bitcast(dt)

        v16 = tiny(256).rearrange("p (c k) -> p c k", c=16)
        i16 = tiny(256, U32).rearrange("p (c k) -> p c k", c=16)
        f16 = tiny(256).rearrange("p (c k) -> p c k", c=16)
        ts16 = tiny(128).rearrange("p (h k) -> p h k", h=PH)
        pos, phi = tiny(128, U32), tiny(128, U32)
        phf, e1, e2 = tiny(128), tiny(128), tiny(128)
        s8 = tiny(8)
        cand = BIG[:, SZ + 9280:SZ + 9280 + 2048]
        hot = BIG[:, SZ + 9280 + 2048:SZ + 9280 + 4096].rearrange("p (k j) -> p k j", j=PTOP)
        big[0] = ZONE
        uslot = [take(D) for _ in range(WB)]
        vslot = [take(D) for _ in range(WB)]
        hP = tiles3(take(2048), 2)
        diag0 = take(WB * P)
        ln2 = take(2048).rearrange("p (a n) -> p a n", a=2)
        yout = take(D)
        zero = take(P)
        gate = take(TILES * P)
        eidx = take(TILES * P).bitcast(U32)
        keysT = take(256).rearrange("p (a n) -> p a n", a=2)
        hS = ST.B[:, 0:D]
        big[0] = SZ
        uslot8 = [take(D) for _ in range(PB - WB)] + uslot
        vslot8 = [take(D) for _ in range(PB - WB)] + vslot
        diag8 = take(PB * P).rearrange("p (j n) -> p j n", j=PB)
        slot_sem = [4, 5, 6, 7, 0, 1, 2, 3]
        diag = diag0.rearrange("p (j n) -> p j n", j=WB)

        def htile(t):
            return hP[:, t, :] if t < 2 else hS

        room[0] = [small[:, :], 0]
        for q in (PR, ST):
            n = q.nt * SH
            q.dtr, q.dtv, q.dta, q.dtu, q.dtw, q.av = (tiny(n) for _ in range(6))
            q.acs = tiny(2 * n).rearrange("p (t n) -> p t n", t=q.nt)
            q.ex = tiny(3 * n).rearrange("p (t n) -> p t n", t=q.nt)
            if q is PR:
                room[0][1] = 0
        room[0][1] = 11 * 64
        negA = tiny(SH)
        dec = tiny(128).rearrange("p (c b) -> p c b", c=16)
        m8 = tiny(8)
        nmx, sums, rec = tiny(8), tiny(8), tiny(8)
        ms, rstd = tiny(8), tiny(8)
        norms = [(tiny(12), tiny(2), tiny(2)) for _ in range(2)]
        dots, gl, w8 = ([tiny(WB) for _ in range(2)] for _ in range(3))
        dots8, gl8, w88 = tiny(PB), tiny(PB), tiny(PB)
        islot = [tiny(WB, U32) for _ in range(4)]
        islot8 = [tiny(PB, U32) for _ in range(2)]

        psum = [ctx.enter_context(nc.psum_tensor(f"bank{i}", [P, 512], F32)) for i in range(8)]
        acc = psum[6:8]

        const_in, x_in, rows_in, par_in, wdt_in = (sem(s) for s in ("const_in", "x_in", "rows_in", "par_in", "wdt_in"))
        w_in_sem = [sem("wbuf0_loaded"), sem("wbuf1_loaded")]
        vb_filled, vb_drained = sem("v_bank_filled"), sem("v_bank_drained")
        sb_filled, sb_drained = sem("s_bank_filled"), sem("s_bank_drained")
        dve_step, pool_step = sem("dve_step"), sem("pool_step")
        conv_done, silu_done, tails_ready = sem("conv_done"), sem("silu_done"), sem("tails_ready")
        rope_done, cache_in = sem("rope_done"), sem("cache_in")
        tails_out, kv_out, bg_in, x2_in, ln1_in = ([sem(f"{s}{n}") for n in range(2)]
                                                   for s in ("tails_out", "kv_out", "bg_in", "x2_in", "ln1_in"))
        max_ready, exp_done, probs_ready = sem("max_ready"), sem("exp_done"), sem("probs_ready")
        dt_e, dt_v = sem("dt_steps_by_act"), sem("dt_steps_by_dve")
        a_ready, sum_ready, ex_ready = sem("a_ready"), sem("sums_ready"), sem("decays_ready")
        seg_ready, seg_exp, mt_ready = sem("seg_ready"), sem("seg_exp"), sem("mt_ready")
        old_in = [sem("old_state0_in"), sem("old_state1_in")]
        new_ready, new_out = sem("new_state_ready"), [sem("new_state0_out"), sem("new_state1_out")]
        pso_out = sem("prompt_state_out")
        y_done = sem("tile_y_done")
        gated, ms_ready, rms_root, yn_ready = sem("y_gated"), sem("ms_ready"), sem("rms_root"), sem("yn_ready")
        gate_pre, gate_ready, mixed_ready = sem("gate_pre"), sem("gate_ready"), sem("mixed_ready")
        ln2_in = sem("ln2_in")
        var1_ready, root1_ready, h_ready = sem("var1_ready"), sem("root1_ready"), sem("h_ready")
        keys_in, score_e, score_v = sem("keys_in"), sem("ts_shifted"), sem("ts_exp")
        idx_ready = sem("idx_ready")
        u_in = [sem(f"u_in{j}") for j in range(PB)]
        v_in = [sem(f"v_in{j}") for j in range(PB)]
        dot_done, gelu_done, w_ready, diag_ready, v_used = (sem(s) for s in ("dot_done", "gelu_done", "w_ready", "diag_ready", "v_used"))
        dot8_done, v8_used = sem("stream_dot_done"), sem("stream_v_used")
        acc_full, acc_read = sem("acc_full"), sem("acc_read")
        var2_ready, root2_ready, y_out_ready, y_out = (sem(s) for s in ("var2_ready", "root2_ready", "y_out_ready", "y_out"))

        before, nv, ns = {}, 0, 0
        for q in (PR, ST):
            n, s = q.nt, q.streams
            attn_v = n * (1 + 2 + KVH * 3)
            attn_s = 2 * n + 5 * s + 3 * KVH * n
            ssd_v = n + n * G * 4 + G * sum(t > 0 for t in q.tiles) + G * sum(t < 2 for t in q.tiles) + 32 * s
            ssd_s = 5 * n + (1 + 32 if s else 4)
            for name, v, w in [("start", 2 * n + 3 * (not s), 0), ("conv", 0, 24), ("dt", 0, n), ("qkv", 4 * n, 0),
                               ("tails", 0, 6), ("attention", attn_v, attn_s), ("ya", 2 * n, 0), ("ssd", ssd_v, ssd_s),
                               ("z", 0, 4 * n), ("yT", 0, 4 * n), ("ym", 4 * n, 0), ("gates", 4 * n, 0),
                               ("mixedT", 0, 2 * n), ("out", 2 * n, 0), ("hT", 0, 2 * n), ("wq", 0, 4 * n),
                               ("keysT", 0, int(not s)), ("scores", 4 * n, 4 * n), ("end", 0, 0)]:
                before[q.n, name] = (nv, ns)
                nv, ns = nv + v, ns + w

        block = ctx.enter_context(nc.Block())

        def store_kv(eng, q):
            eng.wait_ge(rope_done, q.n + 1)
            for t in q.tiles:
                for name, o, n in (("k", O_K, 256), ("v", O_V, 256), ("kidx", O_KI, 64)):
                    if t < 2:
                        dst = out["p_" + name][0, 0, t * P:(t + 1) * P]
                        dst = dst.rearrange("s v n -> s (v n)") if n == 256 else dst
                    else:
                        dst = out["s_" + name][0]
                        dst = dst.rearrange("b s v n -> (b s) (v n)") if n == 256 else dst.rearrange("b s n -> (b s) n")
                    eng.dma_start(dst, q.qkv[:, q.tiles.index(t), o:o + n]).then_inc(kv_out[q.n], 16)

        def load_x(eng, q, dst, done):
            if q.streams:
                eng.dma_start(dst[:, 0, :], a["x_sample"].rearrange("b s n -> (b s) n")).then_inc(done, 16)
            else:
                eng.dma_start(dst, a["x_prompt"][0].rearrange("(t p) n -> p t n", p=P)).then_inc(done, 16)

        def load_ln1(eng, q):
            for i, name in enumerate(("ln1_g", "ln1_b")):
                eng.dma_start(q.ln1[:, i, :], a[name][0].partition_broadcast(P)).then_inc(ln1_in[q.n], 16)

        @block.sync
        def _(sp):
            sp.dma_start(cst[:, :], a["table"]).then_inc(const_in, 16)
            load_x(sp, PR, PR.x1, x_in)

            def wtile(w, at, n):
                cols = w[:, at:at + n] if isinstance(at, int) else w[:, ds(at, n)]
                return cols.rearrange("(k p) n -> p k n", p=P)

            w_in = a["w_in"][0]
            free = [None, None]

            def weights(q, name, ring, times, source, width=512, jobs=None):
                first, jobs = before[q.n, name][0 if ring is vb_filled else 1], jobs or q.nt

                def load(turn, b):
                    sp.dma_start(wbuf[b][:, :, 0:width], source(turn, b)).then_inc(w_in_sem[b], 16)

                for b in range(2):
                    if free[b] is not None:
                        sp.wait_ge(*free[b])
                    load(0, b)
                yield
                if times > 1:
                    with sp.Fori(1, times) as i:
                        for b in range(2):
                            sp.wait_ge(ring, i * (2 * jobs) + (first + jobs * (b - 1)))
                            load(i, b)
                for b in range(2):
                    free[b] = (ring, first + 2 * jobs * (times - 1) + jobs * (b + 1))
                yield

            def whole(*args, **kw):
                for _ in weights(*args, **kw):
                    pass

            for q in (PR, ST):
                if q.streams:
                    sp.wait_ge(vb_filled, before[1, "start"][0])
                    load_x(sp, q, q.x1, x_in)
                whole(q, "conv", sb_filled, 4, lambda i, b: wtile(w_in, i * 768 + (O_XBC + 384 * b), 384), 384, 3)
                if q.streams:
                    for v in range(KVH):
                        sp.dma_start(q.kc[:, v, :].rearrange("p (b n) -> p b n", b=DEC_B),
                                     a["cache_k"][0][:, :, v, :].rearrange("b s n -> s b n")).then_inc(cache_in, 16)
                    sp.dma_start(q.kc[:, 4, :].rearrange("p (b n) -> p b n", b=DEC_B),
                                 a["cache_kidx"][0].rearrange("b s n -> s b n")).then_inc(cache_in, 16)
                    sp.dma_start(q.vc, a["cache_v"][0].rearrange("b s v n -> s b (v n)")).then_inc(cache_in, 16)
                whole(q, "qkv", vb_filled, 2, lambda i, b: wtile(w_in, i * 1024 + 512 * b, 512))
                whole(q, "ya", vb_filled, 1, lambda i, b: wtile(a["w_attn_br"][0], 512 * b, 512))
                if q.streams:
                    sp.wait_ge(sb_drained, SR + before[1, "attention"][1])
                    sp.dma_start(out["s_conv"][0].rearrange("b j n -> (b j) n"), q.tails[0:24, :]).then_inc(tails_out[1], 16)
                    store_kv(sp, q)
                z = weights(q, "z", sb_filled, 2, lambda i, b: wtile(w_in, i * 1024 + (O_Z + 512 * b), 512))
                next(z)
                if q.streams:
                    old = a["state_ssm"][0].rearrange("b (c h) q n -> c (h q) b n", h=2)
                    new = out["s_ssm"][0].rearrange("b (c h) q n -> c (h q) b n", h=2)
                    for c in range(18):
                        if c >= 2:
                            sp.wait_ge(new_ready, 2 * (c - 1))
                            sp.dma_start(new[c - 2], q.sst[c % 2]).then_inc(new_out[c % 2], 16)
                        if 2 <= c < 16:
                            sp.wait_ge(new_out[c % 2], 16 * (c // 2))
                        if c < 16:
                            sp.dma_start(q.sst[c % 2], old[c]).then_inc(old_in[c % 2], 16)
                    for b in range(2):
                        sp.wait_ge(new_out[b], 16 * 8)
                    sp.wait_ge(y_done, 3)
                    sp.dma_start(q.bg, a["b_gate"][0].partition_broadcast(P)).then_inc(bg_in[1], 16)
                    load_ln1(sp, q)
                for _ in z:
                    pass
                ym = weights(q, "ym", vb_filled, 2, lambda i, b: wtile(a["w_ssm_br"][0][D * b:D * (b + 1)], i * 512, 512))
                next(ym)
                if q.streams:
                    sp.wait_ge(sb_filled, before[1, "ym"][1])
                    load_x(sp, q, q.x2, x2_in[1])
                for _ in ym:
                    pass
                whole(q, "gates", vb_filled, 2, lambda i, b: wtile(w_in, i * 512 + (O_GATE + 1024 * b), 512))
                whole(q, "out", vb_filled, 1, lambda i, b: wtile(a["w_out"][0], 512 * b, 512))
                whole(q, "wq", sb_filled, 2, lambda i, b: wtile(a["peer_wq"][0], i * 1024 + 512 * b, 512))
            sp.wait_ge(y_out_ready, 3)
            sp.dma_start(out["y_sample"].rearrange("b s n -> (b s) n"), yout).then_inc(y_out, 16)
            sp.wait_ge(y_out, 16 * TILES)
            for n in range(2):
                sp.wait_ge(kv_out[n], 16 * (6, 3)[n])
                sp.wait_ge(tails_out[n], 16)

        @block.gpsimd
        def _(pool):
            own = Own(pool, pool_step)
            pool.dma_start(rowsin[0:24, :], a["state_conv"][0].rearrange("b j n -> (b j) n")).then_inc(rows_in, 16)
            pool.dma_start(rowsin[24:28, :], a["conv_w"][0]).then_inc(rows_in, 16)
            pool.dma_start(rowsin[28:29, :], a["conv_b"]).then_inc(rows_in, 16)
            pool.dma_start(normin[0:16, :], a["ssm_norm_w"][0].rearrange("(c p) -> c p", p=P)).then_inc(rows_in, 16)
            for i, name in enumerate(("dt_bias", "a_log", "d_skip")):
                pool.dma_start(headp[:, i * SH:(i + 1) * SH], a[name][0].partition_broadcast(P)).then_inc(par_in, 16)
            pool.dma_start(wdt, a["w_in"][0][:, O_DT:O_DT + SH].rearrange("(k p) n -> p k n", p=P)).then_inc(wdt_in, 16)
            pool.wait_ge(sb_drained, SR + before[0, "attention"][1])
            pool.dma_start(out["p_conv"][0, 0], PR.tails[0:3, :]).then_inc(tails_out[0], 16)
            store_kv(pool, PR)
            pool.wait_ge(sb_drained, SR + before[0, "z"][1])
            pool.dma_start(out["p_ssm"][0, 0].rearrange("(c h) q n -> (h q) c n", h=2),
                           PR.pso.rearrange("p (c n) -> p c n", c=16)).then_inc(pso_out, 16)
            pool.wait_ge(pso_out, 16)
            pool.wait_ge(y_done, 2)
            pool.dma_start(PR.bg, a["b_gate"][0].partition_broadcast(P)).then_inc(bg_in[0], 16)
            load_ln1(pool, PR)
            for i, name in enumerate(("ln2_g", "ln2_b")):
                pool.dma_start(ln2[:, i, :], a[name][0].partition_broadcast(P)).then_inc(ln2_in, 16)
            pool.dma_start(PR.keys[:, 0, :], a["peer_keys1"][0]).then_inc(keys_in, 16)
            pool.dma_start(PR.keys[:, 1, :], a["peer_keys2"][0]).then_inc(keys_in, 16)
            pool.wait_ge(sb_filled, before[0, "ym"][1])
            load_x(pool, PR, PR.x2, x2_in[0])

            table_u, table_v = a["peer_u"][0], a["peer_v"][0]
            want_u, want_v = pool.alloc_register("want_dots"), pool.alloc_register("want_used")
            pool.reg_mov(want_u, 1)
            pool.reg_mov(want_v, 1)
            pool.sem_inc(dot_done, WB)
            pool.sem_inc(v_used, WB)

            def gather_u(slot, j, idx, done=dot_done):
                pool.wait_ge(done, want_u)
                pool.reg_add(want_u, want_u, 1)
                pool.indirect_dma_start(slot, None, table_u, bass.IndirectOffsetOnAxis(ap=idx, axis=0)).then_inc(u_in[j], 16)

            def gather_v(slot, j, idx, used=v_used):
                pool.wait_ge(used, want_v)
                pool.reg_add(want_v, want_v, 1)
                pool.indirect_dma_start(slot, None, table_v, bass.IndirectOffsetOnAxis(ap=idx, axis=0)).then_inc(v_in[j], 16)

            def rows(b, at, with_v):
                own(pool.tensor_copy(islot[b], eidx[:, at:at + WB] if isinstance(at, int) else eidx[:, ds(at, WB)]))
                own.settle()
                for j in range(WB):
                    gather_u(uslot[j], j, islot[b][:, j:j + 1])
                if with_v:
                    for j in range(WB):
                        gather_v(vslot[j], j, islot[b - 1][:, j:j + 1])

            pool.wait_ge(idx_ready, 1)
            for b in range(4):
                rows(b, b * WB, b > 0)
            for t, first, times in ((0, 4, BLOCKS // 4 - 1), (1, BLOCKS, BLOCKS // 4)):
                pool.wait_ge(idx_ready, t + 1)
                with loop(pool, times, (own.step, 4)) as i:
                    for b in range(4):
                        rows(b, i * (4 * WB) + (first + b) * WB, True)
            for j in range(WB):
                gather_v(vslot[j], j, islot[3][:, j:j + 1])
            pool.wait_ge(idx_ready, 3)
            pool.wait_ge(dot_done, WB * (PROMPT_BLOCKS + 1))
            pool.wait_ge(v_used, WB * (PROMPT_BLOCKS + 1))
            pool.sem_inc(dot8_done, 2 * P + PB)
            pool.sem_inc(v8_used, 2 * P + PB)
            with loop(pool, P // PB // 2, (own.step, 2)) as i:
                for b in range(2):
                    own(pool.tensor_copy(islot8[b], eidx[:, ds(i * (2 * PB) + (2 * P + b * PB), PB)]))
                    own.settle()
                    for j in range(PB):
                        gather_u(uslot8[j], slot_sem[j], islot8[b][:, j:j + 1], dot8_done)
                    for j in range(PB):
                        gather_v(vslot8[j], slot_sem[j], islot8[b][:, j:j + 1], v8_used)

        @block.tensor
        def _(pe):
            vf, vd = Count(vb_filled), Count(vb_drained)
            sf, sd = Count(sb_filled), Count(sb_drained)
            loaded = [Count(s, step=16) for s in w_in_sem]
            ticks = [0]
            mm = nc.tensor.matmul

            def expert_rows(dg, used, j, slots, landed):
                landed.take(pe) if isinstance(landed, Count) else pe.wait_ge(*landed)
                mm(acc[0][:, :], dg[:, j, :], slots[j][:, 0:512], start=False, stop=False, skip_group_check=True)
                mm(acc[1][:, :], dg[:, j, :], slots[j][:, 512:1024], start=False, stop=False,
                   skip_group_check=True).then_inc(used, 1)

            def open_sums(t):
                if t:
                    pe.wait_ge(acc_read, t)
                pe.wait_ge(ln2_in, 32)
                for n in range(2):
                    mm(acc[n][:, :], zero, ln2[:, 0, 0:512], start=True, stop=False, skip_group_check=True)

            def close_sums():
                for n in range(2):
                    last = mm(acc[n][:, :], zero, ln2[:, 0, 0:512], start=False, stop=True, skip_group_check=True)
                last.then_inc(acc_full, 1)

            def tick():
                k = ticks[0]
                ticks[0] += 1
                if k in (1, BLOCKS + 1):
                    open_sums(k // BLOCKS)
                if 1 <= k <= PROMPT_BLOCKS:
                    pe.wait_ge(diag_ready, k)
                    for j in range(WB):
                        expert_rows(diag, v_used, j, vslot, (v_in[j], 16 * k))
                if k in (BLOCKS, PROMPT_BLOCKS):
                    close_sums()

            def vbank():
                vd.take(pe)
                return psum[vf.n % VR]

            def sbank():
                sd.take(pe)
                return psum[VR + sf.n % SR]

            def v_written():
                pe.wait_ge(vb_drained, VR + vf.n)

            def s_written():
                pe.wait_ge(sb_drained, SR + sf.n)

            def turn(dst, src, ids):
                return nc.tensor.transpose(dst, src, ids)

            def mixer(q):
                toks = {t: q.at(t) for t in q.tiles}
                L = {t: q.tiles.index(t) for t in q.tiles}
                step = tick if q.streams else (lambda: None)

                def phase(name):
                    assert (vf.n, sf.n) == before[q.n, name], (name, vf.n, sf.n, before[q.n, name])

                def products(times, lhs, ring, drained, bank):
                    for _ in turns(pe, q.streams or times == 1, times, (ring, 2 * q.nt), (drained, 2 * q.nt),
                                   (loaded[0], 1), (loaded[1], 1)):
                        for b in range(2):
                            loaded[b].take(pe)
                            for t in q.tiles:
                                dst = bank()
                                for k in range(KC):
                                    last = mm(dst[:, :], lhs(b, k, toks[t]), wbuf[b][:, k, :],
                                              start=(k == 0), stop=(k == KC - 1))
                                ring.give(last)
                        step()

                def rows_to_T(src, t, quarter):
                    dst = sbank()
                    for i in range(4):
                        last = turn(dst[:, i * P:(i + 1) * P], src[:, (4 * quarter + i) * P:(4 * quarter + i + 1) * P], ident)
                    sf.give(last)

                phase("start")
                pe.wait_ge(const_in, 16)
                pe.wait_ge(x_in, 16 * (q.n + 1))
                for t in q.tiles:
                    for half in range(2):
                        dst = vbank()
                        for i in range(4):
                            last = turn(dst[:, i * P:(i + 1) * P], q.x1[:, L[t], (4 * half + i) * P:(4 * half + i + 1) * P], ident)
                        vf.give(last)
                if not q.streams:
                    pe.wait_ge(rows_in, 64)
                    for half in range(2):
                        dst = vbank()
                        for i in range(12):
                            last = turn(dst[:, i * ROWS:(i + 1) * ROWS],
                                        rowsin[0:ROWS, (12 * half + i) * P:(12 * half + i + 1) * P], ident[0:ROWS, 0:ROWS])
                        vf.give(last)
                    dst = vbank()
                    vf.give(turn(dst[:, 0:16], normin[0:16, :], ident[0:16, 0:16]))
                v_written()
                step()

                phase("conv")
                for _ in turns(pe, q.streams, 4, (sf, 6), (sd, 6), (loaded[0], 1), (loaded[1], 1)):
                    for b in range(2):
                        loaded[b].take(pe)
                        for j in range(3):
                            dst = sbank()
                            for k in range(KC):
                                last = mm(dst[:, 0:q.tok], wbuf[b][:, k, j * P:(j + 1) * P], q.xT[:, k, :],
                                          start=(k == 0), stop=(k == KC - 1))
                            sf.give(last)
                        step()

                phase("dt")
                pe.wait_ge(wdt_in, 16)
                for t in q.tiles:
                    dst = sbank()
                    for k in range(KC):
                        last = mm(dst[:, 0:SH], q.xT[:, k, toks[t]], wdt[:, k, :], start=(k == 0), stop=(k == KC - 1))
                    sf.give(last)

                def x_part(b, k, tok):
                    return q.xT[:, k, tok]

                phase("qkv")
                products(2, x_part, vf, vd, vbank)

                phase("tails")
                pe.wait_ge(tails_ready, q.n + 1)
                for c in range(6):
                    dst = sbank()
                    for i in range(4):
                        last = turn(dst[0:q.nrow, i * P:(i + 1) * P], q.tail[:, 4 * c + i, :], ident)
                    sf.give(last)
                step()

                phase("attention")
                pe.wait_ge(rope_done, q.n + 1)
                for t in q.tiles:
                    dst = sbank()
                    for v in range(KVH):
                        last = mm(dst[0:64, v * P:(v + 1) * P], q.qkv[:, L[t], O_K + v * HD:O_K + (v + 1) * HD], ident,
                                  start=True, stop=True)
                    sf.give(last)
                    dst = sbank()
                    sf.give(mm(dst[0:64, 0:P], q.qkv[:, L[t], O_KI:O_KI + HD], ident, start=True, stop=True))
                if q.streams:
                    pe.wait_ge(cache_in, 16 * 6)
                    for v in range(5):
                        dst = sbank()
                        for j in range(4):
                            last = turn(dst[:, j * P:(j + 1) * P], q.kc[:, v, j * P:(j + 1) * P], ident)
                        sf.give(last)
                s_written()
                step()

                def turn_q(t, o):
                    dst = vbank()
                    for r in range(REP):
                        for half in range(2 if t == 2 else 1):
                            last = mm(dst[64 * half:64 * half + 64, r * P:(r + 1) * P],
                                      q.qkv[:, L[t], o + r * HD:o + (r + 1) * HD], ident, start=True, stop=True)
                    vf.give(last)
                    v_written()

                def dot_keys(t, v):
                    for pr in range(2):
                        dst = vbank()
                        for r in (2 * pr, 2 * pr + 1):
                            o = (r % 2) * 256
                            if t < 2:
                                last = mm(dst[:, o:o + P * (t + 1)], q.qn[0:64, r, :], q.kT[0:64, v, 0:P * (t + 1)],
                                          start=True, stop=True)
                            else:
                                for j in range(4):
                                    mm(dst[:, o:o + P], q.qm[:, r, j, :], q.kcT[:, v, j, :], start=(j == 0), stop=(j == 3))
                                last = mm(dst[:, o + P:o + 2 * P], q.qn[0:64, r, :], q.kT[0:64, v, :],
                                          start=True, stop=True)
                        vf.give(last)

                def attend(t, v):
                    n = t * KVH + v
                    pe.wait_ge(probs_ready, n + 1)
                    lm = q.lm[n % 2]
                    for half in range(2):
                        dst = sbank()
                        for r in range(REP):
                            if half == 0 or t > 0:
                                last = turn(dst[:, r * P:(r + 1) * P], lm[:, r, half * P:(half + 1) * P], ident)
                            elif r == 0:
                                last = turn(dst[:, 0:P], lm[:, 0, 0:P], ident)
                        sf.give(last)
                    s_written()
                    dst = sbank()
                    for par in range(2):
                        o = dst[64 * par:64 * par + 64, 0:256]
                        vs = slice(O_V + v * HD, O_V + (v + 1) * HD)
                        if t < 2:
                            for half in range(t + 1):
                                last = mm(o, q.qkv[:, half, vs], q.PT[:, half, par::2, :],
                                          start=(half == 0), stop=(half == t))
                        else:
                            mm(o, q.qkv[:, 0, vs], q.PT[:, 1, par::2, :], start=True, stop=False, skip_group_check=True)
                            for b in range(DEC_B):
                                ob = o.rearrange("p (r t) -> p r t", r=2)[:, :, b * DEC_S:(b + 1) * DEC_S]
                                last = mm(ob, q.vc[:, b, v * HD:(v + 1) * HD], q.PT[:, 0, par::2, b * DEC_S:(b + 1) * DEC_S],
                                          start=False, stop=(b == DEC_B - 1), skip_group_check=True)
                    sf.give(last)

                done = None
                for t in q.tiles:
                    turn_q(t, O_QI)
                    dot_keys(t, 4)
                    step()
                    for v in range(KVH):
                        turn_q(t, v * REP * HD)
                        dot_keys(t, v)
                        step()
                        if done is not None:
                            attend(*done)
                            step()
                        done = (t, v)
                attend(*done)
                s_written()

                phase("ya")
                products(1, lambda b, k, tok: q.attnT[:, k, tok], vf, vd, vbank)

                phase("ssd")
                pe.wait_ge(a_ready, q.n + 1)
                pe.wait_ge(silu_done, q.n + 1)
                for t in q.tiles:
                    dst = vbank()
                    at = L[t] * SH
                    mm(dst[:, 0:SH], tri[:, t // 2, :], q.av[:, at:at + SH], start=True, stop=True)
                    vf.give(mm(dst[:, SH:2 * SH], same[:, t // 2, :], q.av[:, at:at + SH], start=True, stop=True))
                for t in q.tiles:
                    tok = toks[t]
                    for c in range(5):
                        dst = sbank()
                        for i in range(4):
                            last = turn(dst[:, i * P:(i + 1) * P], q.xc[:, 4 * c + i, tok], ident)
                        sf.give(last)
                    if t == 2:
                        dst = sbank()
                        for hh in range(SH):
                            last = mm(dst[64 * (hh % 2):64 * (hh % 2) + 64, (hh // 2) * 8:(hh // 2) * 8 + 8],
                                      q.av[:, hh:hh + 1].to_broadcast([P, 64]), blk, start=True, stop=True)
                        sf.give(last)
                    s_written()
                    step()
                    for g in range(G):
                        BT, CT = q.xc[:, 16 + g, tok], q.xc[:, 20 + g, tok]
                        dst = vbank()
                        vf.give(mm(dst[:, 0:P], BT, CT, start=True, stop=True))
                        for half in range(2):
                            dst = vbank()
                            for i in range(4):
                                hh = L[t] * SH + g * 8 + half * 4 + i
                                last = mm(dst[:, i * P:(i + 1) * P], q.av[:, hh:hh + 1].to_broadcast([P, P]),
                                          tri[:, t // 2, :], start=True, stop=True)
                            vf.give(last)
                        pe.wait_ge(seg_ready, t * G + g + 1)
                        Bg = q.xbt[:, DI + g * P:DI + (g + 1) * P]
                        step()
                        if t == 2:
                            for c in range(4 * g, 4 * g + 4):
                                pe.wait_ge(old_in[c % 2], 16 * (c // 2 + 1))
                                for half in range(2):
                                    dst = sbank()
                                    for i in range(4):
                                        last = turn(dst[:, i * P:(i + 1) * P], q.sst[c % 2][:, 4 * half + i, :], ident)
                                    sf.give(last)
                                for half in range(2):
                                    dst = vbank()
                                    vf.give(mm(dst[:, :], q.xdtd[:, c * P:(c + 1) * P], q.Bm[:, 4 * half:4 * half + 4, :],
                                               start=True, stop=True))
                                if c % 4 == 1:
                                    step()
                            s_written()
                            step()
                        if t > 0:
                            dst = vbank()
                            if t == 1:
                                vf.give(mm(dst[:, :], CT, q.stateT[:, g * 512:(g + 1) * 512], start=True, stop=True))
                            else:
                                for b in range(DEC_B):
                                    last = mm(dst[:, :], q.CTm[:, b, :], q.pT[:, b, :], start=(b == 0), stop=(b == DEC_B - 1))
                                vf.give(last)
                        pe.wait_ge(mt_ready, t * G + g + 1)
                        dst = vbank()
                        for r in range(8):
                            last = mm(dst[:, r * HD:(r + 1) * HD], q.MT[:, r, :],
                                      q.xdt[:, g * 512 + r * HD:g * 512 + (r + 1) * HD], start=True, stop=True)
                        vf.give(last)
                        if t < 2:
                            dst = vbank()
                            vf.give(mm(dst[:, :], Bg, q.xdtd[:, g * 512:(g + 1) * 512], start=True, stop=True))
                    if t == 1:
                        v_written()
                        for quarter in range(4):
                            rows_to_T(q.stateT, t, quarter)

                phase("z")
                products(2, x_part, sf, sd, sbank)
                phase("yT")
                for t in q.tiles:
                    pe.wait_ge(yn_ready, t + 1)
                    for quarter in range(4):
                        rows_to_T(q.y[:, L[t], :], t, quarter)
                s_written()
                step()
                phase("ym")
                products(2, lambda b, k, tok: q.yTv[:, 8 * b + k, tok], vf, vd, vbank)
                phase("gates")
                products(2, x_part, vf, vd, vbank)
                phase("mixedT")
                pe.wait_ge(mixed_ready, 2 * q.nt + 4 * q.n)
                for t in q.tiles:
                    for half in range(2):
                        rows_to_T(q.ya[:, L[t], :], t, half)
                s_written()
                phase("out")
                products(1, x_part, vf, vd, vbank)
                phase("hT")
                for t in q.tiles:
                    pe.wait_ge(h_ready, t + 1)
                    for half in range(2):
                        rows_to_T(htile(t), t, half)
                s_written()
                step()
                phase("wq")
                products(2, x_part, sf, sd, sbank)
                phase("keysT")
                if not q.streams:
                    pe.wait_ge(keys_in, 32)
                    dst = sbank()
                    for i in range(2):
                        last = turn(dst[:, i * P:(i + 1) * P], q.keys[:, i, :], ident)
                    sf.give(last)
                phase("scores")
                s_written()
                for t in q.tiles:
                    for quarter in range(4):
                        rows_to_T(q.qp[:, L[t], :], t, quarter)
                    s_written()
                    for quarter in range(4):
                        dst = vbank()
                        for i in range(4):
                            last = mm(dst[:, i * P:(i + 1) * P], q.qT[:, 4 * quarter + i, :], keysT[:, i % 2, :],
                                      start=True, stop=True)
                        vf.give(last)
                    step()
                phase("end")

            mixer(PR)
            pe.wait_ge(idx_ready, 1)
            for _ in range(PAUSES):
                tick()
            mixer(ST)
            while ticks[0] < TICKS:
                tick()
            dg = Count(diag_ready, start=PROMPT_BLOCKS)
            landed = [Count(v_in[s], start=PROMPT_BLOCKS if s < WB else 0, step=16) for s in slot_sem]
            open_sums(2)
            with loop(pe, P // PB, (dg, 1), *((c, 1) for c in landed)):
                dg.take(pe)
                for j in range(PB):
                    expert_rows(diag8, v8_used, j, vslot8, landed[j])
            close_sums()

        @block.scalar
        def _(act):
            sf, sd = Count(sb_filled), Count(sb_drained, start=SR)
            act.sem_inc(sb_drained, SR)
            ticks = [0]

            def bank():
                k = sf.n % SR
                sf.take(act)
                return psum[VR + k]

            def f(o, i, func=ACT.Copy, **kw):
                return nc.scalar.activation(o, i, func, **kw)

            def root(t, which, ready, done):
                mv, rs = norms[which][1:]
                act.wait_ge(ready, t + 1)
                f(rs[:, 0:1], mv[:, 1:2], ACT.Sqrt, bias=eps).then_inc(done, 1)

            def tick():
                k = ticks[0]
                ticks[0] += 1
                if k in (BLOCKS + 1, PROMPT_BLOCKS + 1):
                    root(k // BLOCKS - 1, 1, var2_ready, root2_ready)
                if k in (BLOCKS + 2, PROMPT_BLOCKS + 2):
                    store_y(k // BLOCKS - 1)
                if 1 <= k <= PROMPT_BLOCKS:
                    act.wait_ge(w_ready, k)
                    act.wait_ge(v_used, WB * k)
                    for j in range(WB):
                        last = f(diag[:, j, :], ident, scale=w8[(k - 1) % 2][:, j:j + 1])
                    last.then_inc(diag_ready, 1)
                if k < PROMPT_BLOCKS:
                    act.wait_ge(dot_done, WB * (k + 2))
                    f(gl[k % 2], dots[k % 2], ACT.Gelu).then_inc(gelu_done, 1)

            def store_y(t):
                act.wait_ge(y_out_ready, t + 1)
                act.dma_start(out["y_prompt"][0][t * P:(t + 1) * P], yout).then_inc(y_out, 16)

            def exp_scores(t):
                act.wait_ge(score_e, t + 1)
                f(ts16, ts16, ACT.Exp).then_inc(score_v, 1)

            def mixer(q):
                step = tick if q.streams else (lambda: None)
                L = {t: q.tiles.index(t) for t in q.tiles}
                step()
                for i in turns(act, q.streams, 4, (sf, 6), (sd, 6)):
                    for j in range(6):
                        src = bank()
                        o = i * (6 * q.raw) + j * q.raw
                        row = q.xraw2[:, o:o + q.raw] if q.streams else q.xraw2[:, ds(o, q.raw)]
                        if q.streams:
                            sd.give(f(row.rearrange("p (b s) -> p b s", b=DEC_B)[:, :, 3:SEG],
                                      src[:, 0:P].rearrange("p (b s) -> p b s", b=DEC_B)))
                        else:
                            sd.give(f(row[:, 3:3 + SEQ], src[:, 0:SEQ]))
                        if j % 3 == 2:
                            step()
                for t in q.tiles:
                    src = bank()
                    sd.give(f(q.dtr[:, L[t] * SH:(L[t] + 1) * SH], src[:, 0:SH]))
                act.wait_ge(dt_v, 2 * q.n + 1)
                if not q.streams:
                    f(negA, headp[:, SH:2 * SH], ACT.Exp)
                f(q.dtu, q.dta, ACT.Exp, scale=-1.0).then_inc(dt_e, 1)
                act.wait_ge(dt_v, 2 * q.n + 2)
                f(q.dtw, q.dtw, ACT.Ln).then_inc(dt_e, 1)
                step()
                step()
                act.wait_ge(conv_done, CC * (q.n + 1))
                for c in range(6):
                    last = f(q.xc[:, 4 * c:4 * c + 4, :], q.xc[:, 4 * c:4 * c + 4, :], ACT.Silu)
                last.then_inc(silu_done, 1)
                for c in range(6):
                    src = bank()
                    sd.give(f(q.tails[0:q.nrow, c * 512:(c + 1) * 512], src[0:q.nrow, :]))
                step()

                for t in q.tiles:
                    src = bank()
                    tok = q.at(t)
                    sd.give(f(q.kT[0:64, 0:4, tok], src[0:64, :].rearrange("p (v s) -> p v s", v=4)))
                    src = bank()
                    sd.give(f(q.kT[0:64, 4, tok], src[0:64, 0:P]))
                if q.streams:
                    for v in range(5):
                        src = bank()
                        sd.give(f(q.kcT[:, v, :, :], src[:, :].rearrange("p (j s) -> p j s", j=4)))
                step()

                def exps(n):
                    act.wait_ge(max_ready, n + 1)
                    S = P if n < KVH else 2 * P
                    for r in range(REP):
                        o = 4 * (n % 2) + r
                        v = q.lm[n % 2][:, r, 0:S]
                        last = f(v, v, ACT.Exp, scale=LOG_SCALE, bias=nmx[:, o:o + 1], accum_out=sums[:, o:o + 1])
                    last.then_inc(exp_done, 1)

                def keep(n):
                    t, v = n // KVH, n % KVH
                    for half in range(2):
                        src = bank()
                        if half == 0 or t > 0:
                            sd.give(f(q.PT[:, half, :, :], src[:, :].rearrange("p (r s) -> p r s", r=REP)))
                        else:
                            sd.give(f(q.PT[:, 1, 0, :], src[:, 0:P]))
                    if v == 0 and t != 1:
                        act.wait_ge(tails_out[q.n], 16)
                    src = bank()
                    sd.give(f(q.attnT[:, 2 * v:2 * v + 2, q.at(t)], src[:, 0:256].rearrange("p (r s) -> p r s", r=2)))

                done = None
                for t in q.tiles:
                    step()
                    for v in range(KVH):
                        exps(t * KVH + v)
                        step()
                        if done is not None:
                            keep(done)
                            step()
                        done = t * KVH + v
                keep(done)
                step()

                act.wait_ge(sum_ready, q.n + 1)
                f(q.ex[:, :, 0:2 * SH], q.acs, ACT.Exp)
                f(q.ex[:, :, 2 * SH:3 * SH], q.ex[:, :, 2 * SH:3 * SH], ACT.Exp).then_inc(ex_ready, 1)
                for t in q.tiles:
                    if t == 1:
                        act.wait_ge(y_done, t)
                    else:
                        act.wait_ge(vb_filled, before[q.n, "ssd"][0])
                    for c in range(5):
                        src = bank()
                        sd.give(f(q.xbt[:, c * 512:(c + 1) * 512], src[:, :]))
                    if t == 2:
                        src = bank()
                        sd.give(f(dec.rearrange("p c b -> p (c b)"), src[:, 0:P], ACT.Exp))
                    step()
                    for g in range(G):
                        act.wait_ge(seg_ready, t * G + g + 1)
                        f(q.MT, q.MT, ACT.Exp).then_inc(seg_exp, 1)
                        step()
                        if t == 2:
                            for c in range(4):
                                for half in range(2):
                                    src = bank()
                                    sd.give(f(q.pT[:, 4 * half:4 * half + 4, c * P:(c + 1) * P],
                                              src[:, :].rearrange("p (b s) -> p b s", b=4)))
                                if c == 1:
                                    step()
                            step()
                    if t == 1:
                        for quarter in range(4):
                            src = bank()
                            sd.give(f(q.pso[:, quarter * 512:(quarter + 1) * 512], src[:, :]))

                act.wait_ge(y_done, q.tiles[-1] + 1)
                g0 = q.n * (1 + 4 * PR.nt)
                for i in turns(act, q.streams, 2, (sf, 2 * q.nt), (sd, 2 * q.nt)):
                    act.wait_ge(gated, i * (2 * q.nt) + (g0 + 1))
                    for j in range(2 * q.nt):
                        src = bank()
                        sd.give(f(q.zs[:, j, :], src[:, :], ACT.Silu))
                    step()
                act.wait_ge(ms_ready, q.n + 1)
                f(rstd, ms, ACT.Sqrt, scale=1.0 / 512, bias=eps).then_inc(rms_root, 1)
                for t in q.tiles:
                    for quarter in range(4):
                        src = bank()
                        for i in range(4):
                            c = 4 * quarter + i
                            last = f(q.yTv[:, c, q.at(t)], src[:, i * P:(i + 1) * P], scale=normT[:, c:c + 1])
                        sd.give(last)
                step()
                step()
                step()
                pre = Count(gate_pre, start=q.n * 4 * PR.nt)
                for i in turns(act, q.streams, 2, (pre, 2 * q.nt)):
                    for j in range(2 * q.nt):
                        pre.take(act)
                        f(q.gt[:, j, :], q.gt[:, j, :], ACT.Sigmoid).then_inc(gate_ready, 1)
                    step()

                def keep_T(t, half):
                    src = bank()
                    sd.give(f(q.xT[:, 4 * half:4 * half + 4, q.at(t)], src[:, :].rearrange("p (k s) -> p k s", k=4)))

                for t in q.tiles:
                    for half in range(2):
                        keep_T(t, half)
                step()
                for t in q.tiles:
                    root(t, 0, var1_ready, root1_ready)
                for t in q.tiles:
                    for half in range(2):
                        keep_T(t, half)
                step()
                act.wait_ge(h_ready, q.tiles[-1] + 1)
                for i in turns(act, q.streams, 2, (sf, 2 * q.nt), (sd, 2 * q.nt)):
                    for b in range(2):
                        for k in range(q.nt):
                            src = bank()
                            o = i * 1024 + (k * 2048 + b * 512)
                            sd.give(f(q.YD[:, o:o + 512] if q.streams else q.YD[:, ds(o, 512)], src[:, :]))
                    step()
                if not q.streams:
                    src = bank()
                    sd.give(f(keysT, src[:, 0:256].rearrange("p (a n) -> p a n", a=2)))
                for t in q.tiles:
                    for quarter in range(4):
                        src = bank()
                        sd.give(f(q.qT[:, 4 * quarter:4 * quarter + 4, :], src[:, :].rearrange("p (c s) -> p c s", c=4)))
                    step()

            mixer(PR)
            exp_scores(0)
            for _ in range(PAUSES):
                tick()
            exp_scores(1)
            mixer(ST)
            for _ in range(PAUSES):
                if ticks[0] < TICKS:
                    tick()
            exp_scores(2)
            while ticks[0] < TICKS:
                tick()
            store_y(1)
            dots_c, w_c, vu = Count(dot8_done, start=2 * P + PB), Count(w_ready, start=PROMPT_BLOCKS), Count(v8_used, start=2 * P)
            with loop(act, P // PB, (dots_c, PB), (w_c, 1), (vu, PB)):
                dots_c.n += PB - 1
                dots_c.take(act)
                f(gl8, dots8, ACT.Gelu).then_inc(gelu_done, 1)
                w_c.take(act)
                vu.n += PB - 1
                vu.take(act)
                for j in range(PB):
                    last = f(diag8[:, j, :], ident, scale=w88[:, j:j + 1])
                last.then_inc(diag_ready, 1)
            root(2, 1, var2_ready, root2_ready)

        @block.vector
        def _(dve):
            own = Own(dve, dve_step)
            vf, vd = Count(vb_filled), Count(vb_drained, start=VR)
            dve.sem_inc(vb_drained, VR)
            ticks = [0]
            tt, tsc, stt = nc.vector.tensor_tensor, nc.vector.tensor_scalar, nc.vector.scalar_tensor_tensor
            cp = nc.vector.tensor_copy

            def bank():
                k = vf.n % VR
                vf.take(dve)
                return psum[k]

            def bc(ap, shape):
                return ap.to_broadcast([P] + list(shape))

            def layer_norm(v, o, t, which, g, b, ready, done, final):
                bns, mv, rs = norms[which]
                for half in range(2):
                    own(nc.vector.bn_stats(bns[:, 6 * half:6 * half + 6], v[:, half * 512:(half + 1) * 512]))
                own.settle()
                own(nc.vector.bn_aggr(mv, bns))
                own.settle()
                dve.sem_inc(ready, 1)
                dve.wait_ge(done, t + 1)
                own(nc.vector.reciprocal(rs[:, 1:2], rs[:, 0:1]))
                own.settle()
                own(tsc(v, v, mv[:, 0:1], rs[:, 1:2], ALU.subtract, ALU.mult))
                own.settle()
                own(tt(v, v, g, ALU.mult))
                own.settle()
                tt(o, v, b, ALU.add).then_inc(final, 1)

            def finish(t):
                dve.wait_ge(acc_full, t + 1)
                hv = htile(t)
                for n in range(2):
                    c = slice(n * 512, (n + 1) * 512)
                    own(stt(hv[:, c], hv[:, c], ALPHA, acc[n][:, :], ALU.mult, ALU.add))
                own.settle()
                dve.sem_inc(acc_read, 1)
                if t:
                    dve.wait_ge(y_out, 16 * t)
                layer_norm(hv, yout, t, 1, ln2[:, 0, :], ln2[:, 1, :], var2_ready, root2_ready, y_out_ready)

            def tick():
                k = ticks[0]
                ticks[0] += 1
                if k in (BLOCKS + 1, PROMPT_BLOCKS + 1):
                    finish(k // BLOCKS - 1)
                if 1 <= k <= PROMPT_BLOCKS:
                    dve.wait_ge(gelu_done, k)
                    tt(w8[(k - 1) % 2], gl[(k - 1) % 2], gate[:, (k - 1) * WB:k * WB], ALU.mult).then_inc(w_ready, 1)
                if k < PROMPT_BLOCKS:
                    for j in range(WB):
                        dve.wait_ge(u_in[j], 16 * (k + 1))
                        nc.vector.tensor_tensor_reduce(uslot[j], uslot[j], htile(k // BLOCKS), 1.0, 0.0, ALU.mult, ALU.add,
                                                       dots[k % 2][:, j:j + 1]).then_inc(dot_done, 1)

            def mixer(q):
                step = tick if q.streams else (lambda: None)
                L = {t: q.tiles.index(t) for t in q.tiles}
                nt = q.nt
                for t in q.tiles:
                    for half in range(2):
                        src = bank()
                        vd.give(cp(q.xT[:, 4 * half:4 * half + 4, q.at(t)], src[:, :].rearrange("p (k s) -> p k s", k=4)))
                if not q.streams:
                    for half in range(2):
                        src = bank()
                        own(cp(rowsT[:, 12 * half:12 * half + 12, :], src[:, 0:12 * ROWS].rearrange("p (c r) -> p c r", c=12)), vd)
                    src = bank()
                    own(cp(normT[:, :], src[:, 0:16]), vd)
                    own.settle()
                    own(nc.vector.memset(q.xraw[:, :, 0:3], 0.0))
                else:
                    own(cp(q.xraw.rearrange("p c (b s) -> p c b s", b=DEC_B)[:, :, :, 0:3],
                           rowsT[:, :, 0:24].rearrange("p c (b j) -> p c b j", b=DEC_B)))
                own.settle()
                step()

                arrived = Count(sb_drained, start=SR + before[q.n, "conv"][1])
                conv_c = Count(conv_done, start=CC * q.n)
                for i in turns(dve, q.streams, 4, (own.step, 6 * 3), (arrived, 6), (conv_c, 6)):
                    for j in range(6):
                        arrived.take(dve)
                        o = i * (6 * q.raw) + j * q.raw
                        row = q.xraw2[:, o:o + q.raw] if q.streams else q.xraw2[:, ds(o, q.raw)]
                        o = i * (6 * q.tok) + j * q.tok
                        res = q.C[:, o:o + q.tok] if q.streams else q.C[:, ds(o, q.tok)]
                        o = i * (6 * ROWS) + j * ROWS
                        wr = rowsT.rearrange("p c r -> p (c r)")
                        wr = wr[:, o:o + ROWS] if q.streams else wr[:, ds(o, ROWS)]
                        if q.streams:
                            res = res.rearrange("p (b s) -> p b s", b=DEC_B)
                            row = row.rearrange("p (b s) -> p b s", b=DEC_B)
                        taps = [row[:, :, k:k + DEC_S] if q.streams else row[:, k:k + SEQ] for k in range(CW)]
                        own(tsc(res, taps[0], wr[:, 24:25], wr[:, 28:29], ALU.mult, ALU.add))
                        own.settle()
                        for k in range(1, CW - 1):
                            own(stt(res, taps[k], wr[:, 24 + k:25 + k], res, ALU.mult, ALU.add))
                            own.settle()
                        conv_c.give(stt(res, taps[3], wr[:, 27:28], res, ALU.mult, ALU.add))
                        if j % 3 == 2:
                            step()
                if q.streams:
                    o, i = (q.tail.rearrange("p c (b j) -> p c b j", b=DEC_B),
                            q.xraw.rearrange("p c (b s) -> p c b s", b=DEC_B)[:, :, :, DEC_S:SEG])
                else:
                    o, i = q.tail, q.xraw[:, :, SEQ:SEQ + 3]
                cp(o, i).then_inc(tails_ready, 1)

                dve.wait_ge(par_in, 48)
                dve.wait_ge(sb_drained, SR + before[q.n, "dt"][1] + nt)
                t3 = [nt, SH]
                dtr, dta, dtu, dtw, dtv = q.dtr, q.dta, q.dtu, q.dtw, q.dtv

                def by_tile(v):
                    return v.rearrange("p (t n) -> p t n", t=nt)

                own(tt(by_tile(dtr), by_tile(dtr), bc(headp[:, 0:SH].unsqueeze(1), t3), ALU.add))
                own.settle()
                own(tsc(dta, dtr, -1.0, None, ALU.mult))
                own.settle()
                tt(dta, dta, dtr, ALU.max).then_inc(dt_v, 1)
                dve.wait_ge(dt_e, 2 * q.n + 1)
                tsc(dtw, dtu, 1.0, None, ALU.add).then_inc(dt_v, 1)
                own(tsc(dtv, dtu, 1.0, -1.0, ALU.add, ALU.add))
                dve.wait_ge(dt_e, 2 * q.n + 2)
                own.settle()
                own(tsc(dta, dtv, 0.0, None, ALU.is_equal))
                own.settle()
                own(tt(dtv, dtv, dta, ALU.add))
                own(tt(dtw, dtw, dta, ALU.add))
                own.settle()
                own(nc.vector.reciprocal(dtv, dtv))
                own.settle()
                own(tt(dtw, dtw, dtu, ALU.mult))
                own.settle()
                own(tt(dtv, dtv, dtw, ALU.mult))
                own.settle()
                own(stt(dtv, dtr, 0.0, dtv, ALU.max, ALU.add))
                if not q.streams:
                    own(tsc(negA, negA, -1.0, None, ALU.mult))
                own.settle()
                tt(by_tile(q.av), by_tile(dtv), bc(negA.unsqueeze(1), t3), ALU.mult).then_inc(a_ready, 1)

                for i in turns(dve, q.streams, 2, (vf, 2 * nt), (vd, 2 * nt)):
                    for b in range(2):
                        for k in range(nt):
                            src = bank()
                            o = i * 1024 + (k * 2048 + b * 512)
                            vd.give(cp(q.B[:, o:o + 512] if q.streams else q.B[:, ds(o, 512)], src[:, :]))
                    step()
                vd.upto(dve)

                def rope(o, heads):
                    v = {t: q.qkv[:, L[t], o:o + heads * HD].rearrange("p (h n) -> p h n", h=heads) for t in q.tiles}
                    T = [x[:, 0:nt * heads * 8].rearrange("p (t h n) -> p t h n", t=nt, h=heads) for x in q.rtmp]
                    for t in q.tiles:
                        c, s = bc(cos[:, t, :].unsqueeze(1), [heads, 8]), bc(sin[:, t, :].unsqueeze(1), [heads, 8])
                        own(tt(T[0][:, L[t]], v[t][:, :, 0:8], c, ALU.mult))
                        own(tt(T[1][:, L[t]], v[t][:, :, 8:16], s, ALU.mult))
                        own(tt(T[2][:, L[t]], v[t][:, :, 8:16], c, ALU.mult))
                        own(tt(T[3][:, L[t]], v[t][:, :, 0:8], s, ALU.mult))
                    own.settle()
                    for t in q.tiles:
                        own(tt(v[t][:, :, 0:8], T[0][:, L[t]], T[1][:, L[t]], ALU.subtract))
                        own(tt(v[t][:, :, 8:16], T[2][:, L[t]], T[3][:, L[t]], ALU.add))
                    own.settle()

                dve.wait_ge(sb_filled, before[q.n, "attention"][1])
                rope(0, HEADS + KVH)
                rope(O_QI, IH + 1)
                dve.sem_inc(rope_done, 1)
                step()
                step()

                def keep_q(t):
                    src = bank()
                    v = src[:, :].rearrange("p (r s) -> p r s", r=REP)
                    if t < 2:
                        vd.give(cp(q.qn[0:64, :, :], v[0:64]))
                    else:
                        cp(q.qn[0:64, :, :], v[0:64])
                        for r in range(REP):
                            last = tt(q.qm[:, r, :, :], bc(v[:, r, :].unsqueeze(1), [4, P]), pair, ALU.mult)
                        vd.give(last)

                def select(t):
                    S = P if t == 0 else 2 * P
                    s, tmp, neg = q.score[:, 0:S], q.scoret[:, 0:S], q.negm[:, 0:S]
                    for pr in range(2):
                        src = bank()
                        for r in range(2):
                            hh = 2 * pr + r
                            wi = q.qkv[:, L[t], O_WI + hh:O_WI + hh + 1]
                            o = s if hh == 0 else tmp
                            own(tsc(o, src[:, r * 256:r * 256 + S], 0.0, wi, ALU.max, ALU.mult), vd if r == 1 else None)
                            own.settle()
                            if hh:
                                own(tt(s, s, tmp, ALU.add))
                                own.settle()
                    own(tt(s, s, adm[:, t, 0:S], ALU.mult))
                    own.settle()
                    own(tt(s, s, nadm[:, t, 0:S], ALU.add))
                    own.settle()
                    k = TOPK_P if t < 2 else TOPK_S
                    while k > 0:
                        own(nc.vector.max(m8, s))
                        own.settle()
                        if k < 8:
                            own(nc.vector.memset(m8[:, k:8], GONE))
                            own.settle()
                        own(nc.vector.match_replace(s, m8, s, GONE))
                        own.settle()
                        k -= 8
                    own(tsc(neg, s, GONE, NEG, ALU.not_equal, ALU.mult))
                    own.settle()

                first_s = before[q.n, "attention"][1] + 2 * nt + 5 * q.streams

                def logits(n):
                    S = P if n < KVH else 2 * P
                    k = n - q.tiles[0] * KVH
                    if k >= 2:
                        dve.wait_ge(sb_filled, first_s + 3 * (k - 2) + 2)
                    lm = q.lm[n % 2]
                    for pr in range(2):
                        src = bank()
                        own(tt(lm[:, 2 * pr:2 * pr + 2, 0:S], src[:, :].rearrange("p (r s) -> p r s", r=2)[:, :, 0:S],
                               bc(q.negm[:, 0:S].unsqueeze(1), [2, S]), ALU.add), vd)
                    own.settle()
                    o = 4 * (n % 2)
                    own(nc.vector.tensor_reduce(nmx[:, o:o + 4], lm[:, :, 0:S], AX_X, ALU.max))
                    own.settle()
                    tsc(nmx[:, o:o + 4], nmx[:, o:o + 4], -LOG_SCALE, None, ALU.mult).then_inc(max_ready, 1)

                def normalise(n):
                    S = P if n < KVH else 2 * P
                    o = 4 * (n % 2)
                    dve.wait_ge(exp_done, n + 1)
                    own(nc.vector.reciprocal(rec[:, o:o + 4], sums[:, o:o + 4]))
                    own.settle()
                    lm = q.lm[n % 2]
                    tt(lm[:, :, 0:S], lm[:, :, 0:S], bc(rec[:, o:o + 4].unsqueeze(2), [REP, S]), ALU.mult).then_inc(probs_ready, 1)

                if q.streams:
                    dve.wait_ge(cache_in, 16 * 6)
                done = None
                for t in q.tiles:
                    keep_q(t)
                    select(t)
                    step()
                    for v in range(KVH):
                        n = t * KVH + v
                        keep_q(t)
                        logits(n)
                        step()
                        normalise(n)
                        if done is not None:
                            step()
                        done = n
                for j in range(2 * nt):
                    src = bank()
                    b, k = j // nt, j % nt
                    vd.give(cp(q.ya[:, k, b * 512:(b + 1) * 512], src[:, :]))
                step()

                for t in q.tiles:
                    src = bank()
                    own(cp(q.acs[:, L[t], :], src[:, 0:64]), vd)
                own.settle()
                tt(q.ex[:, :, 2 * SH:3 * SH], q.acs[:, :, SH:2 * SH], q.acs[:, :, 0:SH], ALU.subtract).then_inc(sum_ready, 1)
                dve.wait_ge(ex_ready, q.n + 1)
                dve.wait_ge(kv_out[q.n], 16 * 3 * nt)
                for t in q.tiles:
                    dve.wait_ge(sb_drained, SR + before[q.n, "ssd"][1] + 5 * (L[t] + 1) + (t == 2))
                    step()
                    xs = q.xbt[:, 0:DI].rearrange("p (h n) -> p h n", h=SH)
                    at = L[t] * SH
                    own(tt(q.xdt.rearrange("p (h n) -> p h n", h=SH), xs, bc(dtv[:, at:at + SH].unsqueeze(2), [SH, HD]), ALU.mult))
                    own.settle()
                    own(tt(q.xdtd.rearrange("p (h n) -> p h n", h=SH), q.xdt.rearrange("p (h n) -> p h n", h=SH),
                           bc(q.ex[:, L[t], 2 * SH:3 * SH].unsqueeze(2), [SH, HD]), ALU.mult))
                    for g in range(G):
                        src = bank()
                        own(tt(q.cbm, src[:, 0:P], tri[:, t // 2, :], ALU.mult), vd)
                        for half in range(2):
                            src = bank()
                            for i in range(4):
                                hh = g * 8 + half * 4 + i
                                own(tsc(q.MT[:, half * 4 + i, :], src[:, i * P:(i + 1) * P], q.acs[:, L[t], hh:hh + 1], 0.0,
                                        ALU.subtract, ALU.min), vd if i == 3 else None)
                        if t == 2:
                            own(tt(q.CTm, bc(q.xc[:, 20 + g, :].unsqueeze(1), [DEC_B, P]), blkcol, ALU.mult))
                            own(tt(q.Bm, bc(q.xbt[:, DI + g * P:DI + (g + 1) * P].unsqueeze(1), [DEC_B, P]),
                                   bc(blk.unsqueeze(2), [DEC_B, P]), ALU.mult))
                        own.settle()
                        dve.sem_inc(seg_ready, 1)
                        step()
                        dve.wait_ge(seg_exp, t * G + g + 1)
                        tt(q.MT, q.MT, bc(q.cbm.unsqueeze(1), [8, P]), ALU.mult).then_inc(mt_ready, 1)
                        if t == 2:
                            for c in range(4 * g, 4 * g + 4):
                                for half in range(2):
                                    src = bank()
                                    for b in range(4):
                                        bb = 4 * half + b
                                        sv = q.sst[c % 2][:, bb, :]
                                        last = stt(sv, sv, dec[:, c, bb:bb + 1], src[:, b * P:(b + 1) * P], ALU.mult, ALU.add)
                                    own(last, vd)
                                    own.settle()
                                    dve.sem_inc(new_ready, 1)
                                if c % 4 == 1:
                                    step()
                            step()
                        yg = q.y[:, L[t], g * 512:(g + 1) * 512]
                        y3 = yg.rearrange("p (r n) -> p r n", r=8)
                        hs = slice(g * 8, g * 8 + 8)
                        dsk = headp[:, 2 * SH + g * 8:2 * SH + g * 8 + 8]
                        own(tt(y3, xs[:, hs, :], bc(dsk.unsqueeze(2), [8, HD]), ALU.mult))
                        own.settle()
                        if t > 0:
                            src = bank()
                            own(tt(q.ytmp.rearrange("p (r n) -> p r n", r=8), src[:, :].rearrange("p (r n) -> p r n", r=8),
                                   bc(q.ex[:, L[t], hs].unsqueeze(2), [8, HD]), ALU.mult), vd)
                            own.settle()
                            own(tt(yg, yg, q.ytmp, ALU.add))
                            own.settle()
                        src = bank()
                        own(tt(yg, yg, src[:, :], ALU.add), vd)
                        if t < 2:
                            src = bank()
                            st = q.stateT[:, g * 512:(g + 1) * 512]
                            if t == 0:
                                own(cp(st, src[:, :]), vd)
                            else:
                                s3 = st.rearrange("p (r n) -> p r n", r=8)
                                own(tt(s3, s3, bc(q.ex[:, 1, SH + g * 8:SH + g * 8 + 8].unsqueeze(2), [8, HD]), ALU.mult))
                                own.settle()
                                own(tt(st, st, src[:, :], ALU.add), vd)
                    own.settle()
                    dve.sem_inc(y_done, 1)

                dve.sem_inc(gated, 1)
                g0 = q.n * (1 + 4 * PR.nt)
                zin, gated_c = Count(sb_drained, start=SR + before[q.n, "z"][1]), Count(gated, start=g0 + 1)
                for i in turns(dve, q.streams, 2, (zin, 2 * nt), (gated_c, 2 * nt)):
                    for j in range(2 * nt):
                        zin.take(dve)
                        b, k = j // nt, j % nt
                        o = i * 1024 + (k * 2048 + b * 512)
                        yv = q.B[:, o:o + 512] if q.streams else q.B[:, ds(o, 512)]
                        gated_c.give(tt(yv, yv, q.zs[:, j, :], ALU.mult))
                    step()
                gated_c.upto(dve)
                for k in range(nt):
                    for g in range(G):
                        n = k * G + g
                        yg = q.y[:, k, g * 512:(g + 1) * 512]
                        own(nc.vector.tensor_tensor_reduce((q.zs if n < 4 else q.gt)[:, n % 4, :], yg, yg, 1.0, 0.0,
                                                           ALU.mult, ALU.add, ms[:, n:n + 1]))
                own.settle()
                dve.sem_inc(ms_ready, 1)
                dve.wait_ge(rms_root, q.n + 1)
                own(nc.vector.reciprocal(rstd, rstd))
                own.settle()
                for k in range(nt):
                    y4 = q.y[:, k, :].rearrange("p (g n) -> p g n", g=G)
                    tt(y4, y4, bc(rstd[:, k * G:(k + 1) * G].unsqueeze(2), [G, 512]), ALU.mult).then_inc(yn_ready, 1)
                step()

                for i in turns(dve, q.streams, 2, (vf, 2 * nt), (vd, 2 * nt)):
                    for b in range(2):
                        for k in range(nt):
                            src = bank()
                            o = i * 512 + (nt * D + k * D)
                            v = q.YD[:, o:o + 512] if q.streams else q.YD[:, ds(o, 512)]
                            if b == 0:
                                vd.give(cp(v, src[:, :]))
                            else:
                                if k == 0:
                                    vd.upto(dve)
                                vd.give(tt(v, v, src[:, :], ALU.add))
                    step()
                vd.upto(dve)

                dve.wait_ge(bg_in[q.n], 16)
                mixed_c = Count(mixed_ready, start=q.n * 2 * PR.nt)
                gr, gp = Count(gate_ready, start=q.n * 4 * PR.nt), Count(gate_pre, start=q.n * 4 * PR.nt)
                for i in turns(dve, q.streams, 2, (vf, 2 * nt), (vd, 2 * nt), (gr, 2 * nt), (gp, 2 * nt), (own.step, 2 * nt),
                               (mixed_c, nt)):
                    def part(v, o):
                        return v[:, o:o + 512] if q.streams else v[:, ds(o, 512)]
                    for b in range(2):
                        for k in range(nt):
                            src = bank()
                            own(tt(q.gt[:, nt * b + k, :], src[:, :], part(q.bg, i * 512 + b * 1024), ALU.add), vd)
                        vd.upto(dve)
                        dve.sem_inc(gate_pre, nt)
                        gp.n += nt
                    for k in range(nt):
                        gr.take(dve)
                        yav = part(q.YD, i * 512 + k * D)
                        own(tt(yav, yav, q.gt[:, k, :], ALU.mult))
                    for k in range(nt):
                        gr.take(dve)
                        own(tt(q.gt[:, nt + k, :], q.gt[:, nt + k, :], part(q.YD, i * 512 + (nt * D + k * D)), ALU.mult))
                    own.settle()
                    for k in range(nt):
                        yav = part(q.YD, i * 512 + k * D)
                        mixed_c.give(tt(yav, yav, q.gt[:, nt + k, :], ALU.add))
                    step()

                dve.wait_ge(x2_in[q.n], 16)
                for j in range(2 * nt):
                    src = bank()
                    b, k = j // nt, j % nt
                    c = slice(b * 512, (b + 1) * 512)
                    own(stt(htile(q.tiles[k])[:, c], q.x2[:, k, c], ALPHA, src[:, :], ALU.mult, ALU.add), vd)
                own.settle()
                step()
                dve.wait_ge(ln1_in[q.n], 32)
                for t in q.tiles:
                    layer_norm(htile(t), htile(t), t, 0, q.ln1[:, 0, :], q.ln1[:, 1, :], var1_ready, root1_ready, h_ready)
                step()
                step()
                step()

                for t in q.tiles:
                    for quarter in range(4):
                        src = bank()
                        own(cp(sc[t][:, quarter * 512:(quarter + 1) * 512], src[:, :]), vd)
                    own.settle()
                    step()

            def pick(t, pause):
                for c in range(16):
                    s = sc[t][:, c * NK:(c + 1) * NK]
                    own(nc.vector.max(v16[:, c, 0:8], s))
                    own.settle()
                    own(nc.vector.max_index(i16[:, c, 0:8], v16[:, c, 0:8], s))
                    own.settle()
                    own(nc.vector.match_replace(s, v16[:, c, 0:8], s, GONE))
                    own.settle()
                    own(nc.vector.max(v16[:, c, 8:16], s))
                    own.settle()
                    own(nc.vector.max_index(i16[:, c, 8:16], v16[:, c, 8:16], s))
                    if c % 4 == 3:
                        own.settle()
                        pause()
                own(cp(f16, i16))
                v4 = v16.rearrange("p (h a) k -> p h a k", a=2)
                for hh in range(PH):
                    own(tt(cand[:, hh * 256:(hh + 1) * 256].rearrange("p (i j) -> p i j", i=PTOP),
                           bc(v4[:, hh, 0, :].unsqueeze(2), [PTOP, PTOP]), bc(v4[:, hh, 1, :].unsqueeze(1), [PTOP, PTOP]),
                           ALU.add))
                own.settle()
                for hh in range(PH):
                    s = cand[:, hh * 256:(hh + 1) * 256]
                    o = hh * PTOP
                    own(nc.vector.max(ts16[:, hh, 0:8], s))
                    own.settle()
                    own(nc.vector.max_index(pos[:, o:o + 8], ts16[:, hh, 0:8], s))
                    own.settle()
                    own(nc.vector.match_replace(s, ts16[:, hh, 0:8], s, GONE))
                    own.settle()
                    own(nc.vector.max(ts16[:, hh, 8:16], s))
                    own.settle()
                    own(nc.vector.max_index(pos[:, o + 8:o + 16], ts16[:, hh, 8:16], s))
                own.settle()
                pause()
                f4 = f16.rearrange("p (h a) k -> p h a k", a=2)
                for half, (op, by, e) in enumerate(((ALU.logical_shift_right, 4, e1), (ALU.bitwise_and, 15, e2))):
                    own(tsc(phi, pos, by, None, op))
                    own.settle()
                    own(cp(phf, phi))
                    own.settle()
                    own(tt(hot, bc(phf.unsqueeze(2), [128, PTOP]), bc(iota.unsqueeze(1), [128, PTOP]), ALU.is_equal))
                    own.settle()
                    for hh in range(PH):
                        hv = hot[:, hh * PTOP:(hh + 1) * PTOP, :]
                        own(tt(hv, hv, bc(f4[:, hh, half, :].unsqueeze(1), [PTOP, PTOP]), ALU.mult))
                    own.settle()
                    own(nc.vector.tensor_reduce(e, hot, AX_X, ALU.add))
                    own.settle()
                own(stt(eidx[:, t * P:(t + 1) * P], e1, float(NK), e2, ALU.mult, ALU.add))
                own(cp(s8, ts16[:, :, 0]))
                own.settle()
                tt(ts16, ts16, bc(s8.unsqueeze(2), [PH, PTOP]), ALU.subtract).then_inc(score_e, 1)
                dve.sem_inc(idx_ready, 1)
                dve.wait_ge(score_v, t + 1)
                own(nc.vector.tensor_reduce(s8, ts16, AX_X, ALU.add))
                own.settle()
                own(nc.vector.reciprocal(s8, s8))
                own.settle()
                own(tt(gate[:, t * P:(t + 1) * P].rearrange("p (h k) -> p h k", h=PH), ts16, bc(s8.unsqueeze(2), [PH, PTOP]),
                       ALU.mult))
                own.settle()

            mixer(PR)
            own(nc.vector.memset(zero, 0.0))
            pick(0, lambda: None)
            pick(1, tick)
            mixer(ST)
            pick(2, lambda: ticks[0] < TICKS and tick())
            while ticks[0] < TICKS:
                tick()
            landed = [Count(u_in[s], start=PROMPT_BLOCKS if s < WB else 0, step=16) for s in slot_sem]
            gelu_c, w_c = Count(gelu_done, start=PROMPT_BLOCKS), Count(w_ready, start=PROMPT_BLOCKS)
            with loop(dve, P // PB, (gelu_c, 1), (w_c, 1), *((c, 1) for c in landed)) as i:
                for j in range(PB):
                    landed[j].take(dve)
                    nc.vector.tensor_tensor_reduce(uslot8[j], uslot8[j], hS, 1.0, 0.0, ALU.mult, ALU.add,
                                                   dots8[:, j:j + 1]).then_inc(dot8_done, 1)
                gelu_c.take(dve)
                w_c.give(tt(w88, gl8, gate[:, ds(i * PB + 2 * P, PB)], ALU.mult))
            finish(2)


_INS = ['x_prompt', 'x_sample', 'cache_k', 'cache_v', 'cache_kidx', 'state_conv', 'state_ssm', 'w_in', 'b_gate', 'conv_w',
        'conv_b', 'dt_bias', 'a_log', 'd_skip', 'ssm_norm_w', 'w_attn_br', 'w_ssm_br', 'w_out', 'ln1_g', 'ln1_b',
        'peer_wq', 'peer_keys1', 'peer_keys2', 'peer_u', 'peer_v', 'ln2_g', 'ln2_b']
_OUTS = [("y_prompt", (1, SEQ, D)), ("y_sample", (DEC_B, DEC_S, D)), ("p_k", (1, 1, SEQ, KVH, HD)), ("p_v", (1, 1, SEQ, KVH, HD)),
         ("p_kidx", (1, 1, SEQ, HD)), ("p_conv", (1, 1, CW - 1, CONV)), ("p_ssm", (1, 1, SH, HD, N)),
         ("s_k", (1, DEC_B, DEC_S, KVH, HD)), ("s_v", (1, DEC_B, DEC_S, KVH, HD)), ("s_kidx", (1, DEC_B, DEC_S, HD)),
         ("s_conv", (1, DEC_B, CW - 1, CONV)), ("s_ssm", (1, DEC_B, SH, HD, N))]


def kernel(**inputs):
    import concourse.bacc as _bacc
    from concourse import mybir as _mybir
    from concourse.bass_utils import run_bass_kernel_spmd as _run

    nc = _bacc.Bacc("TRN2", target_bir_lowering=False, num_devices=1)
    arrays, a, out = {}, {}, {}
    table, where = const_table()
    for name in _INS + ["table"]:
        v = np.ascontiguousarray(table if name == "table" else inputs[name])
        arrays[f"in_{name}_dram"] = v
        a[name] = nc.dram_tensor(f"in_{name}_dram", v.shape, _mybir.dt.from_np(v.dtype), kind="ExternalInput").ap()
    for name, shape in _OUTS:
        out[name] = nc.dram_tensor(f"out_{name}_dram", shape, F32, kind="ExternalOutput").ap()
    build(nc, a, out, where)
    r = _run(nc, [arrays], core_ids=[0])
    return tuple(r.results[0][f"out_{name}_dram"] for name, _ in _OUTS)
```

```python
from contextlib import ExitStack, contextmanager

import numpy as np

import concourse.bass as bass
from concourse import mybir
from concourse.alu_op_type import AluOpType as ALU

ACT = mybir.ActivationFunctionType
F32 = mybir.dt.float32
U32 = mybir.dt.uint32
AX_X = mybir.AxisListType.X
ds = bass.ds

P = 128
D = 1024
KC = D // P
TILES = 3
TOK = TILES * P
SEQ, DEC_B, DEC_S, PAST = 256, 8, 16, 128
HEADS, HD, KVH, REP = 16, 64, 4, 4
IH = 4
CHUNK = 64
TOPK_P, TOPK_S = 64, 36
DI, SH, G, N = 2048, 32, 4, 128
CONV, CW = 3072, 4
CC = CONV // P
PH, NK, PTOP = 8, 128, 16
ALPHA = 2.0 ** 0.25
EPS = 1e-5
NEG = -1e30
GONE = -3e38
LOG_SCALE = HD ** -0.5

O_K, O_V, O_QI, O_KI, O_WI = 1024, 1280, 1536, 1792, 1856
O_Z = 1860
O_XBC = O_Z + DI
O_DT = O_XBC + CONV
O_GATE = O_DT + SH

SEG = DEC_S + CW - 1
ROWS = DEC_B * (CW - 1) + CW + 1
VR, SR = 4, 2

WB = 2
SLOTS = 2 * WB
BLOCKS = PH * PTOP // WB
PROMPT_BLOCKS = 2 * BLOCKS
TICKS = PROMPT_BLOCKS + 3
PB = 8
PICK_STEPS = 8
TICKS_AT = dict(pick=1, conv=1, dt=1, qkv=1, tails=2, rope=1, keys=2, item1=2, item2=1, item3=1, ya=1,
                select=1, xbt=2, seg=1, state=1, group=1, y=1, z=1, yT=1, ym=0, gates=1, mixedT=1, out=1, hT=1, wq=1,
                scores=2)


def const_table():
    t = np.arange(P)
    parts = {}
    parts["ident"] = np.eye(P)
    stream = t // DEC_S
    same = (stream[:, None] == stream[None, :])
    causal = (t[:, None] <= t[None, :])
    parts["tri"] = np.stack([causal, causal & same], 1)
    parts["same"] = np.stack([np.ones((P, P)), same], 1)
    adm = np.zeros((P, TILES, 2 * P))
    for tile in range(2):
        q = (tile * P + t) // CHUNK
        k = np.arange(2 * P) // CHUNK
        adm[:, tile] = k[None, :] <= q[:, None]
    adm[:, 2, :P] = 1
    adm[:, 2, P:] = same
    parts["adm"] = adm
    parts["nadm"] = (1 - adm) * NEG
    parts["blk"] = stream[:, None] == np.arange(DEC_B)[None, :]
    parts["blkcol"] = np.broadcast_to(np.arange(DEC_B)[:, None] == stream[None, :], (P, DEC_B, P))
    pair = np.zeros((P, 4, P))
    for j in range(4):
        pair[:64, j] = stream == 2 * j
        pair[64:, j] = stream == 2 * j + 1
    parts["pair"] = pair
    rd = HD // 4
    half = rd // 2
    inv = np.float32(500000.0) ** (-(np.arange(half, dtype=np.float32) * np.float32(2)) / np.float32(rd))
    pos = np.stack([t, P + t, PAST + t % DEC_S], 1).astype(np.float32)
    ang = pos[:, :, None] * inv.astype(np.float32)
    parts["cos"] = np.cos(ang.astype(np.float32))
    parts["sin"] = np.sin(ang.astype(np.float32))
    parts["iota"] = np.broadcast_to(np.arange(PTOP), (P, PTOP))
    parts["eps"] = np.full((P, 1), EPS)
    at, cols = 0, []
    where = {}
    for name, v in parts.items():
        v = np.ascontiguousarray(v, dtype=np.float32)
        where[name] = (at, v.shape[1:])
        at += int(np.prod(v.shape[1:]))
        cols.append(v.reshape(P, -1))
    return np.concatenate(cols, 1), where


class Steps:

    def __init__(self, tick):
        self.tick, self.n, self.seen = tick, 0, []

    def run(self, times):
        for _ in range(times):
            if self.n < TICKS:
                self.tick(self.n)
                self.n += 1

    def at(self, place):
        self.seen.append(place)
        self.run(TICKS_AT[place])


class Count:

    def __init__(self, sem, start=0, step=1):
        self.sem, self.n, self.step, self.extra = sem, start, step, None

    def value(self, n=None):
        n = self.n if n is None else n
        return n * self.step if self.extra is None else (self.extra + n) * self.step

    def give(self, ins):
        ins.then_inc(self.sem, self.step)
        self.n += 1
        return ins

    def take(self, eng):
        self.n += 1
        eng.wait_ge(self.sem, self.value())

    def upto(self, eng):
        eng.wait_ge(self.sem, self.value())


class Own:

    def __init__(self, eng, sem):
        self.eng, self.step = eng, Count(sem)
        self.last = self.step

    def __call__(self, ins, signal=None):
        self.last = self.step if signal is None else signal
        return self.last.give(ins)

    def settle(self):
        self.last.upto(self.eng)


@contextmanager
def loop(eng, times, *per):
    starts = [c.n for c, _ in per]
    with eng.Fori(0, times) as i:
        for c, k in per:
            c.extra = i * k
        yield i
        for (c, k), s in zip(per, starts):
            assert c.n == s + k, (c.sem, c.n, s, k)
    for (c, k), s in zip(per, starts):
        c.extra, c.n = None, s + times * k


def turns(eng, straight, times, *per):
    if straight:
        yield from range(times)
    else:
        with loop(eng, times, *per) as i:
            yield i


class Pass:

    def __init__(self, n, tiles):
        self.n, self.tiles, self.nt, self.streams = n, tiles, len(tiles), n == 1
        self.tok = P * self.nt
        self.raw = DEC_B * SEG if self.streams else CW - 1 + SEQ

    def at(self, t):
        k = self.tiles.index(t)
        return slice(k * P, (k + 1) * P)


def build(nc, a, out, where):
    ctx = ExitStack()
    with ctx:
        def sb(name, words, dt=F32):
            return ctx.enter_context(nc.sbuf_tensor(name, [P, words], dt))

        def sem(name):
            return ctx.enter_context(nc.semaphore(name))

        cst = sb("cst", a["table"].shape[1])

        def const(name):
            at, shape = where[name]
            v = cst[:, at:at + int(np.prod(shape))]
            if len(shape) == 2:
                v = v.rearrange("p (a b) -> p a b", a=shape[0])
            return v

        ident, tri, same, adm, nadm = (const(k) for k in ("ident", "tri", "same", "adm", "nadm"))
        blk, blkcol, pair, cos, sin, iota = (const(k) for k in ("blk", "blkcol", "pair", "cos", "sin", "iota"))
        eps = const("eps")
        rowsT = sb("rowsT", CC * ROWS)[:, :].rearrange("p (c r) -> p c r", c=CC)
        normT = sb("normT", 16)
        headp = sb("headp", 3 * SH)
        wdt = sb("wdt", KC * SH)[:, :].rearrange("p (k n) -> p k n", k=KC)
        wbuf = [sb(f"wbuf{i}", KC * 512)[:, :].rearrange("p (k n) -> p k n", k=KC) for i in range(2)]
        small = sb("small", 1050)

        ZONE = 24128
        EX = 2 * SLOTS * D
        BIG = sb("BIG", ZONE + EX + 2048 + SLOTS * P + 2048 + D + P + 2 * TILES * P + 256)
        big = [0]

        def take(words, end=None):
            v = BIG[:, big[0]:big[0] + words]
            big[0] += words
            assert end is None or big[0] <= end, (big[0], end)
            return v

        def tiles3(v, nt):
            return v.rearrange("p (t n) -> p t n", t=nt)

        def lay(q, end):
            nt, tok, first = q.nt, q.tok, big[0]
            q.xT = take(KC * tok).rearrange("p (k t) -> p k t", k=KC)
            YD = take(nt * D + 2560)
            q.YD = YD
            q.ya = tiles3(YD[:, 0:nt * D], nt)
            q.attnT = YD[:, nt * D:2 * nt * D].rearrange("p (k t) -> p k t", k=KC)
            q.xbt = YD[:, nt * D:nt * D + 2560]
            q.ym = tiles3(YD[:, nt * D:2 * nt * D], nt)
            q.tails = YD[:, 0:3072]
            q.qp = tiles3(YD[:, 0:nt * 2048], nt)
            q.B = take(nt * 2048)
            q.qkv = q.y = tiles3(q.B, nt)
            q.C = take(CC * tok)
            q.xc = q.C.rearrange("p (c t) -> p c t", c=CC)
            q.yTv = q.C[:, 0:16 * tok].rearrange("p (k t) -> p k t", k=16)
            A = q.A = big[0]

            def cut(v, pattern=None, **kw):
                return v if pattern is None else v.rearrange(pattern, **kw)

            q.xraw2 = take(CC * q.raw)
            q.xraw = q.xraw2.rearrange("p (c t) -> p c t", c=CC)
            q.x1 = tiles3(take(nt * D), nt)
            q.nrow = DEC_B * (CW - 1) if q.streams else CW - 1
            if q.streams:
                assert big[0] - A == 4672
                q.kc = take(5 * 512).rearrange("p (v n) -> p v n", v=5)
                q.vc = take(2048).rearrange("p (b n) -> p b n", b=DEC_B)
            q.tail = take(CC * q.nrow).rearrange("p (c j) -> p c j", c=CC)
            top = big[0]
            big[0] = A
            q.kT = take(5 * tok).rearrange("p (v t) -> p v t", v=5)
            if q.streams:
                q.kcT = take(5 * 512).rearrange("p (v j s) -> p v j s", v=5, j=4)
            q.qn = take(512).rearrange("p (r t) -> p r t", r=REP)
            q.score, q.negm = ([take(256) for _ in q.tiles] for _ in range(2))
            q.scoret = take(256)
            if q.streams:
                assert big[0] <= A + 4672
                big[0] = A + 4672 + 5 * 512 + 2048
            q.lm = [take(1024).rearrange("p (r s) -> p r s", r=REP) for _ in range(2)]
            q.PT = take(1024).rearrange("p (h r t) -> p h r t", h=2, r=REP)
            spot = big[0]
            if q.streams:
                q.qm = take(2048).rearrange("p (r j t) -> p r j t", r=REP, j=4)
            top = max(top, big[0])
            big[0] = spot
            q.rtmp = [take(nt * 160) for _ in range(4)]
            top = max(top, big[0])
            big[0] = A
            q.xdt, q.xdtd = take(2048), take(2048)
            q.ahead = not q.streams
            q.MT = [take(1024).rearrange("p (r l) -> p r l", r=8) for _ in range(1 + q.ahead)]
            if q.streams:
                q.CTm = take(1024).rearrange("p (b t) -> p b t", b=DEC_B)
                q.Bm = take(1024).rearrange("p (b n) -> p b n", b=DEC_B)
                q.pT = take(4096).rearrange("p (b n) -> p b n", b=DEC_B)
                q.sst = [take(1024).rearrange("p (b n) -> p b n", b=DEC_B) for _ in range(2)]
            else:
                q.stateT, q.pso = take(2048), take(2048)
            q.cbm, q.ytmp = [take(128) for _ in range(1 + q.ahead)], take(512)
            top = max(top, big[0])
            big[0] = A
            q.zs = take(2048).rearrange("p (j n) -> p j n", j=4)
            q.gt = take(2048).rearrange("p (j n) -> p j n", j=4)
            q.bg = take(2048)
            q.ln1 = take(2048).rearrange("p (a n) -> p a n", a=2)
            q.keys = take(256).rearrange("p (a n) -> p a n", a=2)
            top = max(top, big[0])
            big[0] = A
            q.qT = take(2048).rearrange("p (c t) -> p c t", c=16)
            q.x2 = tiles3(q.B[:, nt * D:2 * nt * D], nt)
            if not q.streams:
                big[0] = top
                q.gx = take(2048).rearrange("p (j n) -> p j n", j=4)
                top = big[0]
            assert top - first <= end, (top, first, end)
            big[0] = top

        PR, ST = Pass(0, (0, 1)), Pass(1, (2,))
        lay(PR, ZONE + EX)
        big[0] = 0
        lay(ST, ZONE)
        rowsin = PR.YD[:, 0:3072]
        normin = PR.YD[:, 3072:3072 + P]
        SZ = ST.A
        sc = [ST.C[:, 0:2048], ST.B, ST.C[:, 0:2048]]
        room = [[BIG[:, 1024:4608], 0]]

        def tiny(words, dt=F32):
            r = room[0]
            v = r[0][:, r[1]:r[1] + words]
            r[1] += words
            assert r[1] <= r[0].shape[1], r[1]
            return v if dt is F32 else v.bitcast(dt)

        v16 = tiny(256).rearrange("p (c k) -> p c k", c=16)
        i16 = tiny(256, U32).rearrange("p (c k) -> p c k", c=16)
        f16 = tiny(256).rearrange("p (c k) -> p c k", c=16)
        ts16 = tiny(128).rearrange("p (h k) -> p h k", h=PH)
        pos, phi = tiny(128, U32), tiny(128, U32)
        phf, e1, e2 = tiny(128), tiny(128), tiny(128)
        s8 = tiny(8)
        cand = BIG[:, SZ + 9280:SZ + 9280 + 2048]
        hot = BIG[:, SZ + 9280 + 2048:SZ + 9280 + 4096].rearrange("p (k j) -> p k j", j=PTOP)
        big[0] = ZONE
        uslot = [take(D) for _ in range(SLOTS)]
        vslot = [take(D) for _ in range(SLOTS)]
        hP = tiles3(take(2048), 2)
        diag0 = take(SLOTS * P)
        ln2 = take(2048).rearrange("p (a n) -> p a n", a=2)
        yout = take(D)
        zero = take(P)
        gate = take(TILES * P)
        eidx = take(TILES * P).bitcast(U32)
        keysT = take(256).rearrange("p (a n) -> p a n", a=2)
        hS = ST.B[:, 0:D]
        big[0] = SZ
        uslot8 = [take(D) for _ in range(PB - SLOTS)] + uslot
        vslot8 = [take(D) for _ in range(PB - SLOTS)] + vslot
        diag8 = take(PB * P).rearrange("p (j n) -> p j n", j=PB)
        slot_sem = [4, 5, 6, 7, 0, 1, 2, 3]
        diag = diag0.rearrange("p (j n) -> p j n", j=SLOTS)

        def htile(t):
            return hP[:, t, :] if t < 2 else hS

        room[0] = [small[:, :], 0]
        for q in (PR, ST):
            n = q.nt * SH
            q.dtr, q.dtv, q.dta, q.dtu, q.dtw, q.av = (tiny(n) for _ in range(6))
            q.acs = tiny(2 * n).rearrange("p (t n) -> p t n", t=q.nt)
            q.ex = tiny(3 * n).rearrange("p (t n) -> p t n", t=q.nt)
            if q is PR:
                room[0][1] = 0
        room[0][1] = 11 * 64
        negA = tiny(SH)
        dec = tiny(128).rearrange("p (c b) -> p c b", c=16)
        m8 = tiny(16)
        nmx, sums, rec = tiny(8), tiny(8), tiny(8)
        ms, rstd = tiny(8), tiny(8)
        norms = [(tiny(12), tiny(2), tiny(2)) for _ in range(2)]
        dots, gl, w8 = ([tiny(WB) for _ in range(2)] for _ in range(3))
        dots8, gl8, w88 = tiny(PB), tiny(PB), tiny(PB)
        islot = [tiny(4 * WB, U32) for _ in range(2)]
        islot8 = [tiny(PB, U32) for _ in range(2)]

        psum = [ctx.enter_context(nc.psum_tensor(f"bank{i}", [P, 512], F32)) for i in range(8)]
        acc = psum[6:8]

        const_in, x_in, rows_in, par_in, wdt_in = (sem(s) for s in ("const_in", "x_in", "rows_in", "par_in", "wdt_in"))
        w_in_sem = [sem("wbuf0_loaded"), sem("wbuf1_loaded")]
        vb_filled, vb_drained = sem("v_bank_filled"), sem("v_bank_drained")
        sb_filled, sb_drained = sem("s_bank_filled"), sem("s_bank_drained")
        dve_step, pool_step = sem("dve_step"), sem("pool_step")
        conv_done, silu_done, tails_ready = sem("conv_done"), sem("silu_done"), sem("tails_ready")
        rope_done, cache_in = sem("rope_done"), sem("cache_in")
        tails_out, kv_out, bg_in, x2_in, ln1_in = ([sem(f"{s}{n}") for n in range(2)]
                                                   for s in ("tails_out", "kv_out", "bg_in", "x2_in", "ln1_in"))
        max_ready, exp_done, probs_ready = sem("max_ready"), sem("exp_done"), sem("probs_ready")
        dt_e, dt_v = sem("dt_steps_by_act"), sem("dt_steps_by_dve")
        a_ready, sum_ready, ex_ready = sem("a_ready"), sem("sums_ready"), sem("decays_ready")
        seg_ready, seg_exp, mt_ready = sem("seg_ready"), sem("seg_exp"), sem("mt_ready")
        old_in = [sem("old_state0_in"), sem("old_state1_in")]
        new_ready, new_out = sem("new_state_ready"), [sem("new_state0_out"), sem("new_state1_out")]
        pso_out = sem("prompt_state_out")
        y_done = sem("tile_y_done")
        gated, ms_ready, rms_root, yn_ready = sem("y_gated"), sem("ms_ready"), sem("rms_root"), sem("yn_ready")
        gate_pre, gate_ready, mixed_ready = sem("gate_pre"), sem("gate_ready"), sem("mixed_ready")
        ln2_in = sem("ln2_in")
        var1_ready, root1_ready, h_ready = sem("var1_ready"), sem("root1_ready"), sem("h_ready")
        keys_in, score_e, score_v = sem("keys_in"), sem("ts_shifted"), sem("ts_exp")
        idx_ready = sem("idx_ready")
        u_in = [sem(f"u_in{j}") for j in range(PB)]
        v_in = [sem(f"v_in{j}") for j in range(PB)]
        dot_done, gelu_done, w_ready, diag_ready, v_used = (sem(s) for s in ("dot_done", "gelu_done", "w_ready", "diag_ready", "v_used"))
        dot8_done, v8_used = sem("stream_dot_done"), sem("stream_v_used")
        acc_full, acc_read = sem("acc_full"), sem("acc_read")
        var2_ready, root2_ready, y_out_ready, y_out = (sem(s) for s in ("var2_ready", "root2_ready", "y_out_ready", "y_out"))

        before, nv, ns = {}, 0, 0
        EARLY = 3 * 2 + 1 + 2
        for q in (PR, ST):
            n, s = q.nt, q.streams
            attn_v = n * (1 + 2 + KVH * 3) + 2 * (not s)
            attn_s = 2 * n + 5 * s + 3 * KVH * n
            ssd_v = n + n * G * 4 + G * sum(t > 0 for t in q.tiles) + G * sum(t < 2 for t in q.tiles) + 32 * s
            ssd_s = 5 * n + (1 + 32 if s else 4)
            for name, v, w in [("start", 2 * n + 3 * (not s), 0), ("conv", 0, 24), ("dt", 0, n), ("qkv", 4 * n, 0),
                               ("tails", 0, 6), ("early", 2 * (not s), 0), ("attention", attn_v, attn_s), ("ya", 2 * n, 0), ("ssd", ssd_v, ssd_s),
                               ("z", 0, 4 * n), ("yT", 0, 4 * n), ("ym", 4 * n, 0), ("gates", 4 * n if s else 4, 0),
                               ("mixedT", 0, 2 * n), ("out", 2 * n, 0), ("hT", 0, 2 * n), ("wq", 0, 4 * n),
                               ("keysT", 0, int(not s)), ("scores", 4, 4 * n + 4 * (n - 1)), ("end", 0, 0)]:
                before[q.n, name] = (nv, ns)
                nv, ns = nv + v, ns + w

        block = ctx.enter_context(nc.Block())
        places = []

        def attention_items(q):
            return [(t, KVH) for t in q.tiles] + [(t, v) for t in q.tiles for v in range(KVH)]

        def store_kv(eng, q):
            eng.wait_ge(rope_done, q.n + 1)
            for t in q.tiles:
                for name, o, n in (("k", O_K, 256), ("v", O_V, 256), ("kidx", O_KI, 64)):
                    if t < 2:
                        dst = out["p_" + name][0, 0, t * P:(t + 1) * P]
                        dst = dst.rearrange("s v n -> s (v n)") if n == 256 else dst
                    else:
                        dst = out["s_" + name][0]
                        dst = dst.rearrange("b s v n -> (b s) (v n)") if n == 256 else dst.rearrange("b s n -> (b s) n")
                    eng.dma_start(dst, q.qkv[:, q.tiles.index(t), o:o + n]).then_inc(kv_out[q.n], 16)

        def load_x(eng, q, dst, done):
            if q.streams:
                eng.dma_start(dst[:, 0, :], a["x_sample"].rearrange("b s n -> (b s) n")).then_inc(done, 16)
            else:
                eng.dma_start(dst, a["x_prompt"][0].rearrange("(t p) n -> p t n", p=P)).then_inc(done, 16)

        def load_ln1(eng, q):
            for i, name in enumerate(("ln1_g", "ln1_b")):
                eng.dma_start(q.ln1[:, i, :], a[name][0].partition_broadcast(P)).then_inc(ln1_in[q.n], 16)

        @block.sync
        def _(sp):
            sp.dma_start(ident, a["table"][:, 0:P]).then_inc(const_in, 16)
            load_x(sp, PR, PR.x1, x_in)
            sp.dma_start(rowsin[0:24, :], a["state_conv"][0].rearrange("b j n -> (b j) n")).then_inc(rows_in, 16)
            sp.dma_start(rowsin[24:28, :], a["conv_w"][0]).then_inc(rows_in, 16)
            sp.dma_start(rowsin[28:29, :], a["conv_b"]).then_inc(rows_in, 16)
            sp.dma_start(normin[0:16, :], a["ssm_norm_w"][0].rearrange("(c p) -> c p", p=P)).then_inc(rows_in, 16)

            def wtile(w, at, n):
                cols = w[:, at:at + n] if isinstance(at, int) else w[:, ds(at, n)]
                return cols.rearrange("(k p) n -> p k n", p=P)

            w_in = a["w_in"][0]
            free = [None, None]

            def weights(q, name, ring, times, source, width=512, jobs=None):
                first, jobs = before[q.n, name][0 if ring is vb_filled else 1], jobs or q.nt

                def load(turn, b):
                    sp.dma_start(wbuf[b][:, :, 0:width], source(turn, b)).then_inc(w_in_sem[b], 16)

                for b in range(2):
                    if free[b] is not None:
                        sp.wait_ge(*free[b])
                    load(0, b)
                yield
                if times > 1:
                    with sp.Fori(1, times) as i:
                        for b in range(2):
                            sp.wait_ge(ring, i * (2 * jobs) + (first + jobs * (b - 1)))
                            load(i, b)
                for b in range(2):
                    free[b] = (ring, first + 2 * jobs * (times - 1) + jobs * (b + 1))
                yield

            def whole(*args, **kw):
                for _ in weights(*args, **kw):
                    pass

            for q in (PR, ST):
                if q.streams:
                    load_x(sp, q, q.x1, x_in)
                conv = weights(q, "conv", sb_filled, 4, lambda i, b: wtile(w_in, i * 768 + (O_XBC + 384 * b), 384), 384, 3)
                next(conv)
                if q.streams:
                    sp.wait_ge(sb_filled, before[1, "start"][1])
                    for v in range(KVH):
                        sp.dma_start(q.kc[:, v, :].rearrange("p (b n) -> p b n", b=DEC_B),
                                     a["cache_k"][0][:, :, v, :].rearrange("b s n -> s b n")).then_inc(cache_in, 16)
                    sp.dma_start(q.kc[:, 4, :].rearrange("p (b n) -> p b n", b=DEC_B),
                                 a["cache_kidx"][0].rearrange("b s n -> s b n")).then_inc(cache_in, 16)
                    sp.dma_start(q.vc, a["cache_v"][0].rearrange("b s v n -> s b (v n)")).then_inc(cache_in, 16)
                else:
                    sp.dma_start(cst[:, P:], a["table"][:, P:]).then_inc(const_in, 16)
                for _ in conv:
                    pass
                whole(q, "qkv", vb_filled, 2, lambda i, b: wtile(w_in, i * 1024 + 512 * b, 512))
                if not q.streams:
                    for b in range(2):
                        sp.wait_ge(*free[b])
                        sp.dma_start(wbuf[b], wtile(w_in, O_GATE + 1024 * b, 512)).then_inc(w_in_sem[b], 16)
                    at = before[0, "attention"][0]
                    free[:] = [(vb_filled, at), (vb_filled, at + EARLY)]
                whole(q, "ya", vb_filled, 1, lambda i, b: wtile(a["w_attn_br"][0], 512 * b, 512))
                if q.streams:
                    sp.wait_ge(sb_drained, SR + before[1, "attention"][1])
                    sp.dma_start(out["s_conv"][0].rearrange("b j n -> (b j) n"), q.tails[0:24, :]).then_inc(tails_out[1], 16)
                    store_kv(sp, q)
                z = weights(q, "z", sb_filled, 2, lambda i, b: wtile(w_in, i * 1024 + (O_Z + 512 * b), 512))
                next(z)
                if q.streams:
                    old = a["state_ssm"][0].rearrange("b (c h) q n -> c (h q) b n", h=2)
                    new = out["s_ssm"][0].rearrange("b (c h) q n -> c (h q) b n", h=2)
                    for c in range(18):
                        if c >= 2:
                            sp.wait_ge(new_ready, 2 * (c - 1))
                            sp.dma_start(new[c - 2], q.sst[c % 2]).then_inc(new_out[c % 2], 16)
                        if 2 <= c < 16:
                            sp.wait_ge(new_out[c % 2], 16 * (c // 2))
                        if c < 16:
                            sp.dma_start(q.sst[c % 2], old[c]).then_inc(old_in[c % 2], 16)
                    for b in range(2):
                        sp.wait_ge(new_out[b], 16 * 8)
                    sp.wait_ge(y_done, 3)
                    sp.dma_start(q.bg, a["b_gate"][0].partition_broadcast(P)).then_inc(bg_in[1], 16)
                    load_ln1(sp, q)
                for _ in z:
                    pass
                ym = weights(q, "ym", vb_filled, 2, lambda i, b: wtile(a["w_ssm_br"][0][D * b:D * (b + 1)], i * 512, 512))
                next(ym)
                if q.streams:
                    sp.wait_ge(sb_filled, before[1, "ym"][1])
                    load_x(sp, q, q.x2, x2_in[1])
                for _ in ym:
                    pass
                if q.streams:
                    whole(q, "gates", vb_filled, 2, lambda i, b: wtile(w_in, i * 512 + (O_GATE + 1024 * b), 512))
                else:
                    whole(q, "gates", vb_filled, 1, lambda i, b: wtile(w_in, 512 + O_GATE + 1024 * b, 512))
                whole(q, "out", vb_filled, 1, lambda i, b: wtile(a["w_out"][0], 512 * b, 512))
                free[0] = (vb_filled, before[q.n, "hT"][0] - 1)
                whole(q, "wq", sb_filled, 2, lambda i, b: wtile(a["peer_wq"][0], i * 1024 + 512 * b, 512))
            sp.wait_ge(y_out_ready, 3)
            sp.dma_start(out["y_sample"].rearrange("b s n -> (b s) n"), yout).then_inc(y_out, 16)
            sp.wait_ge(y_out, 16 * TILES)
            for n in range(2):
                sp.wait_ge(kv_out[n], 16 * (6, 3)[n])
                sp.wait_ge(tails_out[n], 16)

        @block.gpsimd
        def _(pool):
            own = Own(pool, pool_step)
            for i, name in enumerate(("dt_bias", "a_log", "d_skip")):
                pool.dma_start(headp[:, i * SH:(i + 1) * SH], a[name][0].partition_broadcast(P)).then_inc(par_in, 16)
            pool.dma_start(wdt, a["w_in"][0][:, O_DT:O_DT + SH].rearrange("(k p) n -> p k n", p=P)).then_inc(wdt_in, 16)
            pool.wait_ge(sb_drained, SR + before[0, "attention"][1])
            pool.dma_start(out["p_conv"][0, 0], PR.tails[0:3, :]).then_inc(tails_out[0], 16)
            store_kv(pool, PR)
            pool.wait_ge(sb_drained, SR + before[0, "z"][1])
            pool.dma_start(out["p_ssm"][0, 0].rearrange("(c h) q n -> (h q) c n", h=2),
                           PR.pso.rearrange("p (c n) -> p c n", c=16)).then_inc(pso_out, 16)
            pool.wait_ge(pso_out, 16)
            pool.wait_ge(y_done, 2)
            pool.dma_start(PR.bg, a["b_gate"][0].partition_broadcast(P)).then_inc(bg_in[0], 16)
            load_ln1(pool, PR)
            for i, name in enumerate(("ln2_g", "ln2_b")):
                pool.dma_start(ln2[:, i, :], a[name][0].partition_broadcast(P)).then_inc(ln2_in, 16)
            pool.dma_start(PR.keys[:, 0, :], a["peer_keys1"][0]).then_inc(keys_in, 16)
            pool.dma_start(PR.keys[:, 1, :], a["peer_keys2"][0]).then_inc(keys_in, 16)
            pool.wait_ge(sb_filled, before[0, "ym"][1])
            load_x(pool, PR, PR.x2, x2_in[0])

            table_u, table_v = a["peer_u"][0], a["peer_v"][0]
            want_u, want_v = pool.alloc_register("want_dots"), pool.alloc_register("want_used")
            pool.reg_mov(want_u, 1)
            pool.reg_mov(want_v, 1)
            pool.sem_inc(dot_done, SLOTS)
            pool.sem_inc(v_used, SLOTS)

            def gather_u(slot, j, idx, done=dot_done):
                pool.wait_ge(done, want_u)
                pool.reg_add(want_u, want_u, 1)
                pool.indirect_dma_start(slot, None, table_u, bass.IndirectOffsetOnAxis(ap=idx, axis=0)).then_inc(u_in[j], 16)

            def gather_v(slot, j, idx, used=v_used):
                pool.wait_ge(used, want_v)
                pool.reg_add(want_v, want_v, 1)
                pool.indirect_dma_start(slot, None, table_v, bass.IndirectOffsetOnAxis(ap=idx, axis=0)).then_inc(v_in[j], 16)

            def v_rows(g, b):
                for j in range(WB):
                    gather_v(vslot[b % 2 * WB + j], b % 2 * WB + j, islot[g][:, b * WB + j:b * WB + j + 1])

            def rows(g, at, with_v):
                own(pool.tensor_copy(islot[g], eidx[:, at:at + 4 * WB] if isinstance(at, int) else eidx[:, ds(at, 4 * WB)]))
                own.settle()
                for b in range(4):
                    for j in range(WB):
                        gather_u(uslot[b % 2 * WB + j], b % 2 * WB + j, islot[g][:, b * WB + j:b * WB + j + 1])
                    if with_v or b >= 2:
                        v_rows(g if b >= 2 else 1 - g, (b - 2) % 4)

            pool.wait_ge(idx_ready, 1)
            for g in range(2):
                rows(g, g * 4 * WB, g > 0)
            turn_rows = 2 * 4 * WB
            half_turns = P // 2 // turn_rows
            for n in range(4):
                first, times = (turn_rows, half_turns - 1) if n == 0 else (n * P // 2, half_turns)
                pool.wait_ge(idx_ready, n + 1)
                with loop(pool, times, (own.step, 2)) as i:
                    for g in range(2):
                        rows(g, i * turn_rows + (first + g * 4 * WB), True)
            for b in (2, 3):
                v_rows(1, b)
            pool.wait_ge(idx_ready, 5)
            pool.sem_inc(dot8_done, 2 * P + PB)
            pool.sem_inc(v8_used, 2 * P + PB)

            def rows8(b, at, slots):
                if slots[0] == 0:
                    own(pool.tensor_copy(islot8[b], eidx[:, at:at + PB] if isinstance(at, int) else eidx[:, ds(at, PB)]))
                    own.settle()
                for j in slots:
                    gather_u(uslot8[j], slot_sem[j], islot8[b][:, j:j + 1], dot8_done)
                for j in slots:
                    gather_v(vslot8[j], slot_sem[j], islot8[b][:, j:j + 1], v8_used)

            rows8(0, 2 * P, range(PB - SLOTS))
            pool.wait_ge(dot_done, SLOTS + 2 * P)
            pool.wait_ge(v_used, SLOTS + 2 * P)
            rows8(0, 2 * P, range(PB - SLOTS, PB))
            rows8(1, 2 * P + PB, range(PB))
            half_turns = P // PB // 4
            for first, times in ((2 * P + 2 * PB, half_turns - 1), (2 * P + P // 2, half_turns)):
                with loop(pool, times, (own.step, 2)) as i:
                    for b in range(2):
                        rows8(b, i * (2 * PB) + (first + b * PB), range(PB))
                pool.wait_ge(idx_ready, 6)

        @block.tensor
        def _(pe):
            vf, vd = Count(vb_filled), Count(vb_drained)
            sf, sd = Count(sb_filled), Count(sb_drained)
            loaded = [Count(s, step=16) for s in w_in_sem]
            mm = nc.tensor.matmul

            def expert_rows(dg, used, j, slots, landed):
                landed.take(pe) if isinstance(landed, Count) else pe.wait_ge(*landed)
                mm(acc[0][:, :], dg[:, j, :], slots[j][:, 0:512], start=False, stop=False, skip_group_check=True)
                mm(acc[1][:, :], dg[:, j, :], slots[j][:, 512:1024], start=False, stop=False,
                   skip_group_check=True).then_inc(used, 1)

            def open_sums(t):
                if t:
                    pe.wait_ge(acc_read, t)
                pe.wait_ge(ln2_in, 32)
                for n in range(2):
                    mm(acc[n][:, :], zero, ln2[:, 0, 0:512], start=True, stop=False, skip_group_check=True)

            def close_sums():
                for n in range(2):
                    last = mm(acc[n][:, :], zero, ln2[:, 0, 0:512], start=False, stop=True, skip_group_check=True)
                last.then_inc(acc_full, 1)

            def tick(k):
                b = k - 2
                if b in (0, BLOCKS):
                    open_sums(b // BLOCKS)
                if 0 <= b < PROMPT_BLOCKS:
                    pe.wait_ge(diag_ready, b + 1)
                    for j in range(b % 2 * WB, b % 2 * WB + WB):
                        expert_rows(diag, v_used, j, vslot, (v_in[j], 16 * (b // 2 + 1)))
                if b in (BLOCKS - 1, PROMPT_BLOCKS - 1):
                    close_sums()

            steps = Steps(tick)

            def vbank():
                vd.take(pe)
                return psum[vf.n % VR]

            def sbank():
                sd.take(pe)
                return psum[VR + sf.n % SR]

            def v_written():
                pe.wait_ge(vb_drained, VR + vf.n)

            def s_written():
                pe.wait_ge(sb_drained, SR + sf.n)

            def turn(dst, src, ids):
                return nc.tensor.transpose(dst, src, ids)

            def mixer(q):
                toks = {t: q.at(t) for t in q.tiles}
                L = {t: q.tiles.index(t) for t in q.tiles}
                step = steps.at if q.streams else (lambda place: None)

                def phase(name):
                    assert (vf.n, sf.n) == before[q.n, name], (name, vf.n, sf.n, before[q.n, name])

                def products(name, times, lhs, ring, drained, bank):
                    phase(name)
                    for _ in turns(pe, q.streams or times == 1, times, (ring, 2 * q.nt), (drained, 2 * q.nt),
                                   (loaded[0], 1), (loaded[1], 1)):
                        for b in range(2):
                            loaded[b].take(pe)
                            for t in q.tiles:
                                dst = bank()
                                for k in range(KC):
                                    last = mm(dst[:, :], lhs(b, k, toks[t]), wbuf[b][:, k, :],
                                              start=(k == 0), stop=(k == KC - 1))
                                ring.give(last)
                            step(name)

                def rows_to_T(src, t, quarter):
                    dst = sbank()
                    for i in range(4):
                        last = turn(dst[:, i * P:(i + 1) * P], src[:, (4 * quarter + i) * P:(4 * quarter + i + 1) * P], ident)
                    sf.give(last)

                phase("start")
                pe.wait_ge(const_in, 16)
                pe.wait_ge(x_in, 16 * (q.n + 1))
                for t in q.tiles:
                    for half in range(2):
                        dst = vbank()
                        for i in range(4):
                            last = turn(dst[:, i * P:(i + 1) * P], q.x1[:, L[t], (4 * half + i) * P:(4 * half + i + 1) * P], ident)
                        vf.give(last)
                if not q.streams:
                    pe.wait_ge(rows_in, 64)
                    for half in range(2):
                        dst = vbank()
                        for i in range(12):
                            last = turn(dst[:, i * ROWS:(i + 1) * ROWS],
                                        rowsin[0:ROWS, (12 * half + i) * P:(12 * half + i + 1) * P], ident[0:ROWS, 0:ROWS])
                        vf.give(last)
                    dst = vbank()
                    vf.give(turn(dst[:, 0:16], normin[0:16, :], ident[0:16, 0:16]))
                v_written()

                phase("conv")
                for turn_n in turns(pe, q.streams, 4, (sf, 6), (sd, 6), (loaded[0], 1), (loaded[1], 1)):
                    for b in range(2):
                        loaded[b].take(pe)
                        for j in range(3):
                            dst = sbank()
                            for k in range(KC):
                                last = mm(dst[:, 0:q.tok], wbuf[b][:, k, j * P:(j + 1) * P], q.xT[:, k, :],
                                          start=(k == 0), stop=(k == KC - 1))
                            sf.give(last)
                        if q.streams and turn_n >= 2:
                            if turn_n == 2 and b == 0:
                                pe.wait_ge(idx_ready, 1)
                            step("pick")
                if q.streams:
                    for _ in range(3 * PICK_STEPS - 4):
                        step("pick")
                    for _ in range(8):
                        step("conv")

                phase("dt")
                pe.wait_ge(wdt_in, 16)
                pe.wait_ge(const_in, 32)
                for t in q.tiles:
                    dst = sbank()
                    for k in range(KC):
                        last = mm(dst[:, 0:SH], q.xT[:, k, toks[t]], wdt[:, k, :], start=(k == 0), stop=(k == KC - 1))
                    sf.give(last)
                step("dt")

                def x_part(b, k, tok):
                    return q.xT[:, k, tok]

                products("qkv", 2, x_part, vf, vd, vbank)

                phase("tails")
                pe.wait_ge(tails_ready, q.n + 1)
                for c in range(6):
                    dst = sbank()
                    for i in range(4):
                        last = turn(dst[0:q.nrow, i * P:(i + 1) * P], q.tail[:, 4 * c + i, :], ident)
                    sf.give(last)
                step("tails")
                step("rope")

                def early_gates(b):
                    loaded[b].take(pe)
                    for t in q.tiles:
                        dst = vbank()
                        for k in range(KC):
                            last = mm(dst[:, :], q.xT[:, k, toks[t]], wbuf[b][:, k, :], start=(k == 0), stop=(k == KC - 1))
                        vf.give(last)

                phase("early")
                if not q.streams:
                    early_gates(0)

                phase("attention")
                pe.wait_ge(rope_done, q.n + 1)
                for t in q.tiles:
                    dst = sbank()
                    for v in range(KVH):
                        last = mm(dst[0:64, v * P:(v + 1) * P], q.qkv[:, L[t], O_K + v * HD:O_K + (v + 1) * HD], ident,
                                  start=True, stop=True)
                    sf.give(last)
                    dst = sbank()
                    sf.give(mm(dst[0:64, 0:P], q.qkv[:, L[t], O_KI:O_KI + HD], ident, start=True, stop=True))
                if q.streams:
                    pe.wait_ge(cache_in, 16 * 6)
                    for v in range(5):
                        dst = sbank()
                        for j in range(4):
                            last = turn(dst[:, j * P:(j + 1) * P], q.kc[:, v, j * P:(j + 1) * P], ident)
                        sf.give(last)
                s_written()
                step("keys")

                def turn_q(t, o):
                    dst = vbank()
                    for r in range(REP):
                        for half in range(2 if t == 2 else 1):
                            last = mm(dst[64 * half:64 * half + 64, r * P:(r + 1) * P],
                                      q.qkv[:, L[t], o + r * HD:o + (r + 1) * HD], ident, start=True, stop=True)
                    vf.give(last)

                def dot_keys(t, v):
                    for pr in range(2):
                        dst = vbank()
                        for r in (2 * pr, 2 * pr + 1):
                            o = (r % 2) * 256
                            if t < 2:
                                last = mm(dst[:, o:o + P * (t + 1)], q.qn[0:64, r, :], q.kT[0:64, v, 0:P * (t + 1)],
                                          start=True, stop=True)
                            else:
                                for j in range(4):
                                    mm(dst[:, o:o + P], q.qm[:, r, j, :], q.kcT[:, v, j, :], start=(j == 0), stop=(j == 3))
                                last = mm(dst[:, o + P:o + 2 * P], q.qn[0:64, r, :], q.kT[0:64, v, :],
                                          start=True, stop=True)
                        vf.give(last)

                def turn_probs(t, v):
                    n = t * KVH + v
                    pe.wait_ge(probs_ready, n + 1)
                    lm = q.lm[n % 2]
                    for half in range(2):
                        dst = sbank()
                        for r in range(REP):
                            if half == 0 or t > 0:
                                last = turn(dst[:, r * P:(r + 1) * P], lm[:, r, half * P:(half + 1) * P], ident)
                            elif r == 0:
                                last = turn(dst[:, 0:P], lm[:, 0, 0:P], ident)
                        sf.give(last)

                def times_values(t, v):
                    s_written()
                    dst = sbank()
                    for par in range(2):
                        o = dst[64 * par:64 * par + 64, 0:256]
                        vs = slice(O_V + v * HD, O_V + (v + 1) * HD)
                        if t < 2:
                            for half in range(t + 1):
                                last = mm(o, q.qkv[:, half, vs], q.PT[:, half, par::2, :],
                                          start=(half == 0), stop=(half == t))
                        else:
                            mm(o, q.qkv[:, 0, vs], q.PT[:, 1, par::2, :], start=True, stop=False, skip_group_check=True)
                            for b in range(DEC_B):
                                ob = o.rearrange("p (r t) -> p r t", r=2)[:, :, b * DEC_S:(b + 1) * DEC_S]
                                last = mm(ob, q.vc[:, b, v * HD:(v + 1) * HD], q.PT[:, 0, par::2, b * DEC_S:(b + 1) * DEC_S],
                                          start=False, stop=(b == DEC_B - 1), skip_group_check=True)
                    sf.give(last)

                items = attention_items(q)
                turn_q(items[0][0], O_QI)
                for m, (t, v) in enumerate(items):
                    last_kv = m > 0 and items[m - 1][1] < KVH
                    v_written()
                    dot_keys(t, v)
                    if v == KVH:
                        step("select")
                        step("select")
                    step("item1")
                    if last_kv:
                        turn_probs(*items[m - 1])
                    if m + 1 < len(items):
                        nt, nv = items[m + 1]
                        turn_q(nt, O_QI if nv == KVH else nv * REP * HD)
                    if m == 1 and not q.streams:
                        early_gates(1)
                        assert vf.n == before[0, "attention"][0] + EARLY
                    step("item2")
                    if last_kv:
                        times_values(*items[m - 1])
                    step("item3")
                turn_probs(*items[-1])
                times_values(*items[-1])
                s_written()

                products("ya", 1, lambda b, k, tok: q.attnT[:, k, tok], vf, vd, vbank)

                phase("ssd")
                pe.wait_ge(a_ready, q.n + 1)
                pe.wait_ge(silu_done, q.n + 1)
                for t in q.tiles:
                    dst = vbank()
                    at = L[t] * SH
                    mm(dst[:, 0:SH], tri[:, t // 2, :], q.av[:, at:at + SH], start=True, stop=True)
                    vf.give(mm(dst[:, SH:2 * SH], same[:, t // 2, :], q.av[:, at:at + SH], start=True, stop=True))
                for t in q.tiles:
                    tok = toks[t]
                    for c in range(5):
                        dst = sbank()
                        for i in range(4):
                            last = turn(dst[:, i * P:(i + 1) * P], q.xc[:, 4 * c + i, tok], ident)
                        sf.give(last)
                    if t == 2:
                        dst = sbank()
                        for hh in range(SH):
                            last = mm(dst[64 * (hh % 2):64 * (hh % 2) + 64, (hh // 2) * 8:(hh // 2) * 8 + 8],
                                      q.av[:, hh:hh + 1].to_broadcast([P, 64]), blk, start=True, stop=True)
                        sf.give(last)
                    s_written()
                    step("xbt")

                    def decays(g):
                        dst = vbank()
                        vf.give(mm(dst[:, 0:P], q.xc[:, 16 + g, tok], q.xc[:, 20 + g, tok], start=True, stop=True))
                        for half in range(2):
                            dst = vbank()
                            for i in range(4):
                                hh = L[t] * SH + g * 8 + half * 4 + i
                                last = mm(dst[:, i * P:(i + 1) * P], q.av[:, hh:hh + 1].to_broadcast([P, P]),
                                          tri[:, t // 2, :], start=True, stop=True)
                            vf.give(last)

                    if q.ahead:
                        decays(0)
                    for g in range(G):
                        CT = q.xc[:, 20 + g, tok]
                        if not q.ahead or g + 1 < G:
                            decays(g + q.ahead)
                        pe.wait_ge(seg_ready, t * G + g + 1)
                        Bg = q.xbt[:, DI + g * P:DI + (g + 1) * P]
                        step("seg")
                        if t == 2:
                            for c in range(4 * g, 4 * g + 4):
                                pe.wait_ge(old_in[c % 2], 16 * (c // 2 + 1))
                                for half in range(2):
                                    dst = sbank()
                                    for i in range(4):
                                        last = turn(dst[:, i * P:(i + 1) * P], q.sst[c % 2][:, 4 * half + i, :], ident)
                                    sf.give(last)
                                for half in range(2):
                                    dst = vbank()
                                    vf.give(mm(dst[:, :], q.xdtd[:, c * P:(c + 1) * P], q.Bm[:, 4 * half:4 * half + 4, :],
                                               start=True, stop=True))
                                step("state")
                            s_written()
                            step("group")
                        if t > 0:
                            dst = vbank()
                            if t == 1:
                                vf.give(mm(dst[:, :], CT, q.stateT[:, g * 512:(g + 1) * 512], start=True, stop=True))
                            else:
                                for b in range(DEC_B):
                                    last = mm(dst[:, :], q.CTm[:, b, :], q.pT[:, b, :], start=(b == 0), stop=(b == DEC_B - 1))
                                vf.give(last)
                        pe.wait_ge(mt_ready, t * G + g + 1)
                        dst = vbank()
                        for r in range(8):
                            last = mm(dst[:, r * HD:(r + 1) * HD], q.MT[g % len(q.MT)][:, r, :],
                                      q.xdt[:, g * 512 + r * HD:g * 512 + (r + 1) * HD], start=True, stop=True)
                        vf.give(last)
                        if t < 2:
                            dst = vbank()
                            vf.give(mm(dst[:, :], Bg, q.xdtd[:, g * 512:(g + 1) * 512], start=True, stop=True))
                        step("y")
                    if t == 1:
                        v_written()
                        for quarter in range(4):
                            rows_to_T(q.stateT, t, quarter)

                products("z", 2, x_part, sf, sd, sbank)
                phase("yT")
                for t in q.tiles:
                    pe.wait_ge(yn_ready, t + 1)
                    for quarter in range(4):
                        rows_to_T(q.y[:, L[t], :], t, quarter)
                s_written()
                step("yT")
                products("ym", 2, lambda b, k, tok: q.yTv[:, 8 * b + k, tok], vf, vd, vbank)
                products("gates", 2 if q.streams else 1, x_part, vf, vd, vbank)
                phase("mixedT")
                pe.wait_ge(mixed_ready, 2 * q.nt + 4 * q.n)
                for t in q.tiles:
                    for half in range(2):
                        rows_to_T(q.ya[:, L[t], :], t, half)
                s_written()
                step("mixedT")
                phase("out")
                for t in q.tiles:
                    for b in range(2):
                        if t == q.tiles[0]:
                            loaded[b].take(pe)
                        dst = vbank()
                        for k in range(KC):
                            last = mm(dst[:, :], q.xT[:, k, toks[t]], wbuf[b][:, k, :], start=(k == 0), stop=(k == KC - 1))
                        vf.give(last)
                        step("out")
                phase("hT")
                for t in q.tiles:
                    pe.wait_ge(h_ready, t + 1)
                    for half in range(2):
                        rows_to_T(htile(t), t, half)
                s_written()
                step("hT")
                products("wq", 2, x_part, sf, sd, sbank)
                phase("keysT")
                if not q.streams:
                    pe.wait_ge(keys_in, 32)
                    dst = sbank()
                    for i in range(2):
                        last = turn(dst[:, i * P:(i + 1) * P], q.keys[:, i, :], ident)
                    sf.give(last)
                phase("scores")
                s_written()
                for t in q.tiles:
                    for quarter in range(4):
                        rows_to_T(q.qp[:, L[t], :], t, quarter)
                    s_written()
                    for quarter in range(4):
                        dst = sbank() if t == 1 else vbank()
                        for i in range(4):
                            last = mm(dst[:, i * P:(i + 1) * P], q.qT[:, 4 * quarter + i, :], keysT[:, i % 2, :],
                                      start=True, stop=True)
                        (sf if t == 1 else vf).give(last)
                    step("scores")
                phase("end")

            mixer(PR)
            mixer(ST)
            places.append(steps.seen)
            steps.run(TICKS)
            dg = Count(diag_ready, start=PROMPT_BLOCKS)
            landed = [Count(v_in[s], start=2 * P // SLOTS if s < SLOTS else 0, step=16) for s in slot_sem]
            open_sums(2)
            with loop(pe, P // PB, (dg, 1), *((c, 1) for c in landed)):
                dg.take(pe)
                for j in range(PB):
                    expert_rows(diag8, v8_used, j, vslot8, landed[j])
            close_sums()

        @block.scalar
        def _(act):
            sf, sd = Count(sb_filled), Count(sb_drained, start=SR)
            act.sem_inc(sb_drained, SR)

            def bank():
                k = sf.n % SR
                sf.take(act)
                return psum[VR + k]

            def f(o, i, func=ACT.Copy, **kw):
                return nc.scalar.activation(o, i, func, **kw)

            def root(t, which, ready, done):
                mv, rs = norms[which][1:]
                act.wait_ge(ready, t + 1)
                f(rs[:, 0:1], mv[:, 1:2], ACT.Sqrt, bias=eps).then_inc(done, 1)

            def tick(k):
                if k in (BLOCKS + 2, PROMPT_BLOCKS + 2):
                    root(k // BLOCKS - 1, 1, var2_ready, root2_ready)
                if k in (BLOCKS + 3, PROMPT_BLOCKS + 3):
                    store_y(k // BLOCKS - 1)
                if 1 <= k <= PROMPT_BLOCKS:
                    act.wait_ge(w_ready, k)
                    act.wait_ge(v_used, WB * k)
                    for j in range(WB):
                        last = f(diag[:, (k - 1) % 2 * WB + j, :], ident, scale=w8[(k - 1) % 2][:, j:j + 1])
                    last.then_inc(diag_ready, 1)
                if k < PROMPT_BLOCKS:
                    act.wait_ge(dot_done, SLOTS + WB * (k + 1))
                    f(gl[k % 2], dots[k % 2], ACT.Gelu).then_inc(gelu_done, 1)

            steps = Steps(tick)

            def store_y(t):
                act.wait_ge(y_out_ready, t + 1)
                act.dma_start(out["y_prompt"][0][t * P:(t + 1) * P], yout).then_inc(y_out, 16)

            def exp_scores(n):
                act.wait_ge(score_e, n + 1)
                v = ts16[:, n % 2 * 4:n % 2 * 4 + 4, :]
                f(v, v, ACT.Exp).then_inc(score_v, 1)

            def mixer(q):
                step = steps.at if q.streams else (lambda place: None)
                L = {t: q.tiles.index(t) for t in q.tiles}
                for i in turns(act, q.streams, 4, (sf, 6), (sd, 6)):
                    for j in range(6):
                        src = bank()
                        o = i * (6 * q.raw) + j * q.raw
                        row = q.xraw2[:, o:o + q.raw] if q.streams else q.xraw2[:, ds(o, q.raw)]
                        if q.streams:
                            sd.give(f(row.rearrange("p (b s) -> p b s", b=DEC_B)[:, :, 3:SEG],
                                      src[:, 0:P].rearrange("p (b s) -> p b s", b=DEC_B)))
                        else:
                            sd.give(f(row[:, 3:3 + SEQ], src[:, 0:SEQ]))
                        if q.streams and i >= 2 and j % 3 == 2:
                            step("pick")
                    if q.streams and i == 1:
                        exp_scores(0)
                if q.streams:
                    for n in range(1, 4):
                        for _ in range(PICK_STEPS - (4 if n == 1 else 0)):
                            step("pick")
                        exp_scores(n)
                    for _ in range(8):
                        step("conv")
                for t in q.tiles:
                    src = bank()
                    sd.give(f(q.dtr[:, L[t] * SH:(L[t] + 1) * SH], src[:, 0:SH]))
                act.wait_ge(dt_v, 2 * q.n + 1)
                if not q.streams:
                    f(negA, headp[:, SH:2 * SH], ACT.Exp)
                f(q.dtu, q.dta, ACT.Exp, scale=-1.0).then_inc(dt_e, 1)
                act.wait_ge(dt_v, 2 * q.n + 2)
                f(q.dtw, q.dtw, ACT.Ln).then_inc(dt_e, 1)
                step("dt")
                for _ in range(4):
                    step("qkv")
                act.wait_ge(conv_done, CC * (q.n + 1))
                for c in range(6):
                    last = f(q.xc[:, 4 * c:4 * c + 4, :], q.xc[:, 4 * c:4 * c + 4, :], ACT.Silu)
                last.then_inc(silu_done, 1)
                for c in range(6):
                    src = bank()
                    sd.give(f(q.tails[0:q.nrow, c * 512:(c + 1) * 512], src[0:q.nrow, :]))
                step("tails")
                step("rope")

                for t in q.tiles:
                    src = bank()
                    tok = q.at(t)
                    sd.give(f(q.kT[0:64, 0:4, tok], src[0:64, :].rearrange("p (v s) -> p v s", v=4)))
                    src = bank()
                    sd.give(f(q.kT[0:64, 4, tok], src[0:64, 0:P]))
                if q.streams:
                    for v in range(5):
                        src = bank()
                        sd.give(f(q.kcT[:, v, :, :], src[:, :].rearrange("p (j s) -> p j s", j=4)))
                step("keys")

                def exps(n):
                    act.wait_ge(max_ready, n + 1)
                    S = P if n < KVH else 2 * P
                    for r in range(REP):
                        o = 4 * (n % 2) + r
                        v = q.lm[n % 2][:, r, 0:S]
                        last = f(v, v, ACT.Exp, scale=LOG_SCALE, bias=nmx[:, o:o + 1], accum_out=sums[:, o:o + 1])
                    last.then_inc(exp_done, 1)

                def keep_probs(t, v):
                    for half in range(2):
                        src = bank()
                        if half == 0 or t > 0:
                            sd.give(f(q.PT[:, half, :, :], src[:, :].rearrange("p (r s) -> p r s", r=REP)))
                        else:
                            sd.give(f(q.PT[:, 1, 0, :], src[:, 0:P]))

                def keep_heads(t, v):
                    if v == 0 and t != 1:
                        act.wait_ge(tails_out[q.n], 16)
                    src = bank()
                    sd.give(f(q.attnT[:, 2 * v:2 * v + 2, q.at(t)], src[:, 0:256].rearrange("p (r s) -> p r s", r=2)))

                items = attention_items(q)
                for m, (t, v) in enumerate(items):
                    last_kv = m > 0 and items[m - 1][1] < KVH
                    if v == KVH:
                        step("select")
                        step("select")
                    step("item1")
                    if last_kv:
                        keep_probs(*items[m - 1])
                    if v < KVH:
                        exps(t * KVH + v)
                    step("item2")
                    if last_kv:
                        keep_heads(*items[m - 1])
                    step("item3")
                keep_probs(*items[-1])
                keep_heads(*items[-1])
                for _ in range(2):
                    step("ya")

                act.wait_ge(sum_ready, q.n + 1)
                f(q.ex[:, :, 0:2 * SH], q.acs, ACT.Exp)
                f(q.ex[:, :, 2 * SH:3 * SH], q.ex[:, :, 2 * SH:3 * SH], ACT.Exp).then_inc(ex_ready, 1)
                for t in q.tiles:
                    if t == 1:
                        act.wait_ge(y_done, t)
                    else:
                        act.wait_ge(vb_filled, before[q.n, "ssd"][0])
                    for c in range(5):
                        src = bank()
                        sd.give(f(q.xbt[:, c * 512:(c + 1) * 512], src[:, :]))
                    if t == 2:
                        src = bank()
                        sd.give(f(dec.rearrange("p c b -> p (c b)"), src[:, 0:P], ACT.Exp))
                    step("xbt")
                    for g in range(G):
                        act.wait_ge(seg_ready, t * G + g + 1)
                        MT = q.MT[g % len(q.MT)]
                        f(MT, MT, ACT.Exp).then_inc(seg_exp, 1)
                        step("seg")
                        if t == 2:
                            for c in range(4):
                                for half in range(2):
                                    src = bank()
                                    sd.give(f(q.pT[:, 4 * half:4 * half + 4, c * P:(c + 1) * P],
                                              src[:, :].rearrange("p (b s) -> p b s", b=4)))
                                step("state")
                            step("group")
                        step("y")
                    if t == 1:
                        for quarter in range(4):
                            src = bank()
                            sd.give(f(q.pso[:, quarter * 512:(quarter + 1) * 512], src[:, :]))

                act.wait_ge(y_done, q.tiles[-1] + 1)
                g0 = q.n * (1 + 4 * PR.nt)
                for i in turns(act, q.streams, 2, (sf, 2 * q.nt), (sd, 2 * q.nt)):
                    act.wait_ge(gated, i * (2 * q.nt) + (g0 + 1))
                    for j in range(2 * q.nt):
                        src = bank()
                        sd.give(f(q.zs[:, j, :], src[:, :], ACT.Silu))
                        if j % q.nt == q.nt - 1:
                            step("z")
                act.wait_ge(ms_ready, q.n + 1)
                f(rstd, ms, ACT.Sqrt, scale=1.0 / 512, bias=eps).then_inc(rms_root, 1)
                for t in q.tiles:
                    for quarter in range(4):
                        src = bank()
                        for i in range(4):
                            c = 4 * quarter + i
                            last = f(q.yTv[:, c, q.at(t)], src[:, i * P:(i + 1) * P], scale=normT[:, c:c + 1])
                        sd.give(last)
                step("yT")
                for _ in range(4):
                    step("ym")
                pre = Count(gate_pre, start=q.n * 4 * PR.nt)
                for i in range(2):
                    for j in range(2 * q.nt):
                        pre.take(act)
                        f(q.gt[:, j, :], q.gt[:, j, :], ACT.Sigmoid).then_inc(gate_ready, 1)
                        if j % q.nt == q.nt - 1:
                            step("gates")

                def keep_T(t, half):
                    src = bank()
                    sd.give(f(q.xT[:, 4 * half:4 * half + 4, q.at(t)], src[:, :].rearrange("p (k s) -> p k s", k=4)))

                for t in q.tiles:
                    for half in range(2):
                        keep_T(t, half)
                step("mixedT")
                for _ in range(2):
                    step("out")
                for t in q.tiles:
                    root(t, 0, var1_ready, root1_ready)
                for t in q.tiles:
                    for half in range(2):
                        keep_T(t, half)
                step("hT")
                act.wait_ge(h_ready, q.tiles[-1] + 1)
                for i in turns(act, q.streams, 2, (sf, 2 * q.nt), (sd, 2 * q.nt)):
                    for b in range(2):
                        for k in range(q.nt):
                            src = bank()
                            o = i * 1024 + (k * 2048 + b * 512)
                            sd.give(f(q.YD[:, o:o + 512] if q.streams else q.YD[:, ds(o, 512)], src[:, :]))
                        step("wq")
                if not q.streams:
                    src = bank()
                    sd.give(f(keysT, src[:, 0:256].rearrange("p (a n) -> p a n", a=2)))
                for t in q.tiles:
                    for quarter in range(4):
                        src = bank()
                        sd.give(f(q.qT[:, 4 * quarter:4 * quarter + 4, :], src[:, :].rearrange("p (c s) -> p c s", c=4)))
                    if t == 1:
                        for quarter in range(4):
                            src = bank()
                            sd.give(f(sc[1][:, quarter * 512:(quarter + 1) * 512], src[:, :]))
                    step("scores")

            mixer(PR)
            mixer(ST)
            places.append(list(steps.seen))
            for n in (4, 5):
                for _ in range(PICK_STEPS):
                    steps.at("pick")
                exp_scores(n)
            steps.run(TICKS)
            store_y(1)
            dots_c, w_c, vu = Count(dot8_done, start=2 * P + PB), Count(w_ready, start=PROMPT_BLOCKS), Count(v8_used, start=2 * P)
            with loop(act, P // PB, (dots_c, PB), (w_c, 1), (vu, PB)):
                dots_c.n += PB - 1
                dots_c.take(act)
                f(gl8, dots8, ACT.Gelu).then_inc(gelu_done, 1)
                w_c.take(act)
                vu.n += PB - 1
                vu.take(act)
                for j in range(PB):
                    last = f(diag8[:, j, :], ident, scale=w88[:, j:j + 1])
                last.then_inc(diag_ready, 1)
            root(2, 1, var2_ready, root2_ready)

        @block.vector
        def _(dve):
            own = Own(dve, dve_step)
            vf, vd = Count(vb_filled), Count(vb_drained, start=VR)
            dve.sem_inc(vb_drained, VR)
            tt, tsc, stt = nc.vector.tensor_tensor, nc.vector.tensor_scalar, nc.vector.scalar_tensor_tensor
            cp = nc.vector.tensor_copy

            def bank():
                k = vf.n % VR
                vf.take(dve)
                return psum[k]

            def bc(ap, shape):
                return ap.to_broadcast([P] + list(shape))

            def layer_norm(v, o, t, which, g, b, ready, done, final):
                bns, mv, rs = norms[which]
                for half in range(2):
                    own(nc.vector.bn_stats(bns[:, 6 * half:6 * half + 6], v[:, half * 512:(half + 1) * 512]))
                own.settle()
                own(nc.vector.bn_aggr(mv, bns))
                own.settle()
                dve.sem_inc(ready, 1)
                dve.wait_ge(done, t + 1)
                own(nc.vector.reciprocal(rs[:, 1:2], rs[:, 0:1]))
                own.settle()
                own(tsc(v, v, mv[:, 0:1], rs[:, 1:2], ALU.subtract, ALU.mult))
                own.settle()
                own(tt(v, v, g, ALU.mult))
                own.settle()
                tt(o, v, b, ALU.add).then_inc(final, 1)

            def finish(t):
                dve.wait_ge(acc_full, t + 1)
                hv = htile(t)
                for n in range(2):
                    c = slice(n * 512, (n + 1) * 512)
                    own(stt(hv[:, c], hv[:, c], ALPHA, acc[n][:, :], ALU.mult, ALU.add))
                own.settle()
                dve.sem_inc(acc_read, 1)
                if t:
                    dve.wait_ge(y_out, 16 * t)
                layer_norm(hv, yout, t, 1, ln2[:, 0, :], ln2[:, 1, :], var2_ready, root2_ready, y_out_ready)

            def tick(k):
                if k in (BLOCKS + 2, PROMPT_BLOCKS + 2):
                    finish(k // BLOCKS - 1)
                if 1 <= k <= PROMPT_BLOCKS:
                    dve.wait_ge(gelu_done, k)
                    tt(w8[(k - 1) % 2], gl[(k - 1) % 2], gate[:, (k - 1) * WB:k * WB], ALU.mult).then_inc(w_ready, 1)
                if k < PROMPT_BLOCKS:
                    for j in range(WB):
                        slot = k % 2 * WB + j
                        dve.wait_ge(u_in[slot], 16 * (k // 2 + 1))
                        nc.vector.tensor_tensor_reduce(uslot[slot], uslot[slot], htile(k // BLOCKS), 1.0, 0.0, ALU.mult,
                                                       ALU.add, dots[k % 2][:, j:j + 1]).then_inc(dot_done, 1)

            steps = Steps(tick)

            def mixer(q):
                step = steps.at if q.streams else (lambda place: None)
                L = {t: q.tiles.index(t) for t in q.tiles}
                nt = q.nt
                def x_to_T():
                    for t in q.tiles:
                        for half in range(2):
                            src = bank()
                            vd.give(cp(q.xT[:, 4 * half:4 * half + 4, q.at(t)], src[:, :].rearrange("p (k s) -> p k s", k=4)))

                def start_streams(place):
                    if place == 1:
                        x_to_T()
                        own(cp(q.xraw.rearrange("p c (b s) -> p c b s", b=DEC_B)[:, :, :, 0:3],
                               rowsT[:, :, 0:24].rearrange("p c (b j) -> p c b j", b=DEC_B)))
                        own.settle()

                if not q.streams:
                    x_to_T()
                    for half in range(2):
                        src = bank()
                        own(cp(rowsT[:, 12 * half:12 * half + 12, :], src[:, 0:12 * ROWS].rearrange("p (c r) -> p c r", c=12)), vd)
                    src = bank()
                    own(cp(normT[:, :], src[:, 0:16]), vd)
                    own.settle()
                    own(nc.vector.memset(q.xraw[:, :, 0:3], 0.0))
                    own.settle()
                else:
                    pick(0, 0, start_streams)
                    pick(0, 1, lambda place: steps.at("pick"))
                    dve.wait_ge(sb_drained, SR + before[1, "start"][1])
                    for half in range(2):
                        pick(1, half, lambda place: steps.at("pick"))

                arrived = Count(sb_drained, start=SR + before[q.n, "conv"][1])
                conv_c = Count(conv_done, start=CC * q.n)
                for i in turns(dve, q.streams, 4, (own.step, 6 * 3), (arrived, 6), (conv_c, 6)):
                    for j in range(6):
                        arrived.take(dve)
                        o = i * (6 * q.raw) + j * q.raw
                        row = q.xraw2[:, o:o + q.raw] if q.streams else q.xraw2[:, ds(o, q.raw)]
                        o = i * (6 * q.tok) + j * q.tok
                        res = q.C[:, o:o + q.tok] if q.streams else q.C[:, ds(o, q.tok)]
                        o = i * (6 * ROWS) + j * ROWS
                        wr = rowsT.rearrange("p c r -> p (c r)")
                        wr = wr[:, o:o + ROWS] if q.streams else wr[:, ds(o, ROWS)]
                        if q.streams:
                            res = res.rearrange("p (b s) -> p b s", b=DEC_B)
                            row = row.rearrange("p (b s) -> p b s", b=DEC_B)
                        taps = [row[:, :, k:k + DEC_S] if q.streams else row[:, k:k + SEQ] for k in range(CW)]
                        own(tsc(res, taps[0], wr[:, 24:25], wr[:, 28:29], ALU.mult, ALU.add))
                        own.settle()
                        for k in range(1, CW - 1):
                            own(stt(res, taps[k], wr[:, 24 + k:25 + k], res, ALU.mult, ALU.add))
                            own.settle()
                        conv_c.give(stt(res, taps[3], wr[:, 27:28], res, ALU.mult, ALU.add))
                        if j % 3 == 2:
                            step("conv")
                if q.streams:
                    o, i = (q.tail.rearrange("p c (b j) -> p c b j", b=DEC_B),
                            q.xraw.rearrange("p c (b s) -> p c b s", b=DEC_B)[:, :, :, DEC_S:SEG])
                else:
                    o, i = q.tail, q.xraw[:, :, SEQ:SEQ + 3]
                cp(o, i).then_inc(tails_ready, 1)

                dve.wait_ge(par_in, 48)
                dve.wait_ge(sb_drained, SR + before[q.n, "dt"][1] + nt)
                t3 = [nt, SH]
                dtr, dta, dtu, dtw, dtv = q.dtr, q.dta, q.dtu, q.dtw, q.dtv

                def by_tile(v):
                    return v.rearrange("p (t n) -> p t n", t=nt)

                own(tt(by_tile(dtr), by_tile(dtr), bc(headp[:, 0:SH].unsqueeze(1), t3), ALU.add))
                own.settle()
                own(tsc(dta, dtr, -1.0, None, ALU.mult))
                own.settle()
                tt(dta, dta, dtr, ALU.max).then_inc(dt_v, 1)
                dve.wait_ge(dt_e, 2 * q.n + 1)
                tsc(dtw, dtu, 1.0, None, ALU.add).then_inc(dt_v, 1)
                own(tsc(dtv, dtu, 1.0, -1.0, ALU.add, ALU.add))
                dve.wait_ge(dt_e, 2 * q.n + 2)
                own.settle()
                own(tsc(dta, dtv, 0.0, None, ALU.is_equal))
                own.settle()
                own(tt(dtv, dtv, dta, ALU.add))
                own(tt(dtw, dtw, dta, ALU.add))
                own.settle()
                own(nc.vector.reciprocal(dtv, dtv))
                own.settle()
                own(tt(dtw, dtw, dtu, ALU.mult))
                own.settle()
                own(tt(dtv, dtv, dtw, ALU.mult))
                own.settle()
                own(stt(dtv, dtr, 0.0, dtv, ALU.max, ALU.add))
                if not q.streams:
                    own(tsc(negA, negA, -1.0, None, ALU.mult))
                own.settle()
                tt(by_tile(q.av), by_tile(dtv), bc(negA.unsqueeze(1), t3), ALU.mult).then_inc(a_ready, 1)

                step("dt")

                for i in turns(dve, q.streams, 2, (vf, 2 * nt), (vd, 2 * nt)):
                    for b in range(2):
                        for k in range(nt):
                            src = bank()
                            o = i * 1024 + (k * 2048 + b * 512)
                            vd.give(cp(q.B[:, o:o + 512] if q.streams else q.B[:, ds(o, 512)], src[:, :]))
                        step("qkv")
                vd.upto(dve)

                def rope(o, heads):
                    v = {t: q.qkv[:, L[t], o:o + heads * HD].rearrange("p (h n) -> p h n", h=heads) for t in q.tiles}
                    T = [x[:, 0:nt * heads * 8].rearrange("p (t h n) -> p t h n", t=nt, h=heads) for x in q.rtmp]
                    for t in q.tiles:
                        c, s = bc(cos[:, t, :].unsqueeze(1), [heads, 8]), bc(sin[:, t, :].unsqueeze(1), [heads, 8])
                        own(tt(T[0][:, L[t]], v[t][:, :, 0:8], c, ALU.mult))
                        own(tt(T[1][:, L[t]], v[t][:, :, 8:16], s, ALU.mult))
                        own(tt(T[2][:, L[t]], v[t][:, :, 8:16], c, ALU.mult))
                        own(tt(T[3][:, L[t]], v[t][:, :, 0:8], s, ALU.mult))
                    own.settle()
                    for t in q.tiles:
                        own(tt(v[t][:, :, 0:8], T[0][:, L[t]], T[1][:, L[t]], ALU.subtract))
                        own(tt(v[t][:, :, 8:16], T[2][:, L[t]], T[3][:, L[t]], ALU.add))
                    own.settle()

                step("tails")
                dve.wait_ge(sb_filled, before[q.n, "attention"][1])
                rope(0, HEADS + KVH)
                rope(O_QI, IH + 1)
                dve.sem_inc(rope_done, 1)

                def early_gates(b):
                    for k in range(nt):
                        src = bank()
                        vd.give(cp(q.gx[:, nt * b + k, :], src[:, :]))

                if not q.streams:
                    early_gates(0)
                step("rope")
                step("keys")

                def keep_q(t):
                    src = bank()
                    v = src[:, :].rearrange("p (r s) -> p r s", r=REP)
                    if t < 2:
                        vd.give(cp(q.qn[0:64, :, :], v[0:64]))
                    else:
                        cp(q.qn[0:64, :, :], v[0:64])
                        for r in range(REP):
                            last = tt(q.qm[:, r, :, :], bc(v[:, r, :].unsqueeze(1), [4, P]), pair, ALU.mult)
                        vd.give(last)

                def widths(t):
                    return P if t == 0 else 2 * P

                def index_scores(t):
                    S = widths(t)
                    s, tmp = q.score[L[t]][:, 0:S], q.scoret[:, 0:S]
                    for pr in range(2):
                        src = bank()
                        for r in range(2):
                            hh = 2 * pr + r
                            wi = q.qkv[:, L[t], O_WI + hh:O_WI + hh + 1]
                            o = s if hh == 0 else tmp
                            own(tsc(o, src[:, r * 256:r * 256 + S], 0.0, wi, ALU.max, ALU.mult), vd if r == 1 else None)
                            own.settle()
                            if hh:
                                own(tt(s, s, tmp, ALU.add))
                                own.settle()
                    own(tt(s, s, adm[:, t, 0:S], ALU.mult))
                    own.settle()
                    own(tt(s, s, nadm[:, t, 0:S], ALU.add))
                    own.settle()

                def select():
                    rows = [(q.score[k][:, 0:widths(t)], q.negm[k][:, 0:widths(t)], m8[:, 8 * k:8 * k + 8])
                            for k, t in enumerate(q.tiles)]
                    step("select")
                    k = TOPK_S if q.streams else TOPK_P
                    while k > 0:
                        for s, _, best in rows:
                            own(nc.vector.max(best, s))
                        own.settle()
                        if k < 8:
                            for _, _, best in rows:
                                own(nc.vector.memset(best[:, k:8], GONE))
                            own.settle()
                        for s, _, best in rows:
                            own(nc.vector.match_replace(s, best, s, GONE))
                        own.settle()
                        k -= 8
                        if 8 < k <= 16:
                            step("select")
                    for s, neg, _ in rows:
                        own(tsc(neg, s, GONE, NEG, ALU.not_equal, ALU.mult))
                    own.settle()

                first_s = before[q.n, "attention"][1] + 2 * nt + 5 * q.streams

                def logits(n):
                    S = P if n < KVH else 2 * P
                    k = n - q.tiles[0] * KVH
                    if k >= 2:
                        dve.wait_ge(sb_filled, first_s + 3 * (k - 2) + 2)
                    lm = q.lm[n % 2]
                    for pr in range(2):
                        src = bank()
                        own(tt(lm[:, 2 * pr:2 * pr + 2, 0:S], src[:, :].rearrange("p (r s) -> p r s", r=2)[:, :, 0:S],
                               bc(q.negm[L[n // KVH]][:, 0:S].unsqueeze(1), [2, S]), ALU.add), vd)
                    own.settle()
                    o = 4 * (n % 2)
                    own(nc.vector.tensor_reduce(nmx[:, o:o + 4], lm[:, :, 0:S], AX_X, ALU.max))
                    own.settle()
                    tsc(nmx[:, o:o + 4], nmx[:, o:o + 4], -LOG_SCALE, None, ALU.mult).then_inc(max_ready, 1)

                def normalise(n):
                    S = P if n < KVH else 2 * P
                    o = 4 * (n % 2)
                    dve.wait_ge(exp_done, n + 1)
                    own(nc.vector.reciprocal(rec[:, o:o + 4], sums[:, o:o + 4]))
                    own.settle()
                    lm = q.lm[n % 2]
                    tt(lm[:, :, 0:S], lm[:, :, 0:S], bc(rec[:, o:o + 4].unsqueeze(2), [REP, S]), ALU.mult).then_inc(probs_ready, 1)

                if q.streams:
                    dve.wait_ge(cache_in, 16 * 6)
                items = attention_items(q)
                keep_q(items[0][0])
                for m, (t, v) in enumerate(items):
                    if v == KVH:
                        index_scores(t)
                        if t == q.tiles[-1]:
                            select()
                    else:
                        logits(t * KVH + v)
                    step("item1")
                    if m + 1 < len(items):
                        keep_q(items[m + 1][0])
                    if m == 1 and not q.streams:
                        early_gates(1)
                    step("item2")
                    if v < KVH:
                        normalise(t * KVH + v)
                    step("item3")
                for b in range(2):
                    for k in range(nt):
                        src = bank()
                        vd.give(cp(q.ya[:, k, b * 512:(b + 1) * 512], src[:, :]))
                    step("ya")

                for t in q.tiles:
                    src = bank()
                    own(cp(q.acs[:, L[t], :], src[:, 0:64]), vd)
                own.settle()
                tt(q.ex[:, :, 2 * SH:3 * SH], q.acs[:, :, SH:2 * SH], q.acs[:, :, 0:SH], ALU.subtract).then_inc(sum_ready, 1)
                dve.wait_ge(ex_ready, q.n + 1)
                dve.wait_ge(kv_out[q.n], 16 * 3 * nt)
                for t in q.tiles:
                    dve.wait_ge(sb_drained, SR + before[q.n, "ssd"][1] + 5 * (L[t] + 1) + (t == 2))
                    step("xbt")
                    xs = q.xbt[:, 0:DI].rearrange("p (h n) -> p h n", h=SH)
                    at = L[t] * SH
                    own(tt(q.xdt.rearrange("p (h n) -> p h n", h=SH), xs, bc(dtv[:, at:at + SH].unsqueeze(2), [SH, HD]), ALU.mult))
                    own.settle()
                    own(tt(q.xdtd.rearrange("p (h n) -> p h n", h=SH), q.xdt.rearrange("p (h n) -> p h n", h=SH),
                           bc(q.ex[:, L[t], 2 * SH:3 * SH].unsqueeze(2), [SH, HD]), ALU.mult))

                    def decays(g):
                        src = bank()
                        own(tt(q.cbm[g % len(q.MT)], src[:, 0:P], tri[:, t // 2, :], ALU.mult), vd)
                        for half in range(2):
                            src = bank()
                            for i in range(4):
                                hh = g * 8 + half * 4 + i
                                own(tsc(q.MT[g % len(q.MT)][:, half * 4 + i, :], src[:, i * P:(i + 1) * P],
                                        q.acs[:, L[t], hh:hh + 1], 0.0, ALU.subtract, ALU.min), vd if i == 3 else None)
                        if t == 2:
                            own(tt(q.CTm, bc(q.xc[:, 20 + g, :].unsqueeze(1), [DEC_B, P]), blkcol, ALU.mult))
                            own(tt(q.Bm, bc(q.xbt[:, DI + g * P:DI + (g + 1) * P].unsqueeze(1), [DEC_B, P]),
                                   bc(blk.unsqueeze(2), [DEC_B, P]), ALU.mult))
                        own.settle()
                        dve.sem_inc(seg_ready, 1)

                    if q.ahead:
                        decays(0)
                    for g in range(G):
                        if not q.ahead:
                            decays(g)
                        step("seg")
                        dve.wait_ge(seg_exp, t * G + g + 1)
                        MT, cbm = q.MT[g % len(q.MT)], q.cbm[g % len(q.MT)]
                        tt(MT, MT, bc(cbm.unsqueeze(1), [8, P]), ALU.mult).then_inc(mt_ready, 1)
                        if q.ahead and g + 1 < G:
                            decays(g + 1)
                        if t == 2:
                            for c in range(4 * g, 4 * g + 4):
                                for half in range(2):
                                    src = bank()
                                    for b in range(4):
                                        bb = 4 * half + b
                                        sv = q.sst[c % 2][:, bb, :]
                                        last = stt(sv, sv, dec[:, c, bb:bb + 1], src[:, b * P:(b + 1) * P], ALU.mult, ALU.add)
                                    own(last, vd)
                                    own.settle()
                                    dve.sem_inc(new_ready, 1)
                                step("state")
                            step("group")
                        yg = q.y[:, L[t], g * 512:(g + 1) * 512]
                        y3 = yg.rearrange("p (r n) -> p r n", r=8)
                        hs = slice(g * 8, g * 8 + 8)
                        dsk = headp[:, 2 * SH + g * 8:2 * SH + g * 8 + 8]
                        own(tt(y3, xs[:, hs, :], bc(dsk.unsqueeze(2), [8, HD]), ALU.mult))
                        own.settle()
                        if t > 0:
                            src = bank()
                            own(tt(q.ytmp.rearrange("p (r n) -> p r n", r=8), src[:, :].rearrange("p (r n) -> p r n", r=8),
                                   bc(q.ex[:, L[t], hs].unsqueeze(2), [8, HD]), ALU.mult), vd)
                            own.settle()
                            own(tt(yg, yg, q.ytmp, ALU.add))
                            own.settle()
                        src = bank()
                        own(tt(yg, yg, src[:, :], ALU.add), vd)
                        if t < 2:
                            src = bank()
                            st = q.stateT[:, g * 512:(g + 1) * 512]
                            if t == 0:
                                own(cp(st, src[:, :]), vd)
                            else:
                                s3 = st.rearrange("p (r n) -> p r n", r=8)
                                own(tt(s3, s3, bc(q.ex[:, 1, SH + g * 8:SH + g * 8 + 8].unsqueeze(2), [8, HD]), ALU.mult))
                                own.settle()
                                own(tt(st, st, src[:, :], ALU.add), vd)
                        step("y")
                    own.settle()
                    dve.sem_inc(y_done, 1)

                dve.sem_inc(gated, 1)
                g0 = q.n * (1 + 4 * PR.nt)
                zin, gated_c = Count(sb_drained, start=SR + before[q.n, "z"][1]), Count(gated, start=g0 + 1)
                for i in range(2):
                    for j in range(2 * nt):
                        zin.take(dve)
                        k, g = j % nt, 2 * i + j // nt
                        yg = q.y[:, k, g * 512:(g + 1) * 512]
                        gated_c.give(tt(yg, yg, q.zs[:, j, :], ALU.mult))
                        gated_c.upto(dve)
                        own(nc.vector.tensor_tensor_reduce(q.gt[:, j, :], yg, yg, 1.0, 0.0, ALU.mult, ALU.add,
                                                           ms[:, k * G + g:k * G + g + 1]))
                        if k == nt - 1:
                            step("z")
                own.settle()
                dve.sem_inc(ms_ready, 1)
                dve.wait_ge(rms_root, q.n + 1)
                own(nc.vector.reciprocal(rstd, rstd))
                own.settle()
                for k in range(nt):
                    y4 = q.y[:, k, :].rearrange("p (g n) -> p g n", g=G)
                    tt(y4, y4, bc(rstd[:, k * G:(k + 1) * G].unsqueeze(2), [G, 512]), ALU.mult).then_inc(yn_ready, 1)
                step("yT")

                for i in turns(dve, q.streams, 2, (vf, 2 * nt), (vd, 2 * nt)):
                    for b in range(2):
                        for k in range(nt):
                            src = bank()
                            o = i * 512 + (nt * D + k * D)
                            v = q.YD[:, o:o + 512] if q.streams else q.YD[:, ds(o, 512)]
                            if b == 0:
                                vd.give(cp(v, src[:, :]))
                            else:
                                if k == 0:
                                    vd.upto(dve)
                                vd.give(tt(v, v, src[:, :], ALU.add))
                        step("ym")
                vd.upto(dve)

                dve.wait_ge(bg_in[q.n], 16)
                mixed_c = Count(mixed_ready, start=q.n * 2 * PR.nt)
                gr, gp = Count(gate_ready, start=q.n * 4 * PR.nt), Count(gate_pre, start=q.n * 4 * PR.nt)
                for i in range(2):
                    c = slice(i * 512, i * 512 + 512)
                    for b in range(2):
                        for k in range(nt):
                            bias = q.bg[:, b * 1024 + i * 512:b * 1024 + i * 512 + 512]
                            if i == 0 and not q.streams:
                                own(tt(q.gt[:, nt * b + k, :], q.gx[:, nt * b + k, :], bias, ALU.add))
                            else:
                                src = bank()
                                own(tt(q.gt[:, nt * b + k, :], src[:, :], bias, ALU.add), vd)
                        own.settle()
                        dve.sem_inc(gate_pre, nt)
                        gp.n += nt
                        step("gates")
                    for k in range(nt):
                        gr.take(dve)
                        own(tt(q.ya[:, k, c], q.ya[:, k, c], q.gt[:, k, :], ALU.mult))
                    for k in range(nt):
                        gr.take(dve)
                        own(tt(q.gt[:, nt + k, :], q.gt[:, nt + k, :], q.ym[:, k, c], ALU.mult))
                    own.settle()
                    for k in range(nt):
                        mixed_c.give(tt(q.ya[:, k, c], q.ya[:, k, c], q.gt[:, nt + k, :], ALU.add))
                step("mixedT")

                dve.wait_ge(x2_in[q.n], 16)
                dve.wait_ge(ln1_in[q.n], 32)
                for t in q.tiles:
                    for b in range(2):
                        src = bank()
                        c = slice(b * 512, (b + 1) * 512)
                        own(stt(htile(t)[:, c], q.x2[:, L[t], c], ALPHA, src[:, :], ALU.mult, ALU.add), vd)
                        step("out")
                    own.settle()
                    layer_norm(htile(t), htile(t), t, 0, q.ln1[:, 0, :], q.ln1[:, 1, :], var1_ready, root1_ready, h_ready)
                step("hT")
                for _ in range(4):
                    step("wq")

                for t in q.tiles[:1]:
                    for quarter in range(4):
                        src = bank()
                        own(cp(sc[t][:, quarter * 512:(quarter + 1) * 512], src[:, :]), vd)
                    own.settle()
                    step("scores")

            def best_of_two(rows):
                for at in (slice(0, 8), slice(8, 16)):
                    for s, val, idx in rows:
                        own(nc.vector.max(val[:, at], s))
                    own.settle()
                    for s, val, idx in rows:
                        own(nc.vector.max_index(idx[:, at], val[:, at], s))
                    own.settle()
                    if at.start == 0:
                        for s, val, idx in rows:
                            own(nc.vector.match_replace(s, val[:, at], s, GONE))
                        own.settle()

            def pick(t, half, pause):
                chunks, heads = range(8 * half, 8 * half + 8), range(4 * half, 4 * half + 4)
                hs, ns = slice(4 * half, 4 * half + 4), slice(64 * half, 64 * half + 64)
                for c in chunks[::2]:
                    best_of_two([(sc[t][:, x * NK:(x + 1) * NK], v16[:, x, :], i16[:, x, :]) for x in (c, c + 1)])
                    pause(c % 8 // 2)
                own(cp(f16[:, chunks[0]:chunks[-1] + 1, :], i16[:, chunks[0]:chunks[-1] + 1, :]))
                v4 = v16.rearrange("p (h a) k -> p h a k", a=2)
                for hh in heads:
                    own(tt(cand[:, hh * 256:(hh + 1) * 256].rearrange("p (i j) -> p i j", i=PTOP),
                           bc(v4[:, hh, 0, :].unsqueeze(2), [PTOP, PTOP]), bc(v4[:, hh, 1, :].unsqueeze(1), [PTOP, PTOP]),
                           ALU.add))
                own.settle()
                for hh in heads[::2]:
                    best_of_two([(cand[:, x * 256:(x + 1) * 256], ts16[:, x, :], pos[:, x * PTOP:(x + 1) * PTOP])
                                 for x in (hh, hh + 1)])
                    pause(4 + hh % 4 // 2)
                f4 = f16.rearrange("p (h a) k -> p h a k", a=2)
                for a_half, (op, by, e) in enumerate(((ALU.logical_shift_right, 4, e1), (ALU.bitwise_and, 15, e2))):
                    own(tsc(phi[:, ns], pos[:, ns], by, None, op))
                    own.settle()
                    own(cp(phf[:, ns], phi[:, ns]))
                    own.settle()
                    own(tt(hot[:, ns, :], bc(phf[:, ns].unsqueeze(2), [64, PTOP]), bc(iota.unsqueeze(1), [64, PTOP]),
                           ALU.is_equal))
                    own.settle()
                    for hh in heads:
                        hv = hot[:, hh * PTOP:(hh + 1) * PTOP, :]
                        own(tt(hv, hv, bc(f4[:, hh, a_half, :].unsqueeze(1), [PTOP, PTOP]), ALU.mult))
                    own.settle()
                    own(nc.vector.tensor_reduce(e[:, ns], hot[:, ns, :], AX_X, ALU.add))
                    own.settle()
                    if a_half == 0:
                        pause(6)
                at = slice(t * P + 64 * half, t * P + 64 * half + 64)
                own(stt(eidx[:, at], e1[:, ns], float(NK), e2[:, ns], ALU.mult, ALU.add))
                own(cp(s8[:, hs], ts16[:, hs, 0]))
                own.settle()
                dve.sem_inc(idx_ready, 1)
                own(tt(ts16[:, hs, :], ts16[:, hs, :], bc(s8[:, hs].unsqueeze(2), [4, PTOP]), ALU.subtract))
                own.settle()
                dve.sem_inc(score_e, 1)
                pause(7)
                dve.wait_ge(score_v, 2 * t + half + 1)
                own(nc.vector.tensor_reduce(s8[:, hs], ts16[:, hs, :], AX_X, ALU.add))
                own.settle()
                own(nc.vector.reciprocal(s8[:, hs], s8[:, hs]))
                own.settle()
                own(tt(gate[:, at].rearrange("p (h k) -> p h k", h=4), ts16[:, hs, :], bc(s8[:, hs].unsqueeze(2), [4, PTOP]),
                       ALU.mult))
                own.settle()

            own(nc.vector.memset(zero, 0.0))
            mixer(PR)
            mixer(ST)
            places.append(list(steps.seen))
            for half in range(2):
                pick(2, half, lambda place: steps.at("pick"))
            steps.run(TICKS)
            landed = [Count(u_in[s], start=2 * P // SLOTS if s < SLOTS else 0, step=16) for s in slot_sem]
            gelu_c, w_c = Count(gelu_done, start=PROMPT_BLOCKS), Count(w_ready, start=PROMPT_BLOCKS)
            with loop(dve, P // PB, (gelu_c, 1), (w_c, 1), *((c, 1) for c in landed)) as i:
                for j in range(PB):
                    landed[j].take(dve)
                    nc.vector.tensor_tensor_reduce(uslot8[j], uslot8[j], hS, 1.0, 0.0, ALU.mult, ALU.add,
                                                   dots8[:, j:j + 1]).then_inc(dot8_done, 1)
                gelu_c.take(dve)
                w_c.give(tt(w88, gl8, gate[:, ds(i * PB + 2 * P, PB)], ALU.mult))
            finish(2)
        assert places[0] == places[1] == places[2], "ticks out of step"


_INS = ['x_prompt', 'x_sample', 'cache_k', 'cache_v', 'cache_kidx', 'state_conv', 'state_ssm', 'w_in', 'b_gate', 'conv_w',
        'conv_b', 'dt_bias', 'a_log', 'd_skip', 'ssm_norm_w', 'w_attn_br', 'w_ssm_br', 'w_out', 'ln1_g', 'ln1_b',
        'peer_wq', 'peer_keys1', 'peer_keys2', 'peer_u', 'peer_v', 'ln2_g', 'ln2_b']
_OUTS = [("y_prompt", (1, SEQ, D)), ("y_sample", (DEC_B, DEC_S, D)), ("p_k", (1, 1, SEQ, KVH, HD)), ("p_v", (1, 1, SEQ, KVH, HD)),
         ("p_kidx", (1, 1, SEQ, HD)), ("p_conv", (1, 1, CW - 1, CONV)), ("p_ssm", (1, 1, SH, HD, N)),
         ("s_k", (1, DEC_B, DEC_S, KVH, HD)), ("s_v", (1, DEC_B, DEC_S, KVH, HD)), ("s_kidx", (1, DEC_B, DEC_S, HD)),
         ("s_conv", (1, DEC_B, CW - 1, CONV)), ("s_ssm", (1, DEC_B, SH, HD, N))]


def kernel(**inputs):
    import concourse.bacc as _bacc
    from concourse import mybir as _mybir
    from concourse.bass_utils import run_bass_kernel_spmd as _run

    nc = _bacc.Bacc("TRN2", target_bir_lowering=False, num_devices=1)
    arrays, a, out = {}, {}, {}
    table, where = const_table()
    for name in _INS + ["table"]:
        v = np.ascontiguousarray(table if name == "table" else inputs[name])
        arrays[f"in_{name}_dram"] = v
        a[name] = nc.dram_tensor(f"in_{name}_dram", v.shape, _mybir.dt.from_np(v.dtype), kind="ExternalInput").ap()
    for name, shape in _OUTS:
        out[name] = nc.dram_tensor(f"out_{name}_dram", shape, F32, kind="ExternalOutput").ap()
    build(nc, a, out, where)
    r = _run(nc, [arrays], core_ids=[0])
    return tuple(r.results[0][f"out_{name}_dram"] for name, _ in _OUTS)
```
